# Optimizing a Trainium2 kernel written in Bass

```python
import math
import jax, jax.numpy as jnp
from jax import lax
import numpy as np

D_MODEL = 1024
BATCH = 1
SEQ = 256
DEPTH = 2
DEC_BATCH = 8
DEC_SEQ = 1
PAST_LEN = 2048
PAGE_SIZE = 128

S5_GROUP = 16
S5_STATE = 64
S5_WIDTH = D_MODEL
S5_GROUPS = S5_WIDTH // S5_GROUP
SSD_WIDTH = D_MODEL
SSD_HEAD_DIM = 64
SSD_HEADS = SSD_WIDTH // SSD_HEAD_DIM
SSD_GROUPS = 4
SSD_HEADS_PER_GROUP = SSD_HEADS // SSD_GROUPS
SSD_STATE = 128
SSD_CONV = 4
SSD_CONV_DIM = SSD_WIDTH + 2 * SSD_GROUPS * SSD_STATE
RET_HEADS = 4
RET_QK_DIM = 128
RET_V_DIM = 256
RET_QK_WIDTH = RET_HEADS * RET_QK_DIM
RET_WIDTH = RET_HEADS * RET_V_DIM
ROPE_BASE = 10000.0
N_BRANCH = 3
D_FF = 4 * D_MODEL
CHUNK = 128
EPS = 1e-6
IN_SIZES = (S5_WIDTH, SSD_WIDTH, SSD_CONV_DIM, SSD_HEADS, RET_QK_WIDTH, RET_QK_WIDTH, RET_WIDTH, RET_WIDTH, N_BRANCH * D_MODEL)
N_IN = sum(IN_SIZES)

kernel_name = "hybrid_s5_ssd_retention_gated_decoder_step"

F32 = jnp.float32

def rmsnorm(x, w):
    xf = x.astype(F32)
    y = xf * lax.rsqrt(jnp.mean(xf * xf, axis=-1, keepdims=True) + EPS)
    return (y * w.astype(F32)).astype(x.dtype)

def _linear_combine(e_prev, e_next):
    a1, b1 = e_prev
    a2, b2 = e_next
    return a2 * a1, a2 * b1 + b2

def s5_mixer(u, a_re, a_im, log_dt, b_re, b_im, c_re, c_im, d, h0):
    bsz, L, _ = u.shape
    uf = u.astype(F32).reshape(bsz, L, S5_GROUPS, S5_GROUP)
    lam = lax.complex(a_re.astype(F32), a_im.astype(F32))
    lam_dt = lam * jnp.exp(log_dt.astype(F32))[:, None]
    a_bar = jnp.exp(lam_dt)
    b_bar = ((a_bar - 1.0) / lam)[..., None] * lax.complex(b_re.astype(F32), b_im.astype(F32))
    bu = jnp.einsum('blgc,gpc->blgp', uf.astype(jnp.complex64), b_bar)
    a_seq = jnp.broadcast_to(a_bar, bu.shape)
    _, h = lax.associative_scan(_linear_combine, (a_seq, bu), axis=1)
    if h0 is not None:
        steps = jnp.arange(1, L + 1, dtype=F32)[:, None, None]
        h = h + jnp.exp(steps * lam_dt)[None] * h0[:, None]
    c = lax.complex(c_re.astype(F32), c_im.astype(F32))
    y = jnp.real(jnp.einsum('gcp,blgp->blgc', c, h)) + d.astype(F32).reshape(S5_GROUPS, S5_GROUP) * uf
    return y.reshape(bsz, L, S5_WIDTH), h[:, -1]

def chunked_decay_scan(q, k, v, log_a, s0):
    q, k, v, log_a = q.astype(F32), k.astype(F32), v.astype(F32), log_a.astype(F32)
    b, L, g, n = q.shape
    r, p = v.shape[3], v.shape[4]
    Q = CHUNK if L % CHUNK == 0 else L
    nc = L // Q
    if s0 is None:
        s0 = jnp.zeros((b, g, r, p, n), F32)
    s0 = s0.astype(F32)

    def to_chunks(t):
        return jnp.moveaxis(t.reshape((b, nc, Q) + t.shape[2:]), 1, 0)

    causal = jnp.tril(jnp.ones((Q, Q), dtype=bool))[None, :, :, None, None]

    def body(s, inp):
        qc, kc, vc, ac = inp
        acum = jnp.cumsum(ac, axis=1)
        seg = acum[:, :, None] - acum[:, None]
        lmat = jnp.exp(jnp.where(causal, seg, -jnp.inf))
        scores = jnp.einsum('bign,bjgn->bgij', qc, kc)
        y = jnp.einsum('bgij,bijgr,bjgrp->bigrp', scores, lmat, vc)
        y = y + jnp.einsum('bign,bgrpn->bigrp', qc, s) * jnp.exp(acum)[..., None]
        w_end = jnp.exp(acum[:, -1:] - acum)
        s = jnp.exp(acum[:, -1])[..., None, None] * s + jnp.einsum('bjgn,bjgrp->bgrpn', kc, vc * w_end[..., None])
        return s, y

    s_last, ys = lax.scan(body, s0, (to_chunks(q), to_chunks(k), to_chunks(v), to_chunks(log_a)))
    y = jnp.moveaxis(ys, 0, 1).reshape(b, L, g, r, p)
    return y, s_last

def causal_conv_silu(xbc, buf, w, bias):
    L = xbc.shape[1]
    full = jnp.concatenate([buf.astype(xbc.dtype), xbc], axis=1)
    y = bias + full[:, 0:L] * w[0]
    for tap in range(1, SSD_CONV):
        y = y + full[:, tap:tap + L] * w[tap]
    return jax.nn.silu(y), full[:, L:]

def gated_group_rmsnorm(y, z, w):
    yf = y.astype(F32) * jax.nn.silu(z.astype(F32))
    shp = yf.shape
    yg = yf.reshape(shp[:-1] + (SSD_GROUPS, SSD_WIDTH // SSD_GROUPS))
    yg = yg * lax.rsqrt(jnp.mean(yg * yg, axis=-1, keepdims=True) + EPS)
    return yg.reshape(shp) * w.astype(F32)

def rotary(x, pos):
    d = x.shape[-1]
    half = d // 2
    inv = ROPE_BASE ** (-jnp.arange(half, dtype=F32) / half)
    ang = pos.astype(F32)[:, None] * inv[None]
    cos = jnp.cos(ang)[None, :, None, :]
    sin = jnp.sin(ang)[None, :, None, :]
    xf = x.astype(F32)
    x1, x2 = xf[..., :half], xf[..., half:]
    return jnp.concatenate([x1 * cos - x2 * sin, x2 * cos + x1 * sin], axis=-1)

def mixer_layer(h, pos, s5_h0, ssd_s0, conv_buf, ret_s0, p):
    bsz, L, _ = h.shape
    dt_ = h.dtype
    xn = rmsnorm(h, p['norm1_w'])
    proj = xn @ p['w_in']
    split_at = np.cumsum(IN_SIZES)[:-1].tolist()
    u, z, xbc, dt, q, k, v, g, gates = jnp.split(proj, split_at, axis=-1)

    y_s5, s5_last = s5_mixer(u, p['s5_a_re'], p['s5_a_im'], p['s5_log_dt'], p['s5_b_re'], p['s5_b_im'],
                             p['s5_c_re'], p['s5_c_im'], p['s5_d'], s5_h0)
    glu = jax.nn.gelu(y_s5.astype(dt_)) @ p['w_s5_out']
    y_a = glu[..., :D_MODEL] * jax.nn.sigmoid(glu[..., D_MODEL:])

    xbc, conv_new = causal_conv_silu(xbc, conv_buf, p['ssd_conv_w'], p['ssd_conv_b'])
    xs, bs, cs = jnp.split(xbc, [SSD_WIDTH, SSD_WIDTH + SSD_GROUPS * SSD_STATE], axis=-1)
    delta = jax.nn.softplus(dt.astype(F32) + p['ssd_dt_bias'].astype(F32))
    a_head = -jnp.exp(p['ssd_a_log'].astype(F32))
    log_a = (delta * a_head).reshape(bsz, L, SSD_GROUPS, SSD_HEADS_PER_GROUP)
    xs4 = xs.astype(F32).reshape(bsz, L, SSD_HEADS, SSD_HEAD_DIM)
    vv = (xs4 * delta[..., None]).reshape(bsz, L, SSD_GROUPS, SSD_HEADS_PER_GROUP, SSD_HEAD_DIM)
    s0 = None if ssd_s0 is None else ssd_s0.reshape(bsz, SSD_GROUPS, SSD_HEADS_PER_GROUP, SSD_HEAD_DIM, SSD_STATE)
    y_ssd, ssd_s = chunked_decay_scan(cs.reshape(bsz, L, SSD_GROUPS, SSD_STATE),
                                      bs.reshape(bsz, L, SSD_GROUPS, SSD_STATE), vv, log_a, s0)
    y_ssd = y_ssd.reshape(bsz, L, SSD_HEADS, SSD_HEAD_DIM) + p['ssd_d'].astype(F32)[:, None] * xs4
    y_b = gated_group_rmsnorm(y_ssd.reshape(bsz, L, SSD_WIDTH), z, p['ssd_norm_w']).astype(dt_) @ p['w_ssd_out']
    ssd_s = ssd_s.reshape(bsz, SSD_HEADS, SSD_HEAD_DIM, SSD_STATE)

    qr = rotary(q.reshape(bsz, L, RET_HEADS, RET_QK_DIM), pos)
    kr = rotary(k.reshape(bsz, L, RET_HEADS, RET_QK_DIM), pos) * (RET_QK_DIM ** -0.5)
    log_gamma = jnp.log1p(-jnp.exp2(-5.0 - jnp.arange(RET_HEADS, dtype=F32)))
    log_a_c = jnp.broadcast_to(log_gamma[:, None], (bsz, L, RET_HEADS, 1))
    r0 = None if ret_s0 is None else ret_s0.reshape(bsz, RET_HEADS, 1, RET_V_DIM, RET_QK_DIM)
    y_ret, ret_s = chunked_decay_scan(qr, kr, v.reshape(bsz, L, RET_HEADS, 1, RET_V_DIM), log_a_c, r0)
    y_ret = y_ret.reshape(bsz, L, RET_HEADS, RET_V_DIM)
    y_ret = y_ret * lax.rsqrt(jnp.mean(y_ret * y_ret, axis=-1, keepdims=True) + EPS)
    y_ret = y_ret.reshape(bsz, L, RET_WIDTH) * jax.nn.silu(g.astype(F32))
    y_c = y_ret.astype(dt_) @ p['w_ret_out']
    ret_s = ret_s.reshape(bsz, RET_HEADS, RET_V_DIM, RET_QK_DIM)

    gate = jax.nn.sigmoid(gates.reshape(bsz, L, N_BRANCH, D_MODEL))
    merged = gate[:, :, 0] * y_a + gate[:, :, 1] * y_b + gate[:, :, 2] * y_c
    h = h + (merged @ p['w_out']).astype(dt_)

    hn = rmsnorm(h, p['norm2_w'])
    h = h + (jnp.square(jax.nn.relu(hn @ p['w_mlp_up'])) @ p['w_mlp_down']).astype(dt_)
    return h, s5_last, ssd_s, conv_new, ret_s

def run_trunk(x, pos, st, params, final_norm_w):
    h = x
    out_re, out_im, out_ssd, out_conv, out_ret = [], [], [], [], []
    for l in range(DEPTH):
        p = {name: arr[l] for name, arr in params.items()}
        if st is None:
            s5_h0, ssd_s0, ret_s0 = None, None, None
            conv_buf = jnp.zeros((x.shape[0], SSD_CONV - 1, SSD_CONV_DIM), x.dtype)
        else:
            s5_h0 = lax.complex(st[0][l].astype(F32), st[1][l].astype(F32))
            ssd_s0, conv_buf, ret_s0 = st[2][l], st[3][l], st[4][l]
        h, s5_last, ssd_s, conv_new, ret_s = mixer_layer(h, pos, s5_h0, ssd_s0, conv_buf, ret_s0, p)
        out_re.append(jnp.real(s5_last))
        out_im.append(jnp.imag(s5_last))
        out_ssd.append(ssd_s)
        out_conv.append(conv_new)
        out_ret.append(ret_s)
    y = rmsnorm(h, final_norm_w)
    return y, jnp.stack(out_re), jnp.stack(out_im), jnp.stack(out_ssd), jnp.stack(out_conv), jnp.stack(out_ret)

def setup_inputs(seed: int = 0) -> dict:
    key = jax.random.key(seed)
    ks = iter(jax.random.split(key, 40))

    def nrm(shape, scale):
        return jax.random.normal(next(ks), shape, F32) * scale

    def log_uniform(shape, lo, hi):
        uu = jax.random.uniform(next(ks), shape, F32)
        return jnp.exp(uu * (math.log(hi) - math.log(lo)) + math.log(lo))

    Dp = DEPTH
    inp = {}
    inp['x_prompt'] = nrm((BATCH, SEQ, D_MODEL), 1.0)
    inp['x_sample'] = nrm((DEC_BATCH, DEC_SEQ, D_MODEL), 1.0)
    inp['state_s5_re'] = nrm((Dp, DEC_BATCH, S5_GROUPS, S5_STATE), 0.1)
    inp['state_s5_im'] = nrm((Dp, DEC_BATCH, S5_GROUPS, S5_STATE), 0.1)
    inp['state_ssd'] = nrm((Dp, DEC_BATCH, SSD_HEADS, SSD_HEAD_DIM, SSD_STATE), 0.1)
    inp['state_conv'] = nrm((Dp, DEC_BATCH, SSD_CONV - 1, SSD_CONV_DIM), 1.0)
    inp['state_ret'] = nrm((Dp, DEC_BATCH, RET_HEADS, RET_V_DIM, RET_QK_DIM), 0.3)
    inp['norm1_w'] = 1.0 + nrm((Dp, D_MODEL), 0.02)
    inp['w_in'] = nrm((Dp, D_MODEL, N_IN), D_MODEL ** -0.5)
    inp['s5_a_re'] = -0.5 + nrm((Dp, S5_GROUPS, S5_STATE), 0.01)
    inp['s5_a_im'] = math.pi * jnp.arange(S5_STATE, dtype=F32) + nrm((Dp, S5_GROUPS, S5_STATE), 0.01)
    inp['s5_log_dt'] = jnp.log(log_uniform((Dp, S5_GROUPS), 1e-3, 1e-1))
    inp['s5_b_re'] = nrm((Dp, S5_GROUPS, S5_STATE, S5_GROUP), (2 * S5_GROUP) ** -0.5)
    inp['s5_b_im'] = nrm((Dp, S5_GROUPS, S5_STATE, S5_GROUP), (2 * S5_GROUP) ** -0.5)
    inp['s5_c_re'] = nrm((Dp, S5_GROUPS, S5_GROUP, S5_STATE), S5_STATE ** -0.5)
    inp['s5_c_im'] = nrm((Dp, S5_GROUPS, S5_GROUP, S5_STATE), S5_STATE ** -0.5)
    inp['s5_d'] = nrm((Dp, S5_WIDTH), 1.0)
    inp['w_s5_out'] = nrm((Dp, S5_WIDTH, 2 * D_MODEL), S5_WIDTH ** -0.5)
    inp['ssd_conv_w'] = nrm((Dp, SSD_CONV, SSD_CONV_DIM), SSD_CONV ** -0.5)
    inp['ssd_conv_b'] = nrm((Dp, SSD_CONV_DIM), 0.01)
    dt0 = log_uniform((Dp, SSD_HEADS), 1e-3, 1e-1)
    inp['ssd_dt_bias'] = dt0 + jnp.log(-jnp.expm1(-dt0))
    inp['ssd_a_log'] = jnp.log(jax.random.uniform(next(ks), (Dp, SSD_HEADS), F32, 1.0, 16.0))
    inp['ssd_d'] = 1.0 + nrm((Dp, SSD_HEADS), 0.1)
    inp['ssd_norm_w'] = 1.0 + nrm((Dp, SSD_WIDTH), 0.02)
    inp['w_ssd_out'] = nrm((Dp, SSD_WIDTH, D_MODEL), SSD_WIDTH ** -0.5)
    inp['w_ret_out'] = nrm((Dp, RET_WIDTH, D_MODEL), RET_WIDTH ** -0.5)
    inp['w_out'] = nrm((Dp, D_MODEL, D_MODEL), D_MODEL ** -0.5)
    inp['norm2_w'] = 1.0 + nrm((Dp, D_MODEL), 0.02)
    inp['w_mlp_up'] = nrm((Dp, D_MODEL, D_FF), D_MODEL ** -0.5)
    inp['w_mlp_down'] = nrm((Dp, D_FF, D_MODEL), D_FF ** -0.5)
    inp['final_norm_w'] = 1.0 + nrm((D_MODEL,), 0.02)
    return inp

def reference(x_prompt, x_sample, state_s5_re, state_s5_im, state_ssd, state_conv, state_ret,
              norm1_w, w_in, s5_a_re, s5_a_im, s5_log_dt, s5_b_re, s5_b_im, s5_c_re, s5_c_im, s5_d,
              w_s5_out, ssd_conv_w, ssd_conv_b, ssd_dt_bias, ssd_a_log, ssd_d, ssd_norm_w, w_ssd_out,
              w_ret_out, w_out, norm2_w, w_mlp_up, w_mlp_down, final_norm_w):
    params = dict(norm1_w=norm1_w, w_in=w_in, s5_a_re=s5_a_re, s5_a_im=s5_a_im, s5_log_dt=s5_log_dt,
                  s5_b_re=s5_b_re, s5_b_im=s5_b_im, s5_c_re=s5_c_re, s5_c_im=s5_c_im, s5_d=s5_d,
                  w_s5_out=w_s5_out, ssd_conv_w=ssd_conv_w, ssd_conv_b=ssd_conv_b, ssd_dt_bias=ssd_dt_bias,
                  ssd_a_log=ssd_a_log, ssd_d=ssd_d, ssd_norm_w=ssd_norm_w, w_ssd_out=w_ssd_out,
                  w_ret_out=w_ret_out, w_out=w_out, norm2_w=norm2_w, w_mlp_up=w_mlp_up, w_mlp_down=w_mlp_down)
    pos_p = jnp.arange(x_prompt.shape[1], dtype=jnp.int32)
    pos_s = PAST_LEN + jnp.arange(x_sample.shape[1], dtype=jnp.int32)
    y_prompt, re_p, im_p, ssd_p, conv_p, ret_p = run_trunk(x_prompt, pos_p, None, params, final_norm_w)
    y_sample, re_s, im_s, ssd_s, conv_s, ret_s = run_trunk(
        x_sample, pos_s, (state_s5_re, state_s5_im, state_ssd, state_conv, state_ret), params, final_norm_w)
    return (y_prompt, y_sample, re_p, im_p, ssd_p, conv_p, ret_p, re_s, im_s, ssd_s, conv_s, ret_s)


_drawn_inputs = setup_inputs


def setup_inputs(seed=0):
    import zlib

    import numpy as np

    out = dict(_drawn_inputs(seed))
    spreads = {}
    factors = {'s5_a_re': 67.522,
     's5_c_re': 7.527,
     's5_c_im': 7.522,
     'ssd_conv_b': 2.95,
     'ssd_norm_w': 4.484,
     'final_norm_w': 21.456,
     'norm2_w': 3.962}
    for name, (base, spread) in spreads.items():
        noise = np.random.default_rng([zlib.crc32(name.encode()), seed]).standard_normal(out[name].shape)
        drawn = base * np.exp(spread * noise) if base else spread * noise
        out[name] = __import__('jax').numpy.asarray(drawn.astype(out[name].dtype))
    for name, factor in factors.items():
        out[name] = (out[name] * factor).astype(out[name].dtype)
    return out
```

```python
import math
from contextlib import ExitStack

import numpy as np

import concourse.bass as bass
from concourse import mybir

F32 = mybir.dt.float32
ALU = mybir.AluOpType
ACT = mybir.ActivationFunctionType

P = 128
D_MODEL = 1024
SEQ = 256
DEPTH = 2
SAMPLES = 8
PAST_LEN = 2048
TOK = SEQ + SAMPLES
NB = D_MODEL // P
D_FF = 4096
S5_GROUPS, S5_STATE, S5_CH = 64, 64, 16
PAIRS = S5_GROUPS // 2
LIFT = 4
CHUNKS = SEQ // LIFT
HEADS, HEAD_DIM, SSD_G, SSD_N = 16, 64, 4, 128
CONV_DIM = 2048
CB = CONV_DIM // P
TAPS = 4
XC_W = TAPS - 1 + SEQ + SAMPLES * TAPS
CONV_OUT = XC_W - (TAPS - 1)
RET_H, RET_N, RET_P = 4, 128, 256
ROPE_BASE = 10000.0
EPS = 1e-6
N_IN = 10256
COL_U, COL_Z, COL_X, COL_DT, COL_QK, COL_V, COL_G, COL_GATE = 0, 1024, 2048, 4096, 4112, 5136, 6160, 7184
SCORE_W = SEQ + P
RING = 4
TWO_PI = 2.0 * math.pi

C_IDENT, C_ONES, C_MASK = 0, 128, 256
C_COSQ, C_SINQ, C_COSK, C_SINK = 384, 648, 912, 1176
C_DECAY = 1440
C_CAUSAL = C_DECAY + RET_H * SCORE_W
C_EXPAND = C_CAUSAL + SCORE_W
C_WEND = C_EXPAND + NB * P
C_MHALF = C_WEND + 2 * RET_H
CONST_W = C_MHALF + 1


def retention_gammas():
    return [1.0 - 2.0 ** (-5.0 - h) for h in range(RET_H)]


def constant_table():
    t = np.zeros((P, CONST_W), np.float64)
    t[:, C_IDENT:C_IDENT + P] = np.eye(P)
    t[:, C_ONES:C_ONES + P] = 1.0
    row = np.arange(P)
    t[:, C_MASK:C_MASK + P] = ((row[:, None] // 16) % 2) == (row[None, :] // 64)
    half = RET_N // 2
    pos = np.concatenate([np.arange(SEQ), np.full(SAMPLES, PAST_LEN)]).astype(np.float64)
    inv = ROPE_BASE ** (-np.arange(half) / half)
    ang = inv[:, None] * pos[None, :]
    cos = np.concatenate([np.cos(ang), np.cos(ang)])
    sin = np.concatenate([-np.sin(ang), np.sin(ang)])
    t[:, C_COSQ:C_COSQ + TOK] = cos
    t[:, C_SINQ:C_SINQ + TOK] = sin
    t[:, C_COSK:C_COSK + TOK] = cos * RET_N ** -0.5
    t[:, C_SINK:C_SINK + TOK] = sin * RET_N ** -0.5
    dist = np.arange(SEQ)[None, :] - row[:, None]
    causal = (dist >= 0).astype(np.float64)
    for h, gamma in enumerate(retention_gammas()):
        decay = np.where(dist >= 0, gamma ** np.maximum(dist, 0), 0.0)
        t[:, C_DECAY + h * SCORE_W:C_DECAY + (h + 1) * SCORE_W] = np.concatenate([decay, decay[:, :P]], 1)
        for tb in range(2):
            t[:, C_WEND + tb * RET_H + h] = gamma ** (SEQ - 1 - tb * P - row)
    t[:, C_CAUSAL:C_CAUSAL + SCORE_W] = np.concatenate([causal, causal[:, :P]], 1)
    for m in range(NB):
        for h2 in range(2):
            t[2 * m + h2, C_EXPAND + m * P + h2 * 64:C_EXPAND + m * P + (h2 + 1) * 64] = 1.0
    t[:, C_MHALF] = -0.5
    return t.astype(np.float32)


O_CONST = 0
O_PRM = O_CONST + CONST_W
PRM_W = 600
O_H = O_PRM + PRM_W
O_XN = O_H + NB * TOK
O_RING = O_XN + NB * TOK
CHUNK_W = 8 * 256
O_U = O_RING + RING * CHUNK_W
O_Z = O_U + NB * TOK
O_G = O_Z + NB * TOK
O_QK = O_G + NB * TOK
O_V = O_QK + NB * TOK
O_XC = O_V + NB * TOK
O_R = O_XC + CB * XC_W
SLOTS = 1 + CHUNKS + 2 * SAMPLES
U4_W = CHUNKS + 2 * SAMPLES
O_SV = O_R
O_U4 = O_SV + SLOTS * 64
O_GW = O_U4 + PAIRS * U4_W
O_BB = O_GW + 8192
O_CT = O_BB + 1024
O_SM = O_CT + 1024
O_DTS = O_R
O_VTOK = O_DTS + 8 * TOK
O_VW = O_VTOK + 2048
O_BTOK = O_VW + 2048
O_SC = O_BTOK + 1024
O_SEG = O_SC + 2 * SCORE_W
O_EXP = O_SEG + 2 * SCORE_W
O_DEC = O_EXP + 2 * SCORE_W
O_TMP = O_DEC + 2048
O_STOUT = O_TMP + 1024
O_ZG = O_STOUT + 1024
O_M = O_ZG + NB * TOK
O_KST = O_M + NB * TOK
SB_W = max(O_SM + 2048, O_KST + 1024)
O_HID = O_R

UNITS = ["u", "x0", "x1", "qk", "v", "g", "z", "s5a", "s5b", "gate0", "reto", "gate2", "gate1", "ssdo", "wo",
         "up0", "up1", "up2", "up3", "dn0", "dn1", "dn2", "dn3"]
BLOCKS = {}
_at = 0
for _n in UNITS:
    BLOCKS[_n] = _at
    _at += 2 if _n.startswith("dn") else 8

MIXER_FILLS = (
    ["prm", "n1", "s5p", "cre0", "cre1", "cim0", "cim1", "h0", "cs"] + [f"tail{i}" for i in range(4)]
    + [f"G{i}" for i in range(16)] + [f"V{i}" for i in range(16)]
    + [f for hf in range(2) for f in ([f"K{hf}{i}" for i in range(4)] + [f"Y{hf}{i}" for i in range(4)])]
    + ["nss", "nsp", "dt"]
    + [f"rv{i}" for i in range(4)] + ["rk0", "rk1"]
    + [f for h in range(4) for f in (f"rs{h}", f"ry{h}")] + ["rst0", "rst1", "rkT", "rqT"]
    + [f for b in range(8) for f in (f"rkb{b}", f"rqb{b}")] + [f"rn{h}" for h in range(4)]
    + ["sc"] + [f"sv{i}" for i in range(4)] + ["sb0", "sb1"]
    + ["ss0", "sa0"]
    + [f for m in range(8) for f in (([f"ss{(m + 1) // 2}"] if m % 2 and m < 7 else [])
                                     + ([f"sa{m + 1}"] if m < 7 else []) + [f"sy{m}"])]
    + ["sst0", "sst1", "skT", "sqT"]
    + [f for b in range(8) for f in (f"skb{b}", f"sqb{b}")] + [f"sn{h}" for h in range(4)]
    + ["n2"]
)
FILL = {n: (i % 4, i // 4 + 1) for i, n in enumerate(MIXER_FILLS)}

PR_N1, PR_N2, PR_D, PR_SN, PR_CB, PR_CW, PR_FN, PR_ROWS = 0, 8, 16, 24, 32, 48, 112, 120
PR_DTW, PR_C16, PR_COLS, PR_VS, PR_YS = 120, 248, 256, 488, 552 - 16


def build_trunk(nc, t):
    ctx = ExitStack()
    with ctx:
        arena = ctx.enter_context(nc.sbuf_tensor("arena", [P, SB_W], F32))
        small = ctx.enter_context(nc.sbuf_tensor("small", [P, 192], F32))
        banks = [ctx.enter_context(nc.psum_tensor(f"bank{i}", [P, 512], F32)) for i in range(8)]

        def sem(name):
            return ctx.enter_context(nc.semaphore(name))

        def view(off, *dims, p0=0, p1=P):
            n = int(np.prod(dims))
            ap = arena[p0:p1, off:off + n]
            names = "abcd"[:len(dims)]
            if len(dims) > 1:
                ap = ap.rearrange(f"p ({' '.join(names)}) -> p {' '.join(names)}",
                                  **{k: d for k, d in zip(names, dims)})
            return ap

        ident = view(O_CONST + C_IDENT, P)
        ones = view(O_CONST + C_ONES, P)
        s5mask = view(O_CONST + C_MASK, P)
        cosq, sinq = view(O_CONST + C_COSQ, TOK), view(O_CONST + C_SINQ, TOK)
        cosk, sink = view(O_CONST + C_COSK, TOK), view(O_CONST + C_SINK, TOK)
        decay = view(O_CONST + C_DECAY, RET_H, SCORE_W)
        causal = view(O_CONST + C_CAUSAL, SCORE_W)
        expand = view(O_CONST + C_EXPAND, NB, P)
        wend = view(O_CONST + C_WEND, 2, RET_H)
        mhalf = view(O_CONST + C_MHALF, 1)
        prm = view(O_PRM, PR_ROWS)
        dtw = view(O_PRM + PR_DTW, 8, 16)
        c16 = view(O_PRM + PR_C16, 8)
        cols = view(O_PRM + PR_COLS, 232)
        h = view(O_H, NB, TOK)
        xn = view(O_XN, NB, TOK)
        ring = view(O_RING, RING, 8, 256)
        u = view(O_U, NB, TOK)
        zr = view(O_Z, NB, TOK)
        g = view(O_G, NB, TOK)
        qk = view(O_QK, NB, TOK)
        v = view(O_V, NB, TOK)
        xc = view(O_XC, CB, XC_W)
        sv = view(O_SV, SLOTS, 64)
        u4 = view(O_U4, PAIRS, U4_W)
        gw = view(O_GW, 2, PAIRS, P)
        bb = view(O_BB, 2, PAIRS, 16)
        ct = view(O_CT, 2, PAIRS, 16)

        w_landed = [sem(f"w_landed{i}") for i in range(RING)]
        chunk_used = sem("chunk_used")
        proj_filled = sem("proj_filled")
        proj_drained = sem("proj_drained")
        bank_filled = [sem(f"bank_filled{i}") for i in range(4)]
        bank_drained = [sem(f"bank_drained{i}") for i in range(4)]
        dve_step, act_step, pool_step = sem("dve_step"), sem("act_step"), sem("pool_step")
        names = """const_in vec_in s5_in b_in c_in h0_in convst_in head_in dtw_in squares mean_ready rstd_ready xn_ready
            prm_ready s5a_cols trig_arg trig_ready powers_ready pool_zero u4_ready bd_ready bd_used conv_pad conv_y conv_t conv_silu
            tail_ready tails_out convcopy_out rope_done g_silu scan_go scan_done newst_ready s5st_out
            e_ready gelu_arg gelu_tanh gelu_done z_silu ret_kw ret_m st_evac st_out dec_in0 dec_in1 dec_out0 dec_out1
            ret_yc retsq ret_norm gates_m dt_abs dt_exp alog_exp acum_ready wend_exp dt_rows
            ssd_vtok seg_ready exp_ready exp_masked ssd_yz ssdsq ssd_norm merged hid_ready resid x_in y_rows y_out ysmp
            scan_step""".split()
        s = {n: sem(n) for n in names}
        all_sems = w_landed + [chunk_used, proj_filled, proj_drained] + bank_filled + bank_drained \
            + [dve_step, act_step, pool_step] + list(s.values())
        numbers = sorted(x.num for x in all_sems)
        sem_range = range(numbers[0], numbers[-1] + 1)
        assert len(numbers) == len(sem_range)

        def bank(name):
            return banks[4 + FILL[name][0]]

        def filled(eng, name):
            eng.wait_ge(bank_filled[FILL[name][0]], FILL[name][1])

        def drained(eng, name):
            eng.wait_ge(bank_drained[FILL[name][0]], FILL[name][1])

        def is_drained(ins, name):
            ins.then_inc(bank_drained[FILL[name][0]], 1)

        class Chain:

            def __init__(self, eng, semaphore):
                self.eng, self.sem, self.n = eng, semaphore, 0

            def step(self, ins):
                ins.then_inc(self.sem, 1)
                self.n += 1

            def wait(self):
                self.eng.wait_ge(self.sem, self.n)

            def link(self, ins):
                self.step(ins)
                self.wait()

        def layer_of(ap, lyr):
            dims = " ".join("abcde"[:len(ap.shape) - 1])
            first, rest = dims.split(" ")[0], " ".join(dims.split(" ")[1:])
            return ap[bass.ds(lyr, 1)].rearrange(f"o {dims} -> (o {first}) {rest}".strip())

        xld = view(O_R, 2, D_MODEL)
        xsld = view(O_R + 2 * D_MODEL, D_MODEL, p1=SAMPLES)
        with nc.Block() as block:
            @block.sync
            def _(sp):
                sp.dma_start(arena[:, O_CONST:O_CONST + CONST_W], t["consts"]).then_inc(s["const_in"], 16)
                sp.dma_start(xld, t["x_prompt"].rearrange("o (tb p) d -> p (o tb) d", p=P)).then_inc(s["x_in"], 16)
                sp.dma_start(xsld, t["x_sample"].rearrange("b o d -> (b o) d")).then_inc(s["x_in"], 16)

            @block.tensor
            def _(pe):
                pe.wait_ge(s["const_in"], 16)
                pe.wait_ge(s["x_in"], 32)
                for k in range(NB):
                    if k >= 4:
                        pe.wait_ge(proj_drained, k - 3)
                    for tb in range(2):
                        pe.transpose(banks[k % 4][:, tb * P:(tb + 1) * P], xld[:, tb, k * P:(k + 1) * P], ident)
                    pe.transpose(banks[k % 4][:, SEQ:TOK], xsld[:, k * P:(k + 1) * P],
                                 ident[0:SAMPLES, 0:SAMPLES]).then_inc(proj_filled, 1)

            @block.scalar
            def _(act):
                for k in range(NB):
                    act.wait_ge(proj_filled, k + 1)
                    nc.scalar.activation(h[:, k, :], banks[k % 4][:, 0:TOK], ACT.Copy).then_inc(proj_drained, 1)

        nc.all_engine_barrier(sems_to_clear=sem_range)

        pwr = view(O_SM, 5, 2, PAIRS)
        a4r, a4i = view(O_SM + 320, 64), view(O_SM + 384, 64)
        qfac = view(O_SM + 448, 2, PAIRS)
        trig = view(O_SM + 512, 8, 2, PAIRS)
        s5v = view(O_SM + 1024, 4, PAIRS)
        vrow = view(O_SM + 1152, P)
        prow = view(O_SM + 1280, 4, P, p1=PAIRS)
        dtrow = view(O_SM + 1792, 2, p1=PAIRS)
        a1r, a1i = small[:, 64:128], small[:, 128:192]
        et = view(O_SM + 1024, 4, 16, 16)
        news = view(O_SM + 1280, 4, P)
        newp = view(O_SM + 1792, P, p1=64)
        braw = view(O_SV + 1024, 2, PAIRS, 16)
        btmp = view(O_SV + 2048, 4, PAIRS, 16)
        bd = view(O_QK, 2, 16, P)
        convst = view(O_GW, CONV_DIM, p1=SAMPLES * (TAPS - 1))
        craw = view(O_GW + 2048, 2, 8, P)
        h0raw = view(O_GW + 4096, 4, P)
        eb = view(O_GW, 2, 16, 5, 32)
        toep = view(O_GW + 5120, 16, P)
        bblk = view(O_GW + 7168, 2, 16, 32)
        mean_sq, rstd = view(O_G, TOK), view(O_G + TOK, TOK)
        convy = view(O_G, 3, 2, CONV_OUT)
        tailc = view(O_G + 1900, CB, 11)
        tailr = view(O_Z, CONV_DIM, p1=11)
        dts = view(O_DTS, 8, TOK, p1=HEADS)
        DT_X, DT_E, DT_S, DT_DELTA, DT_LA, DT_AC, DT_DW, DT_RHS = range(8)
        vtok, vw = view(O_VTOK, 2, D_MODEL), view(O_VW, 2, D_MODEL)
        btok = view(O_BTOK, 2, 512)
        sc = view(O_SC, 2, SCORE_W)
        seg, ex = view(O_SEG, 2, SCORE_W), view(O_EXP, 2, SCORE_W)
        dec = view(O_DEC, 2, NB, P)
        outer = view(O_TMP, NB, P)
        stout = view(O_STOUT, NB, P)
        zg = view(O_ZG, NB, TOK)
        m_ = view(O_M, NB, TOK)
        rows_k, rows_q = view(O_KST, 512, p1=SAMPLES), view(O_KST + 512, 512, p1=SAMPLES)
        sq8 = view(O_VTOK, NB, TOK)
        gms, grs = view(O_SEG, TOK), view(O_EXP, TOK)
        hid = view(O_HID, 32, TOK)
        vs, ys = view(O_PRM + 488, NB, SAMPLES), small[:, 0:64].rearrange("p (a b) -> p a b", a=NB)
        gam = retention_gammas()

        def at(name):
            return BLOCKS[name]

        def layer(nc, block, t, lyr):
            @block.sync
            def _(sp):
                def cols_of(name, col0):
                    w = layer_of(t[name], lyr).rearrange("(k p) n -> p k n", p=P)
                    return lambda c: w[:, :, bass.ds(col0 + 256 * c, 256)]

                def load(unit_no, source, before):
                    for c in range(RING):
                        before(c)
                        sp.dma_start(ring[:, c, :, :], source(c)).then_inc(w_landed[c], 16)

                def after_unit(first_block):
                    return lambda c: sp.wait_ge(proj_filled, first_block + 2 * c + 2)

                load(0, cols_of("w_in", COL_U), lambda c: None)
                with sp.Fori(0, 2) as j:
                    load(1 + j, cols_of("w_in", COL_X + j * 1024), after_unit(at("u") + 8 * j))
                for name, arr, col in (("qk", "w_in", COL_QK), ("v", "w_in", COL_V), ("g", "w_in", COL_G),
                                       ("z", "w_in", COL_Z), ("s5a", "w_s5_out", 0), ("s5b", "w_s5_out", 1024),
                                       ("gate0", "w_in", COL_GATE), ("reto", "w_ret_out", 0),
                                       ("gate2", "w_in", COL_GATE + 2048), ("gate1", "w_in", COL_GATE + 1024),
                                       ("ssdo", "w_ssd_out", 0), ("wo", "w_out", 0)):
                    n = UNITS.index(name)
                    load(n, cols_of(arr, col), after_unit(at(UNITS[n - 1])))
                with sp.Fori(0, 4) as j:
                    load(15 + j, cols_of("w_mlp_up", j * 1024), after_unit(at("wo") + 8 * j))
                down = layer_of(t["w_mlp_down"], lyr).rearrange("(r k p) n -> p r k n", r=4, p=P)
                load(19, lambda c: down[:, c, :, 0:256], after_unit(at("up3")))
                with sp.Fori(1, 4) as j:
                    def before(c):
                        if c < 3:
                            sp.wait_ge(chunk_used, 3 * j + (c - 2))
                        else:
                            sp.wait_ge(proj_filled, at("dn0") + 2 * j)
                    load(19 + j, lambda c: down[:, c, :, bass.ds(j * 256, 256)], before)

            @block.tensor
            def _(pe):
                def open_fill(name):
                    b, f = FILL[name]
                    if f > 1:
                        pe.wait_ge(bank_drained[b], f - 1)
                    return banks[4 + b]

                def close_fill(ins, name):
                    ins.then_inc(bank_filled[FILL[name][0]], 1)

                def unit(n, first, rhs, fresh=False):
                    for b in range(8):
                        c = b // 2
                        if b % 2 == 0:
                            pe.wait_ge(w_landed[c], n * 16 + 16)
                        if not (fresh and b < 4):
                            pe.wait_ge(proj_drained, first + (b - 3))
                        for k in range(8):
                            mm = pe.matmul(banks[b % 4][:, 0:TOK], ring[:, c, k, (b % 2) * P:(b % 2) * P + P],
                                           rhs[:, k, :], start=(k == 0), stop=(k == 7))
                        mm.then_inc(proj_filled, 1)

                def named(name, rhs):
                    unit(UNITS.index(name), at(name), rhs)

                def sum_squares(name, src, blocks, ready, first):
                    o = open_fill(name)
                    for i, k in enumerate(blocks):
                        pe.wait_ge(s[ready], first + i + 1)
                        mm = pe.matmul(o[:, 0:TOK], ones, src[:, k, :], start=(i == 0), stop=(i == len(blocks) - 1))
                    close_fill(mm, name)

                pe.wait_ge(s["vec_in"], 112)
                o = open_fill("prm")
                close_fill(pe.transpose(o[:, 0:PR_ROWS], vrow[0:PR_ROWS, :], ident[0:PR_ROWS, 0:PR_ROWS]), "prm")
                sum_squares("n1", zr, range(NB), "squares", 0)
                o = open_fill("s5p")
                pe.wait_ge(s["s5a_cols"], 2)
                for i in range(4):
                    mm = pe.transpose(o[:, i * 32:(i + 1) * 32], prow[:, i, :], ident[0:32, 0:32])
                close_fill(mm, "s5p")
                pe.wait_ge(s["c_in"], 64)
                for ri, nm in enumerate(("cre", "cim")):
                    for i in range(2):
                        o = open_fill(f"{nm}{i}")
                        for j in range(4):
                            mm = pe.transpose(o[:, j * P:(j + 1) * P], craw[:, ri, 4 * i + j, :], ident)
                        close_fill(mm, f"{nm}{i}")
                pe.wait_ge(s["h0_in"], 64)
                o = open_fill("h0")
                for j in range(4):
                    mm = pe.transpose(o[:, j * P:(j + 1) * P], h0raw[:, j, :], ident)
                close_fill(mm, "h0")
                pe.wait_ge(s["convst_in"], 16)
                o = open_fill("cs")
                for j in range(CB):
                    mm = pe.transpose(o[:, j * 24:(j + 1) * 24], convst[:, j * P:(j + 1) * P], ident[0:24, 0:24])
                close_fill(mm, "cs")
                pe.wait_ge(s["xn_ready"], 8)
                unit(0, 0, xn, fresh=True)
                with pe.Fori(0, 2) as j:
                    unit(1 + j, 8 * j + 8, xn)
                pe.wait_ge(s["tail_ready"], 2)
                for i in range(4):
                    o = open_fill(f"tail{i}")
                    for j in range(4):
                        mm = pe.transpose(o[0:11, j * P:(j + 1) * P], tailc[:, 4 * i + j, :], ident)
                    close_fill(mm, f"tail{i}")
                for sl in range(2):
                    pe.wait_ge(s["bd_ready"], sl + 1)
                    for ri in range(2):
                        for i in range(4):
                            nm = f"G{8 * sl + 4 * ri + i}"
                            o = open_fill(nm)
                            for j in range(4):
                                mm = pe.transpose(o[:, j * P:(j + 1) * P], bd[:, ri, 4 * i + j, :], ident)
                            close_fill(mm, nm)
                pe.wait_ge(s["u4_ready"], 1)
                for i in range(8):
                    for ri in range(2):
                        nm = f"V{2 * i + ri}"
                        o = open_fill(nm)
                        drained(pe, f"G{8 * (i // 4) + 4 * ri + i % 4}")
                        for j in range(4):
                            m = 4 * i + j
                            mm = pe.matmul(o[:, j * 72:(j + 1) * 72], gw[:, ri, m, :], u4[:, m, 8:80],
                                           start=True, stop=True)
                        close_fill(mm, nm)
                named("qk", xn)
                named("v", xn)
                named("g", xn)
                for hf in range(2):
                    pe.wait_ge(s["e_ready"], hf + 1)
                    for i in range(4):
                        nm = f"K{hf}{i}"
                        o = open_fill(nm)
                        for j in range(4):
                            lm = 4 * i + j
                            pe.matmul(o[0:32, j * P:(j + 1) * P], bblk[:, 0, lm, :],
                                      eb[:, 0, lm, 0:4, :].rearrange("p a b -> p (a b)"), start=True, stop=False)
                            mm = pe.matmul(o[0:32, j * P:(j + 1) * P], bblk[:, 1, lm, :],
                                           eb[:, 1, lm, 0:4, :].rearrange("p a b -> p (a b)"), start=False, stop=True)
                        close_fill(mm, nm)
                    if hf == 0:
                        pe.wait_ge(s["scan_done"], 1)
                    for i in range(4):
                        nm = f"Y{hf}{i}"
                        o = open_fill(nm)
                        drained(pe, f"K{hf}{i}")
                        for j in range(4):
                            lm, m = 4 * i + j, 16 * hf + 4 * i + j
                            out = o[:, j * 72:(j + 1) * 72]
                            pe.matmul(out, toep[:, lm, :], u4[:, m, 0:72], start=True, stop=False)
                            pe.matmul(out, eb[:, 0, lm, 1:5, :].rearrange("p a b -> p (a b)"), sv[:, 0:72, m],
                                      start=False, stop=False)
                            mm = pe.matmul(out, eb[:, 1, lm, 1:5, :].rearrange("p a b -> p (a b)"),
                                           sv[:, 0:72, 32 + m], start=False, stop=True)
                        close_fill(mm, nm)
                pe.wait_ge(s["newst_ready"], 1)
                o = open_fill("nss")
                for j in range(4):
                    mm = pe.transpose(o[:, j * P:(j + 1) * P],
                                      sv[:, 73 + 2 * j:75 + 2 * j, :].rearrange("p a b -> p (a b)"), ident)
                close_fill(mm, "nss")
                o = open_fill("nsp")
                close_fill(pe.transpose(o[0:64, 0:P], sv[:, 72, :], ident), "nsp")
                pe.wait_ge(s["dtw_in"], 16)
                o = open_fill("dt")
                for k in range(8):
                    mm = pe.matmul(o[0:HEADS, 0:TOK], dtw[:, k, :], xn[:, k, :], start=(k == 0), stop=(k == 7))
                close_fill(mm, "dt")
                named("z", xn)

                for i in range(4):
                    o = open_fill(f"rv{i}")
                    for j in range(4):
                        tb = i // 2
                        mm = pe.transpose(o[:, j * P:(j + 1) * P], v[:, 4 * (i % 2) + j, tb * P:(tb + 1) * P], ident)
                    close_fill(mm, f"rv{i}")
                pe.wait_ge(s["rope_done"], 8)
                for tb in range(2):
                    o = open_fill(f"rk{tb}")
                    for hh in range(4):
                        mm = pe.transpose(o[:, hh * P:(hh + 1) * P], qk[:, 4 + hh, tb * P:(tb + 1) * P], ident)
                    close_fill(mm, f"rk{tb}")

                def scores(name, keys, queries):
                    o = open_fill(name)
                    pe.matmul(o[:, 0:SEQ], keys[:, 0:P], queries[:, 0:SEQ], start=True, stop=True)
                    close_fill(pe.matmul(o[:, SEQ:SCORE_W], keys[:, P:SEQ], queries[:, P:SEQ],
                                         start=True, stop=True), name)

                for hh in range(4):
                    scores(f"rs{hh}", qk[:, 4 + hh, :], qk[:, hh, :])
                    o = open_fill(f"ry{hh}")
                    drained(pe, f"rs{hh}")
                    if hh == 0:
                        drained(pe, "rv3")
                    for ph in range(2):
                        vcol = (2 * hh + ph) * P
                        pe.matmul(o[:, ph * SEQ:(ph + 1) * SEQ], vtok[:, 0, vcol:vcol + P], sc[:, hh % 2, 0:SEQ],
                                  start=True, stop=False)
                        mm = pe.matmul(o[:, ph * SEQ + P:(ph + 1) * SEQ], vtok[:, 1, vcol:vcol + P],
                                       sc[:, hh % 2, SEQ:SCORE_W], start=False, stop=True)
                    close_fill(mm, f"ry{hh}")

                def end_states(name, half, left, right):
                    o = open_fill(name)
                    for j in range(4):
                        for tb in range(2):
                            mm = pe.matmul(o[:, j * P:(j + 1) * P], left(tb, 4 * half + j), right(tb, 4 * half + j),
                                           start=(tb == 0), stop=(tb == 1))
                    close_fill(mm, name)

                drained(pe, "rk1")
                for half in range(2):
                    end_states(f"rst{half}", half, lambda tb, b: vtok[:, tb, b * P:(b + 1) * P],
                               lambda tb, b: btok[:, tb, (b // 2) * P:(b // 2 + 1) * P])

                def token_rows(name, src):
                    o = open_fill(name)
                    for j in range(4):
                        mm = pe.transpose(o[0:SAMPLES, j * P:(j + 1) * P], src(j), ident)
                    close_fill(mm, name)

                def spread(name, rows, b):
                    o = open_fill(name)
                    close_fill(pe.matmul(o[:, 0:512], ident[0:SAMPLES, b:b + 1].to_broadcast([SAMPLES, P]), rows,
                                         start=True, stop=True), name)

                token_rows("rkT", lambda j: qk[:, 4 + j, SEQ:TOK])
                token_rows("rqT", lambda j: qk[:, j, SEQ:TOK])
                drained(pe, "rkT")
                drained(pe, "rqT")
                pe.wait_ge(s["gelu_done"], 8)
                for b in range(4):
                    spread(f"rkb{b}", rows_k, b)
                    spread(f"rqb{b}", rows_q, b)
                named("s5a", u)
                for b in range(4, 8):
                    spread(f"rkb{b}", rows_k, b)
                    spread(f"rqb{b}", rows_q, b)
                named("s5b", u)
                for hh in range(4):
                    sum_squares(f"rn{hh}", sq8, (2 * hh, 2 * hh + 1), "retsq", 2 * hh)
                named("gate0", xn)
                pe.wait_ge(s["dt_rows"], 4)
                o = open_fill("sc")
                for i, r in enumerate((DT_AC, DT_DELTA, DT_DW)):
                    for tb in range(2):
                        c = (2 * i + tb) * 16
                        pe.transpose(o[:, c:c + 16], dts[:, r, tb * P:(tb + 1) * P], ident[0:16, 0:16])
                for b in range(NB):
                    mm = pe.matmul(o[:, 96 + 17 * b:96 + 17 * b + 17], expand[0:HEADS, b, :], dts[:, DT_RHS, 0:17],
                                   start=True, stop=True)
                close_fill(mm, "sc")
                for i in range(4):
                    o = open_fill(f"sv{i}")
                    for j in range(4):
                        tb = i // 2
                        mm = pe.transpose(o[:, j * P:(j + 1) * P], xc[:, 4 * (i % 2) + j, tb * P:(tb + 1) * P], ident)
                    close_fill(mm, f"sv{i}")
                for tb in range(2):
                    o = open_fill(f"sb{tb}")
                    for gg in range(4):
                        mm = pe.transpose(o[:, gg * P:(gg + 1) * P], xc[:, 8 + gg, tb * P:(tb + 1) * P], ident)
                    close_fill(mm, f"sb{tb}")
                pe.wait_ge(s["ret_norm"], 8)
                named("reto", v)
                def head_decays(m):
                    o = open_fill(f"sa{m}")
                    for h2 in range(2):
                        mm = pe.matmul(o[:, h2 * SEQ:(h2 + 1) * SEQ],
                                       ident[0:HEADS, 2 * m + h2:2 * m + h2 + 1].to_broadcast([HEADS, P]),
                                       dts[:, DT_AC, 0:SEQ], start=True, stop=True)
                    close_fill(mm, f"sa{m}")

                scores("ss0", xc[:, 8, :], xc[:, 12, :])
                head_decays(0)
                for m in range(8):
                    if m % 2 and m < 7:
                        gg = (m + 1) // 2
                        scores(f"ss{gg}", xc[:, 8 + gg, :], xc[:, 12 + gg, :])
                    if m < 7:
                        head_decays(m + 1)
                    o = open_fill(f"sy{m}")
                    if m == 0:
                        drained(pe, "sv3")
                    for h2 in range(2):
                        pe.wait_ge(s["exp_masked"], 2 * m + h2 + 1)
                        hc = (2 * m + h2) * HEAD_DIM
                        pe.matmul(o[64 * h2:64 * h2 + 64, 0:SEQ], vtok[:, 0, hc:hc + HEAD_DIM], ex[:, h2, 0:SEQ],
                                  start=True, stop=False)
                        mm = pe.matmul(o[64 * h2:64 * h2 + 64, P:SEQ], vtok[:, 1, hc:hc + HEAD_DIM],
                                       ex[:, h2, SEQ:SCORE_W], start=False, stop=True)
                    close_fill(mm, f"sy{m}")
                drained(pe, "sb1")
                for half in range(2):
                    end_states(f"sst{half}", half, lambda tb, b: vw[:, tb, b * P:(b + 1) * P],
                               lambda tb, b: btok[:, tb, (b // 2) * P:(b // 2 + 1) * P])
                named("gate2", xn)
                token_rows("skT", lambda j: xc[:, 8 + j, SEQ:TOK])
                token_rows("sqT", lambda j: xc[:, 12 + j, SEQ:TOK])
                drained(pe, "skT")
                drained(pe, "sqT")
                for b in range(4):
                    spread(f"skb{b}", rows_k, b)
                    spread(f"sqb{b}", rows_q, b)
                named("gate1", xn)
                for b in range(4, 8):
                    spread(f"skb{b}", rows_k, b)
                    spread(f"sqb{b}", rows_q, b)
                for gg in range(4):
                    sum_squares(f"sn{gg}", sq8, (2 * gg, 2 * gg + 1), "ssdsq", 2 * gg)
                pe.wait_ge(s["ssd_norm"], 8)
                named("ssdo", xc[:, :, 0:TOK])
                pe.wait_ge(s["merged"], 8)
                named("wo", m_)
                sum_squares("n2", zr, range(NB), "squares", 8)
                pe.wait_ge(s["xn_ready"], 16)
                with pe.Fori(0, 4) as j:
                    unit(15 + j, at("up0") + 8 * j, xn)
                pe.wait_ge(s["hid_ready"], 32)
                with pe.Fori(0, 2) as jj:
                    for half in range(2):
                        for c in range(4):
                            pe.wait_ge(w_landed[c], (2 * jj + half) * 16 + 320)
                            for b in range(2):
                                if c == 0:
                                    pe.wait_ge(proj_drained, at("dn0") + 4 * jj + (2 * half + b - 3))
                                for k in range(8):
                                    mm = pe.matmul(banks[2 * half + b][:, 0:TOK], ring[:, c, k, b * P:(b + 1) * P],
                                                   hid[:, 8 * c + k, :], start=(c == 0 and k == 0),
                                                   stop=(c == 3 and k == 7))
                                if c == 3:
                                    mm.then_inc(proj_filled, 1)
                            if c < 3:
                                mm.then_inc(chunk_used, 1)

            @block.scalar
            def _(act):
                chain = Chain(act, act_step)

                def copy(out, in_, scale=1.0):
                    return nc.scalar.activation(out, in_, ACT.Copy, scale=scale)

                def tanh(out, in_, scale=0.5):
                    return nc.scalar.activation(out, in_, ACT.Tanh, scale=scale)

                def ret_tiles(name):
                    return layer_of(t[name], lyr).rearrange("b h (q p) n -> b p (h q) n", p=P)

                def ssd_tiles(name):
                    return layer_of(t[name], lyr).rearrange("b (k g) p n -> b (g p) k n", g=2)

                states = {"r": (ret_tiles("state_ret"), ret_tiles("new_ret_s")),
                          "s": (ssd_tiles("state_ssd"), ssd_tiles("new_ssd_s"))}

                def drain_unit(first, block_ops, blocks=8, bank0=0):
                    for b in range(blocks):
                        act.wait_ge(proj_filled, first + (b + 1))
                        block_ops(b, banks[(bank0 + b) % 4][:, 0:TOK]).then_inc(proj_drained, 1)

                def vec(name):
                    return layer_of(t[name], lyr)

                for name, row, n in (("norm1_w", PR_N1, 8), ("norm2_w", PR_N2, 8), ("s5_d", PR_D, 8),
                                     ("ssd_norm_w", PR_SN, 8), ("ssd_conv_b", PR_CB, 16)):
                    act.dma_start(vrow[row:row + n, :], vec(name).rearrange("(r p) -> r p", p=P)).then_inc(s["vec_in"], 16)
                act.dma_start(vrow[PR_CW:PR_FN, :], vec("ssd_conv_w").rearrange("t (r p) -> (t r) p", p=P))\
                   .then_inc(s["vec_in"], 16)
                act.dma_start(vrow[PR_FN:PR_ROWS, :], t["final_norm_w"].rearrange("(r p) -> r p", p=P))\
                   .then_inc(s["vec_in"], 16)
                act.dma_start(prow[:, 0, :], vec("s5_a_re").rearrange("(m g) p -> m (g p)", g=2)).then_inc(s["s5_in"], 16)
                act.dma_start(prow[:, 1, :], vec("s5_a_im").rearrange("(m g) p -> m (g p)", g=2)).then_inc(s["s5_in"], 16)
                act.dma_start(dtrow, vec("s5_log_dt").rearrange("(m g) -> m g", g=2)).then_inc(s["s5_in"], 16)
                for ri, name in enumerate(("s5_b_re", "s5_b_im")):
                    act.dma_start(braw[:, ri, :, :], vec(name).rearrange("(m g) p c -> (g p) m c", g=2))\
                       .then_inc(s["b_in"], 16)
                for ri, name in enumerate(("s5_c_re", "s5_c_im")):
                    for dup in range(2):
                        act.dma_start(craw[:, ri, :, dup * 64:(dup + 1) * 64],
                                      vec(name).rearrange("(t g) c p -> (g c) t p", g=8)).then_inc(s["c_in"], 16)
                for ri, name in enumerate(("state_s5_re", "state_s5_im")):
                    for b2 in range(2):
                        p0 = 64 * b2 + 32 * ri
                        act.dma_start(h0raw[p0:p0 + 32, :, :],
                                      vec(name).rearrange("(bp b) (m g) p -> b m bp (g p)", b=2, g=2)[b2])\
                           .then_inc(s["h0_in"], 16)
                act.dma_start(convst, vec("state_conv").rearrange("b t c -> (b t) c")).then_inc(s["convst_in"], 16)
                for i, name in enumerate(("ssd_dt_bias", "ssd_a_log", "ssd_d")):
                    act.dma_start(c16[0:HEADS, i:i + 1], vec(name).rearrange("(h o) -> h o", o=1)).then_inc(s["head_in"], 16)
                act.dma_start(dtw, vec("w_in").rearrange("(k p) n -> p k n", p=P)[:, :, COL_DT:COL_DT + HEADS])\
                   .then_inc(s["dtw_in"], 16)
                act.dma_start(vec("new_conv_s")[:, 0:TAPS - 2, :], vec("state_conv")[:, 1:TAPS - 1, :])\
                   .then_inc(s["tails_out"], 16)

                for k in range(NB):
                    nc.scalar.activation(zr[:, k, :], h[:, k, :], ACT.Square).then_inc(s["squares"], 1)
                filled(act, "prm")
                is_drained(copy(prm, bank("prm")[:, 0:PR_ROWS]), "prm")
                act.wait_ge(s["s5_in"], 48)
                nc.scalar.activation(dtrow, dtrow, ACT.Exp).then_inc(s["trig_ready"], 1)
                filled(act, "s5p")
                is_drained(copy(s5v, bank("s5p")[:, 0:P].rearrange("p (a b) -> p a b", a=4)), "s5p")
                drained(act, "s5p")
                nc.scalar.activation(trig[:, 7, 0, :], s5v[:, 2, :], ACT.Exp).then_inc(s["trig_ready"], 1)
                for ri, nm in enumerate(("cre", "cim")):
                    for i in range(2):
                        filled(act, f"{nm}{i}")
                        src = bank(f"{nm}{i}").rearrange("p (m g c) -> p m g c", g=2, c=16)
                        copy(ct[0:64, ri, 16 * i:16 * i + 16, :], src[0:64, :, 0, :])
                        is_drained(copy(ct[64:128, ri, 16 * i:16 * i + 16, :], src[64:128, :, 1, :]), f"{nm}{i}")
                filled(act, "h0")
                is_drained(copy(sv[:, 0:SAMPLES, :].rearrange("p a b -> p (a b)"), bank("h0")[:, :]), "h0")
                filled(act, "cs")
                is_drained(copy(xc[:, :, TAPS - 1 + SEQ:].rearrange("p k (b t) -> p k b t", t=TAPS)[:, :, :, 0:TAPS - 1],
                                bank("cs")[:, 0:24 * CB].rearrange("p (k b t) -> p k b t", k=CB, t=TAPS - 1)), "cs")
                act.wait_ge(s["trig_arg"], 1)
                nc.scalar.activation(trig[:, 5, :, :], trig[:, 6, :, :], ACT.Sin).then_inc(s["trig_ready"], 1)
                drain_unit(0, lambda b, ps: copy(u[:, b, :], ps))
                new0 = TAPS - 1 + SEQ + TAPS - 1
                with act.Fori(0, 2) as j:
                    def xbc(b, ps):
                        copy(xc[:, bass.ds(8 * j + b, 1), TAPS - 1:TAPS - 1 + SEQ], ps[:, None, 0:SEQ])
                        return copy(xc[:, bass.ds(8 * j + b, 1), new0:XC_W:TAPS], ps[:, None, SEQ:TOK])
                    drain_unit(8 * j + 8, xbc)
                act.wait_ge(proj_drained, 24)
                copy(tailc[:, :, 0:3], xc[:, :, SEQ:SEQ + 3]).then_inc(s["tail_ready"], 1)
                copy(tailc[:, :, 3:11], xc[:, :, new0:XC_W:TAPS]).then_inc(s["tail_ready"], 1)
                for i in range(4):
                    filled(act, f"tail{i}")
                    is_drained(copy(tailr[:, i * 512:(i + 1) * 512], bank(f"tail{i}")[0:11, :]), f"tail{i}")
                for i in range(4):
                    drained(act, f"tail{i}")
                act.dma_start(vec("new_conv_p").rearrange("b t c -> (b t) c"), tailr[0:3, :]).then_inc(s["tails_out"], 16)
                act.dma_start(vec("new_conv_s")[:, TAPS - 2, :], tailr[3:11, :]).then_inc(s["tails_out"], 16)
                for i in range(8):
                    for ri in range(2):
                        filled(act, f"V{2 * i + ri}")
                        c = 32 * ri + 4 * i
                        is_drained(copy(sv[:, 9:SLOTS, c:c + 4],
                                        bank(f"V{2 * i + ri}")[:, 0:288].rearrange("p (j k) -> p k j", j=4)),
                                   f"V{2 * i + ri}")
                act.wait_ge(s["tails_out"], 48)

                def qk_block(b, ps):
                    copy(qk[:, b, :], ps)
                    copy(zr[0:64, b, :], ps[64:128, :])
                    return copy(zr[64:128, b, :], ps[0:64, :])
                drain_unit(at("qk"), qk_block)
                for k in range(CB):
                    act.wait_ge(s["conv_y"], k + 1)
                    tanh(convy[:, k % 3, 1, :], convy[:, k % 3, 0, :], 1.0).then_inc(s["conv_t"], 1)
                drain_unit(at("v"), lambda b, ps: copy(v[:, b, :], ps))
                act.wait_ge(s["conv_silu"], 16)

                def g_block(b, ps):
                    act.wait_ge(s["rope_done"], b + 1)
                    copy(g[:, b, :], ps, 0.5)
                    return tanh(zr[:, b, :], ps)
                drain_unit(at("g"), g_block)
                for hf in range(2):
                    if hf == 1:
                        filled(act, "Y03")
                    for i in range(4):
                        filled(act, f"K{hf}{i}")
                        src = bank(f"K{hf}{i}")[0:32, :].rearrange("p (j c) -> p j c", j=4)
                        for r in range(LIFT):
                            ins = copy(toep[32 * r:32 * r + 32, 4 * i:4 * i + 4, 32 * r:P], src[:, :, 0:P - 32 * r])
                        is_drained(ins, f"K{hf}{i}")
                    act.wait_ge(s["g_silu"], 8)
                    for i in range(4):
                        filled(act, f"Y{hf}{i}")
                        ps = bank(f"Y{hf}{i}")
                        for mm in range(4):
                            rows = slice(32 * mm, 32 * mm + 32)
                            copy(zr[rows, 4 * hf + i, SEQ:TOK], ps[0:32, 72 * mm:72 * mm + 8])
                            for r in range(LIFT):
                                ins = copy(zr[rows, 4 * hf + i, r:SEQ:LIFT],
                                           ps[32 * r:32 * r + 32, 72 * mm + 8:72 * mm + 72])
                        is_drained(ins, f"Y{hf}{i}")
                filled(act, "nss")
                is_drained(copy(news.rearrange("p a b -> p (a b)"), bank("nss")[:, :]), "nss")
                filled(act, "nsp")
                is_drained(copy(newp, bank("nsp")[0:64, 0:P]), "nsp")
                drained(act, "nss")
                drained(act, "nsp")
                for ri, nm in enumerate(("re", "im")):
                    for b2 in range(2):
                        p0 = 64 * b2 + 32 * ri
                        act.dma_start(vec(f"new_s5_{nm}_s").rearrange("(bp b) (m g) p -> b m bp (g p)", b=2, g=2)[b2],
                                      news[p0:p0 + 32, :, :]).then_inc(s["s5st_out"], 16)
                    act.dma_start(vec(f"new_s5_{nm}_p").rearrange("b (m g) p -> (b m) (g p)", g=2),
                                  newp[32 * ri:32 * ri + 32, :]).then_inc(s["s5st_out"], 16)
                act.wait_ge(s["head_in"], 48)
                nc.scalar.activation(c16[0:HEADS, 3:4], c16[0:HEADS, 1:2], ACT.Exp).then_inc(s["alog_exp"], 1)
                act.wait_ge(s["dt_abs"], 1)
                nc.scalar.activation(dts[:, DT_E, :], dts[:, DT_E, :], ACT.Exp, scale=-1.0).then_inc(s["dt_exp"], 1)
                act.wait_ge(s["acum_ready"], 1)
                nc.scalar.activation(dts[:, DT_DW, 0:SEQ], dts[:, DT_AC, 0:SEQ], ACT.Exp, scale=-1.0,
                                     bias=dts[:, DT_AC, SEQ - 1:SEQ]).then_inc(s["wend_exp"], 1)
                nc.scalar.activation(dts[:, DT_RHS, 8:16], dts[:, DT_LA, SEQ:TOK], ACT.Exp).then_inc(s["dt_rows"], 1)

                def z_block(b, ps):
                    copy(zg[:, b, :], ps, 0.5)
                    return tanh(m_[:, b, :], ps)
                drain_unit(at("z"), z_block)
                for k in range(NB):
                    act.wait_ge(s["gelu_arg"], k + 1)
                    tanh(u[:, k, :], u[:, k, :], math.sqrt(2.0 / math.pi)).then_inc(s["gelu_tanh"], 1)
                for i in range(4):
                    filled(act, f"rv{i}")
                    is_drained(copy(vtok[:, i // 2, (i % 2) * 512:(i % 2) * 512 + 512], bank(f"rv{i}")[:, :]), f"rv{i}")
                for hh in range(4):
                    filled(act, f"ry{hh}")
                    is_drained(copy(v[:, 2 * hh:2 * hh + 2, 0:SEQ],
                                    bank(f"ry{hh}")[:, :].rearrange("p (a b) -> p a b", a=2)), f"ry{hh}")

                def store_states(pfx, dst):
                    for half in range(2):
                        filled(act, f"{pfx}{half}")
                        is_drained(copy(stout[:, 4 * half:4 * half + 4, :],
                                        bank(f"{pfx}{half}")[:, :].rearrange("p (a b) -> p a b", a=4)), f"{pfx}{half}")
                    for half in range(2):
                        drained(act, f"{pfx}{half}")
                    act.dma_start(dst, stout).then_inc(s["st_out"], 16)

                store_states("rst", vec("new_ret_p").rearrange("b h (q p) n -> p (b h q) n", p=P))
                act.wait_ge(s["s5st_out"], 96)

                def keep_rows(pfx):
                    filled(act, f"{pfx}kT")
                    is_drained(copy(rows_k, bank(f"{pfx}kT")[0:SAMPLES, :]), f"{pfx}kT")
                    filled(act, f"{pfx}qT")
                    is_drained(copy(rows_q, bank(f"{pfx}qT")[0:SAMPLES, :]), f"{pfx}qT")

                def load_state(pfx, b):
                    before = 4 * (pfx == "s") + b // 2
                    if before:
                        act.wait_ge(s[f"dec_out{b % 2}"], 16 * before)
                    act.dma_start(dec[:, b % 2, :, :], states[pfx][0][b]).then_inc(s[f"dec_in{b % 2}"], 16)

                def store_state(pfx, b):
                    drained(act, f"{pfx}qb{b}")
                    act.dma_start(states[pfx][1][b], dec[:, b % 2, :, :]).then_inc(s[f"dec_out{b % 2}"], 16)

                def outer_products(pfx, b, vcol):
                    filled(act, f"{pfx}kb{b}")
                    if b > 0:
                        store_state(pfx, b - 1)
                    elif pfx == "s":
                        drained(act, "rqb7")
                    for blk in range(NB):
                        c = (blk // 2) * P
                        ins = copy(outer[:, blk, :], bank(f"{pfx}kb{b}")[:, c:c + P], vcol(blk, b))
                    is_drained(ins, f"{pfx}kb{b}")
                    if 1 <= b < SAMPLES - 1:
                        load_state(pfx, b + 1)

                def ret_v(blk, b):
                    return v[:, blk, SEQ + b:SEQ + b + 1]

                load_state("r", 0)
                load_state("r", 1)
                keep_rows("r")
                for b in range(4):
                    outer_products("r", b, ret_v)
                act.wait_ge(s["gelu_done"], 8)
                drain_unit(at("s5a"), lambda b, ps: copy(zr[:, b, :], ps, 0.25))
                for b in range(4, 8):
                    outer_products("r", b, ret_v)
                store_state("r", 7)
                load_state("s", 0)
                load_state("s", 1)
                act.wait_ge(s["z_silu"], 8)
                drain_unit(at("s5b"), lambda b, ps: tanh(m_[:, b, :], ps, 0.25))
                act.wait_ge(s["ret_yc"], 1)
                for k in range(NB):
                    nc.scalar.activation(sq8[:, k, :], v[:, k, :], ACT.Square).then_inc(s["retsq"], 1)

                def gate0_block(b, ps):
                    act.wait_ge(s["gates_m"], b + 1)
                    return tanh(zr[:, b, :], ps)
                drain_unit(at("gate0"), gate0_block)
                filled(act, "sc")
                is_drained(copy(cols, bank("sc")[:, 0:232]), "sc")
                for tb in range(2):
                    filled(act, f"sb{tb}")
                    is_drained(copy(btok[:, tb, :], bank(f"sb{tb}")[:, :]), f"sb{tb}")
                drain_unit(at("reto"), lambda b, ps: copy(u[:, b, :], ps))
                for m in range(8):
                    drained(act, f"sa{m}")
                    if m >= 1:
                        filled(act, f"sy{m - 1}")
                    for h2 in range(2):
                        nc.scalar.activation(ex[:, h2, :], seg[:, h2, :], ACT.Exp).then_inc(s["exp_ready"], 1)
                act.wait_ge(s["st_out"], 16)
                store_states("sst", vec("new_ssd_p").rearrange("b (k g) p n -> (g p) (b k) n", g=2))

                def gate2_block(b, ps):
                    act.wait_ge(s["gates_m"], 9 + b)
                    return tanh(zr[:, b, :], ps)
                drain_unit(at("gate2"), gate2_block)

                def ssd_v(blk, b):
                    return vs[:, blk, b:b + 1]

                keep_rows("s")
                for b in range(4):
                    outer_products("s", b, ssd_v)
                drain_unit(at("gate1"), lambda b, ps: tanh(qk[:, b, :], ps))
                for b in range(4, 8):
                    outer_products("s", b, ssd_v)
                store_state("s", 7)
                for k in range(NB):
                    act.wait_ge(s["ssd_yz"], k + 1)
                    nc.scalar.activation(sq8[:, k, :], xc[:, k, 0:TOK], ACT.Square).then_inc(s["ssdsq"], 1)

                def ssdo_block(b, ps):
                    act.wait_ge(s["gates_m"], 17 + b)
                    return copy(u[:, b, :], ps)
                drain_unit(at("ssdo"), ssdo_block)
                drain_unit(at("wo"), lambda b, ps: copy(u[:, b, :], ps, 0.5))
                for k in range(NB):
                    act.wait_ge(s["resid"], k + 1)
                    nc.scalar.activation(zr[:, k, :], h[:, k, :], ACT.Square).then_inc(s["squares"], 1)
                with act.Fori(0, 4) as j:
                    drain_unit(at("up0") + 8 * j,
                               lambda b, ps: nc.scalar.activation(hid[:, bass.ds(8 * j + b, 1), :], ps[:, None, :], ACT.Relu))
                with act.Fori(0, 2) as jj:
                    drain_unit(at("dn0") + 4 * jj,
                               lambda b, ps: copy(u[:, bass.ds(4 * jj + b, 1), :], ps[:, None, :]), blocks=4)
                act.wait_ge(s["st_out"], 32)
                for b in range(2):
                    act.wait_ge(s[f"dec_out{b}"], 16 * 8)

            @block.vector
            def _(dve):
                chain = Chain(dve, dve_step)
                V = nc.vector

                def norm_scale(name, width, dst):
                    filled(dve, name)
                    is_drained(V.tensor_scalar(dst, bank(name)[:, 0:TOK], 1.0 / width, EPS, ALU.mult, ALU.add), name)

                def cmul(re, im, ar, ai, br, bi, tmp):
                    chain.step(V.tensor_tensor(tmp[0], ar, br, ALU.mult))
                    chain.step(V.tensor_tensor(tmp[1], ai, bi, ALU.mult))
                    chain.step(V.tensor_tensor(tmp[2], ar, bi, ALU.mult))
                    chain.step(V.tensor_tensor(tmp[3], ai, br, ALU.mult))
                    chain.wait()
                    chain.step(V.tensor_tensor(re, tmp[0], tmp[1], ALU.subtract))
                    chain.step(V.tensor_tensor(im, tmp[2], tmp[3], ALU.add))
                    chain.wait()

                drained(dve, "prm")
                V.tensor_scalar(prm[:, PR_CB:PR_FN], prm[:, PR_CB:PR_FN], 0.5, None, ALU.mult).then_inc(s["prm_ready"], 1)
                norm_scale("n1", D_MODEL, mean_sq)
                dve.wait_ge(s["trig_ready"], 1)
                dve.wait_ge(s["s5_in"], 48)
                for i in range(2):
                    V.tensor_tensor(prow[:, 2 + i, :].rearrange("p (g n) -> p g n", g=2),
                                    prow[:, i, :].rearrange("p (g n) -> p g n", g=2),
                                    dtrow[:, :, None].to_broadcast([PAIRS, 2, 64]), ALU.mult).then_inc(s["s5a_cols"], 1)
                dve.wait_ge(s["rstd_ready"], 1)
                dve.wait_ge(s["prm_ready"], 1)
                for k in range(NB):
                    V.scalar_tensor_tensor(xn[:, k, :], h[:, k, :], prm[:, PR_N1 + k:PR_N1 + k + 1], rstd,
                                           ALU.mult, ALU.mult).then_inc(s["xn_ready"], 1)
                drained(dve, "s5p")
                ang = s5v[:, 3, :]
                big = 12582912.0
                for i, turn in enumerate((0.0, 0.25)):
                    chain.step(V.tensor_scalar(trig[:, 0, i, :], ang, 1.0 / TWO_PI, turn, ALU.mult, ALU.add))
                chain.wait()
                chain.link(V.tensor_scalar(trig[:, 1, :, :], trig[:, 0, :, :], big, None, ALU.add))
                chain.link(V.tensor_scalar(trig[:, 0, :, :], trig[:, 1, :, :], big, None, ALU.subtract))
                c1 = 6.28125
                c2 = float(np.float32(np.floor((TWO_PI - c1) * 2.0 ** 21) / 2.0 ** 21))
                c3 = TWO_PI - c1 - c2
                for i in range(2):
                    chain.step(V.scalar_tensor_tensor(trig[:, 2, i, :], trig[:, 0, i, :], -c1, ang, ALU.mult, ALU.add))
                chain.wait()
                chain.link(V.scalar_tensor_tensor(trig[:, 3, :, :], trig[:, 0, :, :], -c2, trig[:, 2, :, :],
                                                  ALU.mult, ALU.add))
                chain.link(V.scalar_tensor_tensor(trig[:, 2, :, :], trig[:, 0, :, :], -c3, trig[:, 3, :, :],
                                                  ALU.mult, ALU.add))
                chain.link(V.tensor_scalar(trig[:, 2, 1, :], trig[:, 2, 1, :], math.pi / 2, None, ALU.add))
                V.tensor_scalar(trig[:, 6, :, :], trig[:, 2, :, :], 3.1415925, -3.1415925, ALU.min, ALU.max)\
                    .then_inc(s["trig_arg"], 1)
                lre, lim = s5v[:, 0, :], s5v[:, 1, :]
                chain.step(V.tensor_tensor(trig[:, 3, 0, :], lre, lre, ALU.mult))
                chain.step(V.tensor_tensor(trig[:, 3, 1, :], lim, lim, ALU.mult))
                chain.wait()
                chain.link(V.tensor_tensor(trig[:, 4, 0, :], trig[:, 3, 0, :], trig[:, 3, 1, :], ALU.add))
                chain.step(V.reciprocal(trig[:, 4, 1, :], trig[:, 4, 0, :]))
                chain.step(V.memset(pwr[:, 0, 0, :], 1.0))
                chain.step(V.memset(pwr[:, 0, 1, :], 0.0))
                dve.wait_ge(s["trig_ready"], 3)
                chain.step(V.tensor_tensor(pwr[:, 1, 0, :], trig[:, 7, 0, :], trig[:, 5, 1, :], ALU.mult))
                chain.step(V.tensor_tensor(pwr[:, 1, 1, :], trig[:, 7, 0, :], trig[:, 5, 0, :], ALU.mult))
                chain.wait()
                small4 = [trig[:, 1, 0, :], trig[:, 1, 1, :], trig[:, 2, 0, :], trig[:, 2, 1, :]]
                for e_, a_, b_ in ((2, 1, 1), (3, 2, 1), (4, 2, 2)):
                    cmul(pwr[:, e_, 0, :], pwr[:, e_, 1, :], pwr[:, a_, 0, :], pwr[:, a_, 1, :],
                         pwr[:, b_, 0, :], pwr[:, b_, 1, :], small4)
                for dst_r, dst_i, e_ in ((a4r, a4i, 4), (a1r, a1i, 1)):
                    for c in range(2):
                        chain.step(V.tensor_copy(dst_r[:, 32 * c:32 * c + 32], pwr[:, e_, 0, :]))
                    chain.step(V.tensor_scalar(dst_i[:, 32:64], pwr[:, e_, 1, :], -1.0, None, ALU.mult))
                    chain.step(V.tensor_copy(dst_i[:, 0:32], pwr[:, e_, 1, :]))
                chain.wait()
                chain.link(V.tensor_scalar(trig[:, 0, 0, :], pwr[:, 1, 0, :], 1.0, None, ALU.subtract))
                chain.step(V.tensor_tensor(trig[:, 1, 0, :], trig[:, 0, 0, :], lre, ALU.mult))
                chain.step(V.tensor_tensor(trig[:, 1, 1, :], pwr[:, 1, 1, :], lim, ALU.mult))
                chain.step(V.tensor_tensor(trig[:, 2, 0, :], pwr[:, 1, 1, :], lre, ALU.mult))
                chain.step(V.tensor_tensor(trig[:, 2, 1, :], trig[:, 0, 0, :], lim, ALU.mult))
                chain.wait()
                chain.step(V.tensor_tensor(trig[:, 3, 0, :], trig[:, 1, 0, :], trig[:, 1, 1, :], ALU.add))
                chain.step(V.tensor_tensor(trig[:, 3, 1, :], trig[:, 2, 0, :], trig[:, 2, 1, :], ALU.subtract))
                chain.wait()
                for i in range(2):
                    chain.step(V.tensor_tensor(qfac[:, i, :], trig[:, 3, i, :], trig[:, 4, 1, :], ALU.mult))
                chain.wait()
                V.tensor_copy(trig[:, 5, 0, :], trig[:, 3, 0, :]).then_inc(s["powers_ready"], 1)

                def pairwise(ap, n):
                    return ap[:, :, None].to_broadcast([P, n, 16])

                dve.wait_ge(s["b_in"], 32)
                cmul(bb[:, 0, :, :], bb[:, 1, :, :], pairwise(qfac[:, 0, :], PAIRS), pairwise(qfac[:, 1, :], PAIRS),
                     braw[:, 0, :, :], braw[:, 1, :, :], [btmp[:, i, :, :] for i in range(4)])
                dve.wait_ge(s["pool_zero"], 3)
                dve.wait_ge(proj_drained, 8)
                for mm in range(4):
                    src = u[32 * mm:32 * mm + 32, :, :]
                    for r in range(LIFT):
                        V.tensor_copy(u4[32 * r:32 * r + 32, mm:PAIRS:4, 8:72], src[:, :, r:SEQ:LIFT])
                    V.tensor_copy(u4[0:32, mm:PAIRS:4, 0:8], src[:, :, SEQ:TOK])
                    ins = V.tensor_copy(u4[96:128, mm:PAIRS:4, 72:80], src[:, :, SEQ:TOK])
                ins.then_inc(s["u4_ready"], 1)
                for sl in range(2):
                    if sl == 1:
                        filled(dve, "G7")
                    for r in range(LIFT):
                        e_ = LIFT - 1 - r
                        tmp = [btmp[:, i, 16 * (r % 2):16 * (r % 2) + 16, :] for i in range(4)]
                        lo, hi = 16 * sl, 16 * sl + 16
                        ar, ai = pairwise(pwr[:, e_, 0, lo:hi], 16), pairwise(pwr[:, e_, 1, lo:hi], 16)
                        chain.step(V.tensor_tensor(tmp[0], ar, bb[:, 0, lo:hi, :], ALU.mult))
                        chain.step(V.tensor_tensor(tmp[1], ai, bb[:, 1, lo:hi, :], ALU.mult))
                        chain.step(V.tensor_tensor(tmp[2], ar, bb[:, 1, lo:hi, :], ALU.mult))
                        chain.step(V.tensor_tensor(tmp[3], ai, bb[:, 0, lo:hi, :], ALU.mult))
                        chain.wait()
                        tb_ = [x[:, :, None, :].to_broadcast([P, 16, 2, 16]) for x in tmp]
                        out = bd.rearrange("p i m (r g c) -> p i m r g c", r=LIFT, g=2)
                        chain.step(V.tensor_tensor(out[:, 0, :, r, :, :], tb_[0], tb_[1], ALU.subtract))
                        ins = V.tensor_tensor(out[:, 1, :, r, :, :], tb_[2], tb_[3], ALU.add)
                        if r == LIFT - 1:
                            ins.then_inc(s["bd_ready"], 1)
                        else:
                            chain.step(ins)
                    for ri in range(2):
                        for i in range(4):
                            nm = f"G{8 * sl + 4 * ri + i}"
                            filled(dve, nm)
                            is_drained(V.tensor_tensor(gw[:, ri, 16 * sl + 4 * i:16 * sl + 4 * i + 4, :],
                                                       bank(nm)[:, :].rearrange("p (j c) -> p j c", j=4),
                                                       s5mask[:, None, :].to_broadcast([P, 4, P]), ALU.mult), nm)
                drained(dve, "cs")
                dve.wait_ge(proj_drained, 24)
                dve.wait_ge(s["tail_ready"], 2)

                def conv_silu(k):
                    dve.wait_ge(s["conv_t"], k + 1)
                    y, th = convy[:, k % 3, 0, :], convy[:, k % 3, 1, :]
                    V.scalar_tensor_tensor(xc[:, k, 0:SEQ], th[:, 0:SEQ], 1.0, y[:, 0:SEQ], ALU.add, ALU.mult)
                    first = TAPS - 1 + SEQ
                    V.scalar_tensor_tensor(xc[:, k, SEQ:TOK], th[:, first:CONV_OUT:TAPS], 1.0, y[:, first:CONV_OUT:TAPS],
                                           ALU.add, ALU.mult).then_inc(s["conv_silu"], 1)

                for k in range(CB):
                    y = convy[:, k % 3, 0, :]
                    w0 = PR_CW + k
                    chain.link(V.tensor_scalar(y, xc[:, k, 0:CONV_OUT], prm[:, w0:w0 + 1], prm[:, PR_CB + k:PR_CB + k + 1],
                                               ALU.mult, ALU.add))
                    for tap in range(1, TAPS):
                        wt = w0 + CB * tap
                        ins = V.scalar_tensor_tensor(y, xc[:, k, tap:tap + CONV_OUT], prm[:, wt:wt + 1], y,
                                                     ALU.mult, ALU.add)
                        if tap < TAPS - 1:
                            chain.link(ins)
                    ins.then_inc(s["conv_y"], 1)
                    if k >= 1:
                        conv_silu(k - 1)
                conv_silu(CB - 1)
                for k in range(NB):
                    dve.wait_ge(proj_drained, at("qk") + k + 1)
                    cs_, sn_ = (cosq, sinq) if k < 4 else (cosk, sink)
                    chain.step(V.tensor_tensor(qk[:, k, :], qk[:, k, :], cs_, ALU.mult))
                    chain.step(V.tensor_tensor(zr[:, k, :], zr[:, k, :], sn_, ALU.mult))
                    chain.wait()
                    V.tensor_tensor(qk[:, k, :], qk[:, k, :], zr[:, k, :], ALU.add).then_inc(s["rope_done"], 1)

                def output_matrices(hf):
                    lo, hi = 16 * hf, 16 * hf + 16
                    for tau in range(5):
                        pr, pi = pairwise(pwr[:, tau, 0, lo:hi], 16), pairwise(pwr[:, tau, 1, lo:hi], 16)
                        cr, ci = ct[:, 0, lo:hi, :], ct[:, 1, lo:hi, :]
                        chain.step(V.tensor_tensor(et[:, 0, :, :], cr, pr, ALU.mult))
                        chain.step(V.tensor_tensor(et[:, 1, :, :], ci, pi, ALU.mult))
                        chain.step(V.tensor_tensor(et[:, 2, :, :], cr, pi, ALU.mult))
                        chain.step(V.tensor_tensor(et[:, 3, :, :], ci, pr, ALU.mult))
                        chain.wait()
                        for g2 in range(2):
                            hv, cc = slice(64 * g2, 64 * g2 + 64), slice(16 * g2, 16 * g2 + 16)
                            chain.step(V.tensor_tensor(eb[hv, 0, :, tau, cc], et[hv, 0, :, :], et[hv, 1, :, :],
                                                       ALU.subtract))
                            chain.step(V.scalar_tensor_tensor(eb[hv, 1, :, tau, cc], et[hv, 2, :, :], -1.0,
                                                              et[hv, 3, :, :], ALU.mult, ALU.subtract))
                        chain.wait()
                    for g2 in range(2):
                        hv, cc = slice(64 * g2, 64 * g2 + 64), slice(16 * g2, 16 * g2 + 16)
                        for ri in range(2):
                            ins = V.tensor_copy(bblk[hv, ri, :, cc], bb[hv, ri, lo:hi, :])
                            if g2 + ri < 2:
                                chain.step(ins)
                    ins.then_inc(s["e_ready"], 1)

                filled(dve, "V12")
                filled(dve, "V13")
                filled(dve, "V14")
                filled(dve, "V15")
                for ri in range(4):
                    drained(dve, ("cre0", "cre1", "cim0", "cim1")[ri])
                chain.link(V.memset(view(O_GW, 8192), 0.0))
                output_matrices(0)
                for k in range(NB):
                    dve.wait_ge(proj_drained, at("g") + k + 1)
                    V.scalar_tensor_tensor(g[:, k, :], zr[:, k, :], 1.0, g[:, k, :], ALU.add, ALU.mult)\
                        .then_inc(s["g_silu"], 1)
                filled(dve, "Y03")
                output_matrices(1)
                for k in range(NB):
                    drained(dve, f"Y{k // 4}{k % 4}")
                    chain.link(V.scalar_tensor_tensor(zr[:, k, :], u[:, k, :], prm[:, PR_D + k:PR_D + k + 1], zr[:, k, :],
                                                      ALU.mult, ALU.add))
                    chain.link(V.scalar_tensor_tensor(u[:, k, :], zr[:, k, :], 0.044715, zr[:, k, :], ALU.mult, ALU.mult))
                    V.scalar_tensor_tensor(u[:, k, :], u[:, k, :], 1.0, zr[:, k, :], ALU.add, ALU.mult)\
                        .then_inc(s["gelu_arg"], 1)
                filled(dve, "dt")
                dve.wait_ge(s["head_in"], 48)
                X, E_, S_, DL, LA, AC, DW, RH = (dts[:, i, :] for i in range(8))
                is_drained(V.tensor_scalar(X, bank("dt")[0:HEADS, 0:TOK], c16[0:HEADS, 0:1], None, ALU.add), "dt")
                drained(dve, "dt")
                chain.link(V.tensor_scalar(S_, X, -1.0, None, ALU.mult))
                V.tensor_tensor(E_, X, S_, ALU.max).then_inc(s["dt_abs"], 1)
                dve.wait_ge(s["dt_exp"], 1)
                chain.link(V.tensor_scalar(S_, E_, 2.0, None, ALU.add))
                chain.link(V.reciprocal(DL, S_))
                chain.link(V.tensor_tensor(S_, E_, DL, ALU.mult))
                chain.link(V.tensor_tensor(E_, S_, S_, ALU.mult))
                chain.link(V.tensor_scalar(DL, E_, 1.0 / 17.0, None, ALU.mult))
                for n in (15, 13, 11, 9, 7, 5, 3):
                    chain.link(V.scalar_tensor_tensor(DL, DL, 1.0 / n, E_, ALU.add, ALU.mult))
                chain.link(V.scalar_tensor_tensor(DL, DL, 1.0, S_, ALU.add, ALU.mult))
                chain.link(V.tensor_scalar(E_, X, 0.0, None, ALU.max))
                chain.link(V.scalar_tensor_tensor(DL, DL, 2.0, E_, ALU.mult, ALU.add))
                dve.wait_ge(s["alog_exp"], 1)
                chain.link(V.tensor_scalar(LA, DL, c16[0:HEADS, 3:4], -1.0, ALU.mult, ALU.mult))
                V.tensor_tensor_scan(AC[:, 0:SEQ], ones[0:HEADS, 0:1].to_broadcast([HEADS, SEQ]), LA[:, 0:SEQ], 0.0,
                                     ALU.mult, ALU.add).then_inc(s["acum_ready"], 1)
                V.tensor_copy(RH[:, 0:8], DL[:, SEQ:TOK]).then_inc(s["dt_rows"], 1)
                V.tensor_copy(RH[:, 16:17], c16[0:HEADS, 2:3]).then_inc(s["dt_rows"], 1)
                dve.wait_ge(s["wend_exp"], 1)
                V.tensor_tensor(DW[:, 0:SEQ], DW[:, 0:SEQ], DL[:, 0:SEQ], ALU.mult).then_inc(s["dt_rows"], 1)
                for k in range(NB):
                    dve.wait_ge(s["gelu_tanh"], k + 1)
                    V.scalar_tensor_tensor(u[:, k, :], u[:, k, :], 1.0, zr[:, k, :], ALU.add, ALU.mult)\
                        .then_inc(s["gelu_done"], 1)
                for k in range(NB):
                    dve.wait_ge(proj_drained, at("z") + k + 1)
                    V.scalar_tensor_tensor(zg[:, k, :], m_[:, k, :], 1.0, zg[:, k, :], ALU.add, ALU.mult)\
                        .then_inc(s["z_silu"], 1)
                for tb in range(2):
                    filled(dve, f"rk{tb}")
                    is_drained(V.tensor_tensor(btok[:, tb, :].rearrange("p (a b) -> p a b", a=4),
                                               bank(f"rk{tb}")[:, :].rearrange("p (a b) -> p a b", a=4),
                                               wend[:, tb, :][:, :, None].to_broadcast([P, RET_H, P]), ALU.mult), f"rk{tb}")
                for hh in range(4):
                    filled(dve, f"rs{hh}")
                    if hh >= 2:
                        filled(dve, f"ry{hh - 2}")
                    is_drained(V.tensor_tensor(sc[:, hh % 2, :], bank(f"rs{hh}")[:, 0:SCORE_W], decay[:, hh, :], ALU.mult),
                               f"rs{hh}")

                def advance(pfx, nth, b, factor):
                    drained(dve, f"{pfx}kb{b}")
                    dve.wait_ge(s[f"dec_in{b % 2}"], 16 * (4 * nth + b // 2 + 1))
                    for blk in range(NB):
                        st = dec[:, b % 2, blk, :]
                        chain.step(V.scalar_tensor_tensor(st, st, factor(blk, b), outer[:, blk, :], ALU.mult, ALU.add))
                    chain.wait()
                    filled(dve, f"{pfx}qb{b}")
                    for blk in range(NB):
                        c = (blk // 2) * P
                        ins = V.tensor_tensor_reduce(outer[:, blk, :], dec[:, b % 2, blk, :],
                                                     bank(f"{pfx}qb{b}")[:, c:c + P], 1.0, 0.0, ALU.mult, ALU.add,
                                                     ys[:, blk, b:b + 1])
                    is_drained(ins, f"{pfx}qb{b}")

                for b in range(8):
                    advance("r", 0, b, lambda blk, b: gam[blk // 2])
                drained(dve, "rqb7")
                V.tensor_copy(v[:, :, SEQ:TOK], ys).then_inc(s["ret_yc"], 1)
                for k in range(NB):
                    dve.wait_ge(proj_drained, at("s5b") + k + 1)
                    V.scalar_tensor_tensor(m_[:, k, :], m_[:, k, :], 1.0, zr[:, k, :], ALU.add, ALU.mult)\
                        .then_inc(s["gates_m"], 1)
                for hh in range(4):
                    norm_scale(f"rn{hh}", RET_P, gms)
                    dve.wait_ge(s["rstd_ready"], 2 + hh)
                    for k in (2 * hh, 2 * hh + 1):
                        chain.step(V.tensor_tensor(v[:, k, :], v[:, k, :], grs, ALU.mult))
                    chain.wait()
                    for k in (2 * hh, 2 * hh + 1):
                        V.tensor_tensor(v[:, k, :], v[:, k, :], g[:, k, :], ALU.mult).then_inc(s["ret_norm"], 1)
                dve.wait_ge(s["gates_m"], 8)
                for k in range(NB):
                    dve.wait_ge(proj_drained, at("gate0") + k + 1)
                    V.scalar_tensor_tensor(m_[:, k, :], zr[:, k, :], 1.0, m_[:, k, :], ALU.add, ALU.mult)\
                        .then_inc(s["gates_m"], 1)
                drained(dve, "sc")
                per_block = cols[:, 96:232].rearrange("p (k n) -> p k n", k=NB)
                chain.step(V.tensor_tensor(vs, xc[:, 0:NB, SEQ:TOK], per_block[:, :, 0:8], ALU.mult))
                for i in range(4):
                    filled(dve, f"sv{i}")
                    tb, half = i // 2, i % 2
                    src = bank(f"sv{i}")[:, :].rearrange("p (a b) -> p a b", a=8)

                    def weight(row):
                        c = (2 * row + tb) * 16 + 8 * half
                        return cols[:, c:c + 8][:, :, None].to_broadcast([P, 8, HEAD_DIM])

                    def half_of(dst):
                        return dst[:, tb, half * 512:half * 512 + 512].rearrange("p (a b) -> p a b", a=8)
                    V.tensor_tensor(half_of(vtok), src, weight(1), ALU.mult)
                    is_drained(V.tensor_tensor(half_of(vw), src, weight(2), ALU.mult), f"sv{i}")

                def masked_scores(gg):
                    filled(dve, f"ss{gg}")
                    if gg >= 2:
                        dve.wait_ge(s["exp_masked"], 4 * (gg - 1))
                    elif gg == 0:
                        filled(dve, "ry2")
                        filled(dve, "ry3")
                    is_drained(V.tensor_tensor(sc[:, gg % 2, :], bank(f"ss{gg}")[:, 0:SCORE_W], causal, ALU.mult),
                               f"ss{gg}")

                def log_decays(m):
                    filled(dve, f"sa{m}")
                    if m >= 1:
                        dve.wait_ge(s["exp_ready"], 2 * m)
                    for h2 in range(2):
                        hd = 2 * m + h2
                        src = bank(f"sa{m}")[:, h2 * SEQ:(h2 + 1) * SEQ]
                        V.tensor_scalar(seg[:, h2, 0:SEQ], src, cols[:, hd:hd + 1], 0.0, ALU.subtract, ALU.min)
                        ins = V.tensor_scalar(seg[:, h2, SEQ:SCORE_W], src[:, P:SEQ], cols[:, 16 + hd:17 + hd], 0.0,
                                              ALU.subtract, ALU.min)
                    is_drained(ins, f"sa{m}")

                masked_scores(0)
                log_decays(0)
                for m in range(8):
                    if m % 2 and m < 7:
                        masked_scores((m + 1) // 2)
                    if m < 7:
                        log_decays(m + 1)
                    filled(dve, f"sy{m}")
                    is_drained(V.scalar_tensor_tensor(xc[:, m, 0:SEQ], xc[:, m, 0:SEQ], per_block[:, m, 16:17],
                                                      bank(f"sy{m}")[:, 0:SEQ], ALU.mult, ALU.add), f"sy{m}")
                for k in range(NB):
                    dve.wait_ge(proj_drained, at("gate2") + k + 1)
                    chain.link(V.scalar_tensor_tensor(u[:, k, :], zr[:, k, :], 1.0, u[:, k, :], ALU.add, ALU.mult))
                    V.tensor_tensor(m_[:, k, :], m_[:, k, :], u[:, k, :], ALU.add).then_inc(s["gates_m"], 1)
                for b in range(8):
                    advance("s", 1, b, lambda blk, b: per_block[:, blk, 8 + b:9 + b])
                chain.step(V.tensor_tensor(vs, xc[:, 0:NB, SEQ:TOK],
                                           per_block[:, :, 16:17].to_broadcast([P, NB, SAMPLES]), ALU.mult))
                drained(dve, "sqb7")
                chain.wait()
                for i in range(8):
                    drained(dve, f"sy{i}")
                chain.link(V.tensor_tensor(xc[:, 0:NB, SEQ:TOK], vs, ys, ALU.add))
                for k in range(NB):
                    V.tensor_tensor(xc[:, k, 0:TOK], xc[:, k, 0:TOK], zg[:, k, :], ALU.mult).then_inc(s["ssd_yz"], 1)
                for gg in range(4):
                    norm_scale(f"sn{gg}", 2 * P, gms)
                    dve.wait_ge(s["rstd_ready"], 6 + gg)
                    for k in (2 * gg, 2 * gg + 1):
                        V.scalar_tensor_tensor(xc[:, k, 0:TOK], xc[:, k, 0:TOK], prm[:, PR_SN + k:PR_SN + k + 1], grs,
                                               ALU.mult, ALU.mult).then_inc(s["ssd_norm"], 1)
                for k in range(NB):
                    dve.wait_ge(proj_drained, at("ssdo") + k + 1)
                    chain.link(V.scalar_tensor_tensor(u[:, k, :], qk[:, k, :], 1.0, u[:, k, :], ALU.add, ALU.mult))
                    V.tensor_tensor(m_[:, k, :], m_[:, k, :], u[:, k, :], ALU.add).then_inc(s["merged"], 1)
                for k in range(NB):
                    dve.wait_ge(proj_drained, at("wo") + k + 1)
                    V.tensor_tensor(h[:, k, :], h[:, k, :], u[:, k, :], ALU.add).then_inc(s["resid"], 1)
                norm_scale("n2", D_MODEL, mean_sq)
                dve.wait_ge(s["rstd_ready"], 10)
                for k in range(NB):
                    V.scalar_tensor_tensor(xn[:, k, :], h[:, k, :], prm[:, PR_N2 + k:PR_N2 + k + 1], rstd,
                                           ALU.mult, ALU.mult).then_inc(s["xn_ready"], 1)
                with dve.Fori(0, 4) as j:
                    for b in range(8):
                        dve.wait_ge(proj_drained, at("up0") + 8 * j + (b + 1))
                        hb = hid[:, bass.ds(8 * j + b, 1), :]
                        V.tensor_tensor(hb, hb, hb, ALU.mult).then_inc(s["hid_ready"], 1)
                with dve.Fori(0, 2) as jj:
                    for b in range(4):
                        dve.wait_ge(proj_drained, at("dn0") + 4 * jj + (b + 1))
                        hb = h[:, bass.ds(4 * jj + b, 1), :]
                        V.tensor_tensor(hb, hb, u[:, bass.ds(4 * jj + b, 1), :], ALU.add)

            @block.gpsimd
            def _(pool):
                G = nc.gpsimd
                chain = Chain(pool, pool_step)
                G.memset(view(O_U4, PAIRS * U4_W), 0.0).then_inc(s["pool_zero"], 1)
                pool.wait_ge(s["pool_zero"], 1)
                G.memset(sv[:, 8, :], 0.0).then_inc(s["pool_zero"], 1)
                pool.wait_ge(s["pool_zero"], 2)
                G.memset(xc[:, :, 0:TAPS - 1], 0.0).then_inc(s["pool_zero"], 1)

                def inverse_root(name, src, dst):
                    drained(pool, name)
                    G.tensor_tensor(dst, src, mhalf.to_broadcast([P, TOK]), ALU.pow).then_inc(s["rstd_ready"], 1)

                pool.wait_ge(s["pool_zero"], 3)
                inverse_root("n1", mean_sq, rstd)
                pool.wait_ge(s["rstd_ready"], 1)
                p1, p2 = trig[:, 2, :, :], trig[:, 3, :, :]
                pool.wait_ge(s["powers_ready"], 1)
                for i in range(12, 16):
                    drained(pool, f"V{i}")

                chain.link(G.memset(p1, 0.0))

                with pool.Fori(0, CHUNKS) as k:
                    now = sv[:, bass.ds(k + 8, 1), :].rearrange("p o (i m) -> p (o i) m", i=2)
                    new = sv[:, bass.ds(k + 9, 1), :].rearrange("p o (i m) -> p (o i) m", i=2)
                    wide = lambda ap: ap.rearrange("p (i m) -> p i m", i=2)
                    G.tensor_tensor(p1, wide(a4r), now, ALU.mult).then_inc(s["scan_step"], 1)
                    G.tensor_tensor(p2[:, ::-1, :], wide(a4i), now, ALU.mult).then_inc(s["scan_step"], 1)
                    pool.wait_ge(s["scan_step"], 1)
                    G.tensor_tensor(new, new, p1, ALU.add).then_inc(s["scan_step"], 1)
                    pool.wait_ge(s["scan_step"], 3)
                    G.tensor_tensor(new, new, p2, ALU.add).then_inc(s["scan_step"], 1)
                    pool.wait_ge(s["scan_step"], 4)
                    pool.sem_clear(s["scan_step"])
                G.memset(p1, 0.0).then_inc(s["scan_done"], 1)
                pool.wait_ge(s["scan_done"], 1)
                prod = trig.rearrange("p a b c -> p (a b c)").rearrange("p (s i m) -> p s i m", s=SAMPLES, i=2)
                h0 = sv[:, 0:SAMPLES, :].rearrange("p s (i m) -> p s i m", i=2)
                add = sv[:, 73:81, :].rearrange("p s (i m) -> p s i m", i=2)
                fac = lambda ap: ap.rearrange("p (i m) -> p i m", i=2)[:, None, :, :].to_broadcast([P, SAMPLES, 2, PAIRS])
                chain.link(G.tensor_tensor(prod, h0, fac(a1r), ALU.mult))
                chain.link(G.tensor_tensor(add, add, prod, ALU.add))
                chain.link(G.tensor_tensor(prod[:, :, ::-1, :], h0, fac(a1i), ALU.mult))
                G.tensor_tensor(add, add, prod, ALU.add).then_inc(s["newst_ready"], 1)

                for hh in range(4):
                    inverse_root(f"rn{hh}", gms, grs)
                for hd in range(HEADS):
                    pool.wait_ge(s["exp_ready"], hd + 1)
                    if hd % 4 == 0:
                        drained(pool, f"ss{hd // 4}")
                    G.tensor_tensor(ex[:, hd % 2, :], ex[:, hd % 2, :], sc[:, (hd // 4) % 2, :], ALU.mult)\
                        .then_inc(s["exp_masked"], 1)
                for gg in range(4):
                    inverse_root(f"sn{gg}", gms, grs)
                inverse_root("n2", mean_sq, rstd)

        with nc.Fori(0, DEPTH) as lyr:
            with nc.Block() as block:
                layer(nc, block, t, lyr)
            nc.all_engine_barrier(sems_to_clear=sem_range)

        fms, frs = view(O_G, TOK), view(O_G + TOK, TOK)
        ytok = view(O_R, 2, D_MODEL)
        ysam = view(O_R + 2 * D_MODEL, D_MODEL, p1=SAMPLES)
        with nc.Block() as block:
            @block.scalar
            def _(act):
                for k in range(NB):
                    nc.scalar.activation(zr[:, k, :], h[:, k, :], ACT.Square).then_inc(s["squares"], 1)
                for i in range(6):
                    act.wait_ge(proj_filled, 2 + i)
                    src = banks[(1 + i) % 4]
                    if i < 4:
                        ins = nc.scalar.activation(ytok[:, i // 2, (i % 2) * 512:(i % 2) * 512 + 512], src[:, :], ACT.Copy)
                    else:
                        ins = nc.scalar.activation(ysam[:, (i % 2) * 512:(i % 2) * 512 + 512], src[0:SAMPLES, :], ACT.Copy)
                    ins.then_inc(s["y_rows"], 1)

            @block.tensor
            def _(pe):
                for k in range(NB):
                    pe.wait_ge(s["squares"], k + 1)
                    mm = pe.matmul(banks[0][:, 0:TOK], ones, zr[:, k, :], start=(k == 0), stop=(k == NB - 1))
                mm.then_inc(proj_filled, 1)
                pe.wait_ge(s["xn_ready"], 8)
                for i in range(6):
                    if i == 3:
                        pe.wait_ge(s["mean_ready"], 1)
                    elif i > 3:
                        pe.wait_ge(s["y_rows"], i - 3)
                    dst = banks[(1 + i) % 4]
                    for j in range(4):
                        k = 4 * (i % 2) + j
                        if i < 4:
                            mm = pe.transpose(dst[:, j * P:(j + 1) * P], xn[:, k, (i // 2) * P:(i // 2 + 1) * P], ident)
                        else:
                            mm = pe.transpose(dst[0:SAMPLES, j * P:(j + 1) * P], xn[:, k, SEQ:TOK], ident)
                    mm.then_inc(proj_filled, 1)

            @block.gpsimd
            def _(pool):
                pool.wait_ge(s["mean_ready"], 1)
                nc.gpsimd.tensor_tensor(frs, fms, mhalf.to_broadcast([P, TOK]), ALU.pow).then_inc(s["rstd_ready"], 1)

            @block.vector
            def _(dve):
                dve.wait_ge(proj_filled, 1)
                nc.vector.tensor_scalar(fms, banks[0][:, 0:TOK], 1.0 / D_MODEL, EPS, ALU.mult, ALU.add)\
                    .then_inc(s["mean_ready"], 1)
                dve.wait_ge(s["rstd_ready"], 1)
                for k in range(NB):
                    nc.vector.scalar_tensor_tensor(xn[:, k, :], h[:, k, :], prm[:, PR_FN + k:PR_FN + k + 1], frs,
                                                   ALU.mult, ALU.mult).then_inc(s["xn_ready"], 1)

            @block.sync
            def _(sp):
                sp.wait_ge(s["y_rows"], 4)
                sp.dma_start(t["y_prompt"].rearrange("o (tb p) d -> p (o tb) d", p=P), ytok).then_inc(s["y_out"], 16)
                sp.wait_ge(s["y_rows"], 6)
                sp.dma_start(t["y_sample"].rearrange("b o d -> (b o) d"), ysam).then_inc(s["y_out"], 16)
                sp.wait_ge(s["y_out"], 32)


_INS = ["x_prompt", "x_sample", "state_s5_re", "state_s5_im", "state_ssd", "state_conv", "state_ret", "norm1_w", "w_in",
        "s5_a_re", "s5_a_im", "s5_log_dt", "s5_b_re", "s5_b_im", "s5_c_re", "s5_c_im", "s5_d", "w_s5_out",
        "ssd_conv_w", "ssd_conv_b", "ssd_dt_bias", "ssd_a_log", "ssd_d", "ssd_norm_w", "w_ssd_out", "w_ret_out",
        "w_out", "norm2_w", "w_mlp_up", "w_mlp_down", "final_norm_w"]
_OUTS = [("y_prompt", (1, SEQ, D_MODEL)), ("y_sample", (SAMPLES, 1, D_MODEL))]
for _sfx, _b in (("p", 1), ("s", SAMPLES)):
    _OUTS += [(f"new_s5_re_{_sfx}", (DEPTH, _b, S5_GROUPS, S5_STATE)), (f"new_s5_im_{_sfx}", (DEPTH, _b, S5_GROUPS, S5_STATE)),
              (f"new_ssd_{_sfx}", (DEPTH, _b, HEADS, HEAD_DIM, SSD_N)), (f"new_conv_{_sfx}", (DEPTH, _b, TAPS - 1, CONV_DIM)),
              (f"new_ret_{_sfx}", (DEPTH, _b, RET_H, RET_P, RET_N))]


def kernel(**inputs):
    import numpy as _np
    import concourse.bacc as _bacc
    from concourse.bass_utils import run_bass_kernel_spmd as _run

    nc = _bacc.Bacc("TRN2", target_bir_lowering=False, num_devices=1)
    arrays, t = {}, {}
    for name in _INS:
        a = _np.ascontiguousarray(inputs[name])
        arrays[f"in_{name}"] = a
        t[name] = nc.dram_tensor(f"in_{name}", a.shape, F32, kind="ExternalInput").ap()
    arrays["in_consts"] = constant_table()
    t["consts"] = nc.dram_tensor("in_consts", (P, CONST_W), F32, kind="ExternalInput").ap()
    for name, shape in _OUTS:
        t[name] = nc.dram_tensor(f"out_{name}", shape, F32, kind="ExternalOutput").ap()
    build_trunk(nc, t)
    r = _run(nc, [arrays], core_ids=[0])
    return tuple(r.results[0][f"out_{name}"] for name, _ in _OUTS)
```

```python
import math
from contextlib import ExitStack

import numpy as np

import concourse.bass as bass
from concourse import mybir

F32 = mybir.dt.float32
ALU = mybir.AluOpType
ACT = mybir.ActivationFunctionType

P = 128
D_MODEL = 1024
SEQ = 256
DEPTH = 2
SAMPLES = 8
PAST_LEN = 2048
TOK = SEQ + SAMPLES
NB = D_MODEL // P
D_FF = 4096
S5_GROUPS, S5_STATE, S5_CH = 64, 64, 16
PAIRS = S5_GROUPS // 2
LIFT = 4
CHUNKS = SEQ // LIFT
HEADS, HEAD_DIM, SSD_G, SSD_N = 16, 64, 4, 128
CONV_DIM = 2048
CB = CONV_DIM // P
TAPS = 4
XC_W = TAPS - 1 + SEQ + SAMPLES * TAPS
CONV_OUT = XC_W - (TAPS - 1)
RET_H, RET_N, RET_P = 4, 128, 256
ROPE_BASE = 10000.0
EPS = 1e-6
N_IN = 10256
COL_U, COL_Z, COL_X, COL_DT, COL_QK, COL_V, COL_G, COL_GATE = 0, 1024, 2048, 4096, 4112, 5136, 6160, 7184
SCORE_W = SEQ + P
RING = 4
TWO_PI = 2.0 * math.pi

C_IDENT, C_ONES, C_MASK = 0, 128, 256
C_COSQ, C_SINQ, C_COSK, C_SINK = 384, 648, 912, 1176
C_DECAY = 1440
C_CAUSAL = C_DECAY + RET_H * SCORE_W
C_EXPAND = C_CAUSAL + SCORE_W
C_WEND = C_EXPAND + NB * P
C_EPS = C_WEND + 2 * RET_H
CONST_W = C_EPS + 1


def retention_gammas():
    return [1.0 - 2.0 ** (-5.0 - h) for h in range(RET_H)]


def constant_table():
    t = np.zeros((P, CONST_W), np.float64)
    t[:, C_IDENT:C_IDENT + P] = np.eye(P)
    t[:, C_ONES:C_ONES + P] = 1.0
    row = np.arange(P)
    t[:, C_MASK:C_MASK + P] = ((row[:, None] // 16) % 2) == (row[None, :] // 64)
    half = RET_N // 2
    pos = np.concatenate([np.arange(SEQ), np.full(SAMPLES, PAST_LEN)]).astype(np.float64)
    inv = ROPE_BASE ** (-np.arange(half) / half)
    ang = inv[:, None] * pos[None, :]
    cos = np.concatenate([np.cos(ang), np.cos(ang)])
    sin = np.concatenate([-np.sin(ang), np.sin(ang)])
    t[:, C_COSQ:C_COSQ + TOK] = cos
    t[:, C_SINQ:C_SINQ + TOK] = sin
    t[:, C_COSK:C_COSK + TOK] = cos * RET_N ** -0.5
    t[:, C_SINK:C_SINK + TOK] = sin * RET_N ** -0.5
    dist = np.arange(SEQ)[None, :] - row[:, None]
    causal = (dist >= 0).astype(np.float64)
    for h, gamma in enumerate(retention_gammas()):
        decay = np.where(dist >= 0, gamma ** np.maximum(dist, 0), 0.0)
        t[:, C_DECAY + h * SCORE_W:C_DECAY + (h + 1) * SCORE_W] = np.concatenate([decay, decay[:, :P]], 1)
        for tb in range(2):
            t[:, C_WEND + tb * RET_H + h] = gamma ** (SEQ - 1 - tb * P - row)
    t[:, C_CAUSAL:C_CAUSAL + SCORE_W] = np.concatenate([causal, causal[:, :P]], 1)
    for m in range(NB):
        for h2 in range(2):
            t[2 * m + h2, C_EXPAND + m * P + h2 * 64:C_EXPAND + m * P + (h2 + 1) * 64] = 1.0
    t[:, C_EPS] = EPS
    return t.astype(np.float32)


O_CONST = 0
O_PRM = O_CONST + CONST_W
PRM_W = 600
O_H = O_PRM + PRM_W
O_XN = O_H + NB * TOK
O_RING = O_XN + NB * TOK
CHUNK_W = 8 * 256
O_U = O_RING + RING * CHUNK_W
O_Z = O_U + NB * TOK
O_G = O_Z + NB * TOK
O_QK = O_G + NB * TOK
O_V = O_QK + NB * TOK
O_XC = O_V + NB * TOK
O_R = O_XC + CB * XC_W
SLOTS = 1 + CHUNKS + 2 * SAMPLES
U4_W = CHUNKS + 2 * SAMPLES
O_SV = O_R
O_U4 = O_SV + SLOTS * 64
O_GW = O_U4 + PAIRS * U4_W
O_BB = O_GW + 8192
O_CT = O_BB + 1024
O_SM = O_CT + 1024
O_DTS = O_R
O_VTOK = O_DTS + 8 * TOK
O_VW = O_VTOK + 2048
O_BTOK = O_VW + 2048
O_SC = O_BTOK + 1024
O_SEG = O_SC + 2 * SCORE_W
O_EXP = O_SEG + 2 * SCORE_W
O_DEC = O_EXP + 2 * SCORE_W
O_TMP = O_DEC + 2048
O_STOUT = O_TMP + 1024
O_ZG = O_STOUT + 1024
O_M = O_ZG + NB * TOK
SB_W = max(O_SM + 2048, O_M + NB * TOK)
O_HID = O_R

UNITS = ["u", "x0", "x1", "qk", "v", "g", "z", "s5a", "s5b", "gate0", "reto", "gate2", "gate1", "ssdo", "wo",
         "up0", "up1", "up2", "up3", "dn0", "dn1", "dn2", "dn3"]
BLOCKS = {}
_at = 0
for _n in UNITS:
    BLOCKS[_n] = _at
    _at += 2 if _n.startswith("dn") else 8

MIXER_FILLS = (
    ["prm", "n1", "s5p", "cre0", "cre1", "cim0", "cim1", "h0", "cs"]
    + [f"G{i}" for i in range(16)] + [f"V{i}" for i in range(16)] + [f"tail{i}" for i in range(4)]
    + [f for hf in range(2) for f in ([f"K{hf}{i}" for i in range(4)] + [f"Y{hf}{i}" for i in range(4)])]
    + ["nss", "nsp", "dt"]
    + [f"rv{i}" for i in range(4)] + ["rs0", "rs1", "rk0", "rk1", "ry0", "rs2", "ry1", "rs3", "ry2", "ry3", "rst0", "rst1"]
    + [f for b in range(8) for f in (f"rkb{b}", f"rqb{b}")] + [f"rn{h}" for h in range(4)]
    + ["sc"] + [f"sv{i}" for i in range(4)] + ["sb0", "sb1"]
    + ["ss0", "sa0"]
    + [f for m in range(8) for f in (([f"ss{(m + 1) // 2}"] if m % 2 and m < 7 else [])
                                     + ([f"sa{m + 1}"] if m < 7 else []) + [f"sy{m}"])]
    + ["sst0", "sst1"]
    + [f for b in range(8) for f in (f"skb{b}", f"sqb{b}")] + [f"sn{h}" for h in range(4)]
    + ["n2"]
)
TURN = MIXER_FILLS.index("Y00") % 4
FILL = {n: ((i - TURN) % 4, i // 4 + 1) for i, n in enumerate(MIXER_FILLS)}

PR_N1, PR_N2, PR_D, PR_SN, PR_CB, PR_CW, PR_FN, PR_ROWS = 0, 8, 16, 24, 32, 48, 112, 120
PR_DTW, PR_C16, PR_COLS, PR_VS, PR_YS = 120, 248, 256, 488, 552 - 16


def build_trunk(nc, t):
    ctx = ExitStack()
    with ctx:
        arena = ctx.enter_context(nc.sbuf_tensor("arena", [P, SB_W], F32))
        small = ctx.enter_context(nc.sbuf_tensor("small", [P, 192], F32))
        psum = ctx.enter_context(nc.psum_tensor("psum", [P, 8, 512], F32))
        banks = [psum[:, i, :] for i in range(8)]

        def sem(name):
            return ctx.enter_context(nc.semaphore(name))

        def view(off, *dims, p0=0, p1=P):
            n = int(np.prod(dims))
            ap = arena[p0:p1, off:off + n]
            names = "abcd"[:len(dims)]
            if len(dims) > 1:
                ap = ap.rearrange(f"p ({' '.join(names)}) -> p {' '.join(names)}",
                                  **{k: d for k, d in zip(names, dims)})
            return ap

        ident = view(O_CONST + C_IDENT, P)
        ones = view(O_CONST + C_ONES, P)
        s5mask = view(O_CONST + C_MASK, P)
        cosq, sinq = view(O_CONST + C_COSQ, TOK), view(O_CONST + C_SINQ, TOK)
        cosk, sink = view(O_CONST + C_COSK, TOK), view(O_CONST + C_SINK, TOK)
        decay = view(O_CONST + C_DECAY, RET_H, SCORE_W)
        causal = view(O_CONST + C_CAUSAL, SCORE_W)
        expand = view(O_CONST + C_EXPAND, NB, P)
        wend = view(O_CONST + C_WEND, 2, RET_H)
        eps = view(O_CONST + C_EPS, 1)
        prm = view(O_PRM, PR_ROWS)
        dtw = view(O_PRM + PR_DTW, 8, 16)
        c16 = view(O_PRM + PR_C16, 8)
        cols = view(O_PRM + PR_COLS, 232)
        h = view(O_H, NB, TOK)
        xn = view(O_XN, NB, TOK)
        ring = view(O_RING, RING, 8, 256)
        u = view(O_U, NB, TOK)
        zr = view(O_Z, NB, TOK)
        g = view(O_G, NB, TOK)
        qk = view(O_QK, NB, TOK)
        v = view(O_V, NB, TOK)
        xc = view(O_XC, CB, XC_W)
        sv = view(O_SV, SLOTS, 64)
        u4 = view(O_U4, PAIRS, U4_W)
        gw = view(O_GW, 2, PAIRS, P)
        bb = view(O_BB, 2, PAIRS, 16)
        ct = view(O_CT, 2, PAIRS, 16)

        w_landed = [sem(f"w_landed{i}") for i in range(RING)]
        chunk_used = sem("chunk_used")
        proj_filled = sem("proj_filled")
        proj_drained = sem("proj_drained")
        bank_filled = [sem(f"bank_filled{i}") for i in range(4)]
        bank_drained = [sem(f"bank_drained{i}") for i in range(4)]
        dve_step, act_step, pool_step = sem("dve_step"), sem("act_step"), sem("pool_step")
        names = """const_in vec_in s5_in b_in c_in h0_in convst_in head_in dtw_in squares mean_ready rstd_ready xn_ready
            prm_ready s5a_cols trig_arg trig_ready powers_ready pool_zero u4_ready bd_ready bd_used conv_pad conv_y conv_t conv_silu
            tail_ready tails_out convcopy_out rope_done g_silu scan_go scan_done newst_ready s5st_out
            e_ready gelu_arg gelu_tanh gelu_done z_silu ret_kw ret_m st_evac st_out dec_in0 dec_in1 dec_out0 dec_out1
            ret_yc retsq ret_norm gates_m dt_abs dt_exp alog_exp acum_ready wend_exp dt_rows
            ssd_vtok seg_ready exp_ready exp_masked ssd_yz ssdsq ssd_norm merged hid_ready resid x_in y_rows y_out ysmp
            scan_step""".split()
        s = {n: sem(n) for n in names}
        all_sems = w_landed + [chunk_used, proj_filled, proj_drained] + bank_filled + bank_drained \
            + [dve_step, act_step, pool_step] + list(s.values())
        numbers = sorted(x.num for x in all_sems)
        sem_range = range(numbers[0], numbers[-1] + 1)
        assert len(numbers) == len(sem_range)

        def bank(name):
            return banks[4 + FILL[name][0]]

        def filled(eng, name):
            eng.wait_ge(bank_filled[FILL[name][0]], FILL[name][1])

        def drained(eng, name):
            eng.wait_ge(bank_drained[FILL[name][0]], FILL[name][1])

        def is_drained(ins, name):
            ins.then_inc(bank_drained[FILL[name][0]], 1)

        class Chain:

            def __init__(self, eng, semaphore):
                self.eng, self.sem, self.n = eng, semaphore, 0

            def step(self, ins):
                ins.then_inc(self.sem, 1)
                self.n += 1

            def wait(self):
                self.eng.wait_ge(self.sem, self.n)

            def link(self, ins):
                self.step(ins)
                self.wait()

        def layer_of(ap, lyr):
            dims = " ".join("abcde"[:len(ap.shape) - 1])
            first, rest = dims.split(" ")[0], " ".join(dims.split(" ")[1:])
            return ap[bass.ds(lyr, 1)].rearrange(f"o {dims} -> (o {first}) {rest}".strip())

        xld = view(O_R, 2, D_MODEL)
        xsld = view(O_R + 2 * D_MODEL, D_MODEL, p1=SAMPLES)
        with nc.Block() as block:
            @block.sync
            def _(sp):
                sp.dma_start(arena[:, O_CONST:O_CONST + CONST_W], t["consts"]).then_inc(s["const_in"], 16)
                sp.dma_start(xld, t["x_prompt"].rearrange("o (tb p) d -> p (o tb) d", p=P)).then_inc(s["x_in"], 16)
                sp.dma_start(xsld, t["x_sample"].rearrange("b o d -> (b o) d")).then_inc(s["x_in"], 16)

            @block.tensor
            def _(pe):
                pe.wait_ge(s["const_in"], 16)
                pe.wait_ge(s["x_in"], 32)
                for k in range(NB):
                    if k >= 4:
                        pe.wait_ge(proj_drained, k - 3)
                    for tb in range(2):
                        pe.transpose(banks[k % 4][:, tb * P:(tb + 1) * P], xld[:, tb, k * P:(k + 1) * P], ident)
                    pe.transpose(banks[k % 4][:, SEQ:TOK], xsld[:, k * P:(k + 1) * P],
                                 ident[0:SAMPLES, 0:SAMPLES]).then_inc(proj_filled, 1)

            @block.scalar
            def _(act):
                for k in range(NB):
                    act.wait_ge(proj_filled, k + 1)
                    nc.scalar.activation(h[:, k, :], banks[k % 4][:, 0:TOK], ACT.Copy).then_inc(proj_drained, 1)

        nc.all_engine_barrier(sems_to_clear=sem_range)

        pwr = view(O_SM, 5, 2, PAIRS)
        a4r, a4i = view(O_SM + 320, 64), view(O_SM + 384, 64)
        qfac = view(O_SM + 448, 2, PAIRS)
        trig = view(O_SM + 512, 8, 2, PAIRS)
        s5v = view(O_SM + 1024, 4, PAIRS)
        vrow = view(O_SM + 1152, P)
        prow = view(O_SM + 1280, 4, P, p1=PAIRS)
        dtrow = view(O_SM + 1792, 2, p1=PAIRS)
        a1r, a1i = small[:, 64:128], small[:, 128:192]
        et = view(O_SM + 1024, 4, 16, 16)
        news = view(O_SM + 1280, 4, P)
        newp = view(O_SM + 1792, P, p1=64)
        braw = view(O_SV + 1024, 2, PAIRS, 16)
        btmp = view(O_SV + 2048, 4, PAIRS, 16)
        bd = view(O_QK, 2, 16, P)
        convst = view(O_GW, CONV_DIM, p1=SAMPLES * (TAPS - 1))
        craw = view(O_GW + 2048, 2, 8, P)
        h0raw = view(O_GW + 4096, 4, P)
        eb = view(O_GW, 2, 16, 5, 32)
        toep = view(O_GW + 5120, 16, P)
        bblk = view(O_GW + 7168, 2, 16, 32)
        rms, rstd = view(O_G, TOK), view(O_G + TOK, TOK)
        convy = view(O_G, 3, 2, CONV_OUT)
        tailc = view(O_G + 1900, CB, 11)
        tailr = view(O_Z, CONV_DIM, p1=11)
        dts = view(O_DTS, 8, TOK, p1=HEADS)
        DT_X, DT_E, DT_S, DT_DELTA, DT_LA, DT_AC, DT_DW, DT_RHS = range(8)
        vtok, vw = view(O_VTOK, 2, D_MODEL), view(O_VW, 2, D_MODEL)
        btok = view(O_BTOK, 2, 512)
        sc = view(O_SC, 2, SCORE_W)
        seg, ex = view(O_SEG, 2, SCORE_W), view(O_EXP, 2, SCORE_W)
        dec = view(O_DEC, 2, NB, P)
        outer = view(O_TMP, NB, P)
        stout = view(O_STOUT, NB, P)
        zg = view(O_ZG, NB, TOK)
        m_ = view(O_M, NB, TOK)
        sq8 = view(O_VTOK, NB, TOK)
        head_rms = view(O_SEG, 4, TOK)
        hid = view(O_HID, 32, TOK)
        vs, ys = view(O_PRM + 488, NB, SAMPLES), small[:, 0:64].rearrange("p (a b) -> p a b", a=NB)
        gam = retention_gammas()

        def at(name):
            return BLOCKS[name]

        def layer(nc, block, t, lyr):
            @block.sync
            def _(sp):
                def cols_of(name, col0):
                    w = layer_of(t[name], lyr).rearrange("(k p) n -> p k n", p=P)
                    return lambda c: w[:, :, bass.ds(col0 + 256 * c, 256)]

                def load(unit_no, source, before):
                    for c in range(RING):
                        before(c)
                        sp.dma_start(ring[:, c, :, :], source(c)).then_inc(w_landed[c], 16)

                def after_unit(first_block):
                    return lambda c: sp.wait_ge(proj_filled, first_block + 2 * c + 2)

                sp.wait_ge(s["vec_in"], 112)
                sp.wait_ge(s["s5_in"], 48)
                load(0, cols_of("w_in", COL_U), lambda c: None)
                with sp.Fori(0, 2) as j:
                    load(1 + j, cols_of("w_in", COL_X + j * 1024), after_unit(at("u") + 8 * j))
                for name, arr, col in (("qk", "w_in", COL_QK), ("v", "w_in", COL_V), ("g", "w_in", COL_G),
                                       ("z", "w_in", COL_Z), ("s5a", "w_s5_out", 0), ("s5b", "w_s5_out", 1024),
                                       ("gate0", "w_in", COL_GATE), ("reto", "w_ret_out", 0),
                                       ("gate2", "w_in", COL_GATE + 2048), ("gate1", "w_in", COL_GATE + 1024),
                                       ("ssdo", "w_ssd_out", 0), ("wo", "w_out", 0)):
                    n = UNITS.index(name)
                    load(n, cols_of(arr, col), after_unit(at(UNITS[n - 1])))
                with sp.Fori(0, 4) as j:
                    load(15 + j, cols_of("w_mlp_up", j * 1024), after_unit(at("wo") + 8 * j))
                down = layer_of(t["w_mlp_down"], lyr).rearrange("(r k p) n -> p r k n", r=4, p=P)
                load(19, lambda c: down[:, c, :, 0:256], after_unit(at("up3")))
                with sp.Fori(1, 4) as j:
                    def before(c):
                        if c < 3:
                            sp.wait_ge(chunk_used, 3 * j + (c - 2))
                        else:
                            sp.wait_ge(proj_filled, at("dn0") + 2 * j)
                    load(19 + j, lambda c: down[:, c, :, bass.ds(j * 256, 256)], before)

            @block.tensor
            def _(pe):
                def open_fill(name):
                    b, f = FILL[name]
                    if f > 1:
                        pe.wait_ge(bank_drained[b], f - 1)
                    return banks[4 + b]

                def close_fill(ins, name):
                    ins.then_inc(bank_filled[FILL[name][0]], 1)

                def unit(n, first, rhs, fresh=False, ready=None, before=None):
                    for b in range(8):
                        c = b // 2
                        if before:
                            before(b)
                        if b % 2 == 0:
                            pe.wait_ge(w_landed[c], n * 16 + 16)
                        if not (fresh and b < 4):
                            pe.wait_ge(proj_drained, first + (b - 3))
                        for k in range(8):
                            if ready and b == 0:
                                pe.wait_ge(s[ready[0]], ready[1] + k + 1)
                            mm = pe.matmul(banks[b % 4][:, 0:TOK], ring[:, c, k, (b % 2) * P:(b % 2) * P + P],
                                           rhs[:, k, :], start=(k == 0), stop=(k == 7))
                        mm.then_inc(proj_filled, 1)

                def named(name, rhs, **kw):
                    unit(UNITS.index(name), at(name), rhs, **kw)

                def sum_squares(name, src, blocks, ready, first):
                    o = open_fill(name)
                    for i, k in enumerate(blocks):
                        pe.wait_ge(s[ready], first + i + 1)
                        mm = pe.matmul(o[:, 0:TOK], ones, src[:, k, :], start=(i == 0), stop=(i == len(blocks) - 1))
                    close_fill(mm, name)

                pe.wait_ge(s["vec_in"], 112)
                o = open_fill("prm")
                close_fill(pe.transpose(o[:, 0:PR_ROWS], vrow[0:PR_ROWS, :], ident[0:PR_ROWS, 0:PR_ROWS]), "prm")
                sum_squares("n1", zr, range(NB), "squares", 0)
                o = open_fill("s5p")
                pe.wait_ge(s["s5a_cols"], 2)
                for i in range(4):
                    mm = pe.transpose(o[:, i * 32:(i + 1) * 32], prow[:, i, :], ident[0:32, 0:32])
                close_fill(mm, "s5p")
                pe.wait_ge(s["c_in"], 64)
                for ri, nm in enumerate(("cre", "cim")):
                    for i in range(2):
                        o = open_fill(f"{nm}{i}")
                        for j in range(4):
                            mm = pe.transpose(o[:, j * P:(j + 1) * P], craw[:, ri, 4 * i + j, :], ident)
                        close_fill(mm, f"{nm}{i}")
                pe.wait_ge(s["h0_in"], 64)
                o = open_fill("h0")
                for j in range(4):
                    mm = pe.transpose(o[:, j * P:(j + 1) * P], h0raw[:, j, :], ident)
                close_fill(mm, "h0")
                pe.wait_ge(s["convst_in"], 16)
                o = open_fill("cs")
                for j in range(CB):
                    mm = pe.transpose(o[:, j * 24:(j + 1) * 24], convst[:, j * P:(j + 1) * P], ident[0:24, 0:24])
                close_fill(mm, "cs")
                unit(0, 0, xn, fresh=True, ready=("xn_ready", 0))

                def s5_input_matrices(sl):
                    pe.wait_ge(s["bd_ready"], sl + 1)
                    for ri in range(2):
                        for i in range(4):
                            nm = f"G{8 * sl + 4 * ri + i}"
                            o = open_fill(nm)
                            for j in range(4):
                                mm = pe.transpose(o[:, j * P:(j + 1) * P], bd[:, ri, 4 * i + j, :], ident)
                            close_fill(mm, nm)

                def s5_chunk_inputs(i):
                    for ri in range(2):
                        nm = f"V{2 * i + ri}"
                        o = open_fill(nm)
                        drained(pe, f"G{8 * (i // 4) + 4 * ri + i % 4}")
                        for j in range(4):
                            m = 4 * i + j
                            mm = pe.matmul(o[:, j * 72:(j + 1) * 72], gw[:, ri, m, :], u4[:, m, 8:80],
                                           start=True, stop=True)
                        close_fill(mm, nm)

                def in_x0(b):
                    if b == 5:
                        s5_input_matrices(0)

                def in_x1(b):
                    if b == 2:
                        s5_input_matrices(1)
                        pe.wait_ge(s["u4_ready"], 1)
                    elif 3 <= b < 7:
                        s5_chunk_inputs(2 * b - 6)
                        s5_chunk_inputs(2 * b - 5)

                named("x0", xn, before=in_x0)
                named("x1", xn, before=in_x1)
                pe.wait_ge(proj_drained, 24)
                for i in range(4):
                    o = open_fill(f"tail{i}")
                    for j in range(4):
                        mm = pe.transpose(o[0:11, j * P:(j + 1) * P], tailc[:, 4 * i + j, :], ident)
                    close_fill(mm, f"tail{i}")
                named("qk", xn)
                named("v", xn)

                def s5_toeplitz(hf):
                    pe.wait_ge(s["e_ready"], hf + 1)
                    for i in range(4):
                        nm = f"K{hf}{i}"
                        o = open_fill(nm)
                        for j in range(4):
                            lm = 4 * i + j
                            pe.matmul(o[0:32, j * P:(j + 1) * P], bblk[:, 0, lm, :],
                                      eb[:, 0, lm, 0:4, :].rearrange("p a b -> p (a b)"), start=True, stop=False)
                            mm = pe.matmul(o[0:32, j * P:(j + 1) * P], bblk[:, 1, lm, :],
                                           eb[:, 1, lm, 0:4, :].rearrange("p a b -> p (a b)"), start=False, stop=True)
                        close_fill(mm, nm)

                def s5_outputs(hf):
                    if hf == 0:
                        pe.wait_ge(s["scan_done"], 1)
                    for i in range(4):
                        nm = f"Y{hf}{i}"
                        o = open_fill(nm)
                        drained(pe, f"K{hf}{i}")
                        for j in range(4):
                            lm, m = 4 * i + j, 16 * hf + 4 * i + j
                            out = o[:, j * 72:(j + 1) * 72]
                            pe.matmul(out, toep[:, lm, :], u4[:, m, 0:72], start=True, stop=False)
                            pe.matmul(out, eb[:, 0, lm, 1:5, :].rearrange("p a b -> p (a b)"), sv[:, 0:72, m],
                                      start=False, stop=False)
                            mm = pe.matmul(out, eb[:, 1, lm, 1:5, :].rearrange("p a b -> p (a b)"),
                                           sv[:, 0:72, 32 + m], start=False, stop=True)
                        close_fill(mm, nm)

                s5_toeplitz(0)
                named("g", xn, before=lambda b: s5_outputs(0) if b == 4 else None)
                s5_toeplitz(1)
                s5_outputs(1)
                pe.wait_ge(s["newst_ready"], 1)
                o = open_fill("nss")
                for j in range(4):
                    mm = pe.transpose(o[:, j * P:(j + 1) * P],
                                      sv[:, 73 + 2 * j:75 + 2 * j, :].rearrange("p a b -> p (a b)"), ident)
                close_fill(mm, "nss")
                o = open_fill("nsp")
                close_fill(pe.transpose(o[0:64, 0:P], sv[:, 72, :], ident), "nsp")
                pe.wait_ge(s["dtw_in"], 16)
                o = open_fill("dt")
                for k in range(8):
                    mm = pe.matmul(o[0:HEADS, 0:TOK], dtw[:, k, :], xn[:, k, :], start=(k == 0), stop=(k == 7))
                close_fill(mm, "dt")
                named("z", xn)

                for i in range(4):
                    o = open_fill(f"rv{i}")
                    for j in range(4):
                        tb = i // 2
                        mm = pe.transpose(o[:, j * P:(j + 1) * P], v[:, 4 * (i % 2) + j, tb * P:(tb + 1) * P], ident)
                    close_fill(mm, f"rv{i}")
                def scores(name, keys, queries):
                    o = open_fill(name)
                    pe.matmul(o[:, 0:SEQ], keys[:, 0:P], queries[:, 0:SEQ], start=True, stop=True)
                    close_fill(pe.matmul(o[:, SEQ:SCORE_W], keys[:, P:SEQ], queries[:, P:SEQ],
                                         start=True, stop=True), name)

                def ret_scores(hh):
                    scores(f"rs{hh}", qk[:, 4 + hh, :], qk[:, hh, :])

                def ret_outputs(hh):
                    o = open_fill(f"ry{hh}")
                    drained(pe, f"rs{hh}")
                    if hh == 0:
                        drained(pe, "rv3")
                    for ph in range(2):
                        vcol = (2 * hh + ph) * P
                        pe.matmul(o[:, ph * SEQ:(ph + 1) * SEQ], vtok[:, 0, vcol:vcol + P], sc[:, hh % 2, 0:SEQ],
                                  start=True, stop=False)
                        mm = pe.matmul(o[:, ph * SEQ + P:(ph + 1) * SEQ], vtok[:, 1, vcol:vcol + P],
                                       sc[:, hh % 2, SEQ:SCORE_W], start=False, stop=True)
                    close_fill(mm, f"ry{hh}")

                pe.wait_ge(s["rope_done"], 8)
                ret_scores(0)
                ret_scores(1)
                for tb in range(2):
                    o = open_fill(f"rk{tb}")
                    for hh in range(4):
                        mm = pe.transpose(o[:, hh * P:(hh + 1) * P], qk[:, 4 + hh, tb * P:(tb + 1) * P], ident)
                    close_fill(mm, f"rk{tb}")
                ret_outputs(0)
                for hh in range(1, 4):
                    if hh < 3:
                        ret_scores(hh + 1)
                    ret_outputs(hh)

                def end_states(name, half, left, right):
                    o = open_fill(name)
                    for j in range(4):
                        for tb in range(2):
                            mm = pe.matmul(o[:, j * P:(j + 1) * P], left(tb, 4 * half + j), right(tb, 4 * half + j),
                                           start=(tb == 0), stop=(tb == 1))
                    close_fill(mm, name)

                drained(pe, "rk1")
                for half in range(2):
                    end_states(f"rst{half}", half, lambda tb, b: vtok[:, tb, b * P:(b + 1) * P],
                               lambda tb, b: btok[:, tb, (b // 2) * P:(b // 2 + 1) * P])

                def spread(name, column):
                    o = open_fill(name)
                    for j in range(4):
                        mm = pe.transpose(o[:, j * P:(j + 1) * P], column(j).to_broadcast([P, P]), ident)
                    close_fill(mm, name)

                def spread_ret(b):
                    spread(f"rkb{b}", lambda j: qk[:, 4 + j, SEQ + b:SEQ + b + 1])
                    spread(f"rqb{b}", lambda j: qk[:, j, SEQ + b:SEQ + b + 1])

                def spread_ssd(b):
                    spread(f"skb{b}", lambda j: xc[:, 8 + j, SEQ + b:SEQ + b + 1])
                    spread(f"sqb{b}", lambda j: xc[:, 12 + j, SEQ + b:SEQ + b + 1])

                pe.wait_ge(s["gelu_done"], 8)
                named("s5a", u, before=spread_ret)

                def in_s5b(b):
                    if b == 6:
                        for hh in range(4):
                            sum_squares(f"rn{hh}", sq8, (2 * hh, 2 * hh + 1), "retsq", 2 * hh)
                named("s5b", u, before=in_s5b)
                named("gate0", xn)
                pe.wait_ge(s["dt_rows"], 4)
                o = open_fill("sc")
                for i, r in enumerate((DT_AC, DT_DELTA, DT_DW)):
                    for tb in range(2):
                        c = (2 * i + tb) * 16
                        pe.transpose(o[:, c:c + 16], dts[:, r, tb * P:(tb + 1) * P], ident[0:16, 0:16])
                for b in range(NB):
                    mm = pe.matmul(o[:, 96 + 17 * b:96 + 17 * b + 17], expand[0:HEADS, b, :], dts[:, DT_RHS, 0:17],
                                   start=True, stop=True)
                close_fill(mm, "sc")
                for i in range(4):
                    o = open_fill(f"sv{i}")
                    for j in range(4):
                        tb = i // 2
                        mm = pe.transpose(o[:, j * P:(j + 1) * P], xc[:, 4 * (i % 2) + j, tb * P:(tb + 1) * P], ident)
                    close_fill(mm, f"sv{i}")
                for tb in range(2):
                    o = open_fill(f"sb{tb}")
                    for gg in range(4):
                        mm = pe.transpose(o[:, gg * P:(gg + 1) * P], xc[:, 8 + gg, tb * P:(tb + 1) * P], ident)
                    close_fill(mm, f"sb{tb}")

                def head_decays(m):
                    o = open_fill(f"sa{m}")
                    for h2 in range(2):
                        for tb in range(2):
                            c = tb * HEADS + 2 * m + h2
                            mm = pe.transpose(o[:, h2 * SEQ + tb * P:h2 * SEQ + (tb + 1) * P],
                                              cols[:, c:c + 1].to_broadcast([P, P]), ident)
                    close_fill(mm, f"sa{m}")

                drained(pe, "sc")
                scores("ss0", xc[:, 8, :], xc[:, 12, :])
                head_decays(0)

                def head_outputs(m):
                    o = open_fill(f"sy{m}")
                    if m == 0:
                        drained(pe, "sv3")
                    for h2 in range(2):
                        pe.wait_ge(s["exp_masked"], 2 * m + h2 + 1)
                        hc = (2 * m + h2) * HEAD_DIM
                        pe.matmul(o[64 * h2:64 * h2 + 64, 0:SEQ], vtok[:, 0, hc:hc + HEAD_DIM], ex[:, h2, 0:SEQ],
                                  start=True, stop=False)
                        mm = pe.matmul(o[64 * h2:64 * h2 + 64, P:SEQ], vtok[:, 1, hc:hc + HEAD_DIM],
                                       ex[:, h2, SEQ:SCORE_W], start=False, stop=True)
                    close_fill(mm, f"sy{m}")

                def in_reto(m):
                    if m > 0:
                        head_outputs(m - 1)
                    if m % 2 and m < 7:
                        gg = (m + 1) // 2
                        scores(f"ss{gg}", xc[:, 8 + gg, :], xc[:, 12 + gg, :])
                    if m < 7:
                        head_decays(m + 1)

                named("reto", v, ready=("ret_norm", 0), before=in_reto)
                head_outputs(7)
                drained(pe, "sb1")
                for half in range(2):
                    end_states(f"sst{half}", half, lambda tb, b: vw[:, tb, b * P:(b + 1) * P],
                               lambda tb, b: btok[:, tb, (b // 2) * P:(b // 2 + 1) * P])
                named("gate2", xn, before=spread_ssd)

                def in_gate1(b):
                    if b == 6:
                        for gg in range(4):
                            sum_squares(f"sn{gg}", sq8, (2 * gg, 2 * gg + 1), "ssdsq", 2 * gg)
                named("gate1", xn, before=in_gate1)
                named("ssdo", xc[:, :, 0:TOK], ready=("ssd_norm", 0))
                named("wo", m_, ready=("merged", 0))
                sum_squares("n2", zr, range(NB), "squares", 8)
                with pe.Fori(0, 4) as j:
                    unit(15 + j, at("up0") + 8 * j, xn, ready=("xn_ready", 8))
                with pe.Fori(0, 2) as jj:
                    for half in range(2):
                        for c in range(4):
                            pe.wait_ge(w_landed[c], (2 * jj + half) * 16 + 320)
                            pe.wait_ge(s["hid_ready"], 8 * c + 8)
                            for b in range(2):
                                if c == 0:
                                    pe.wait_ge(proj_drained, at("dn0") + 4 * jj + (2 * half + b - 3))
                                for k in range(8):
                                    mm = pe.matmul(banks[2 * half + b][:, 0:TOK], ring[:, c, k, b * P:(b + 1) * P],
                                                   hid[:, 8 * c + k, :], start=(c == 0 and k == 0),
                                                   stop=(c == 3 and k == 7))
                                if c == 3:
                                    mm.then_inc(proj_filled, 1)
                            if c < 3:
                                mm.then_inc(chunk_used, 1)

            @block.scalar
            def _(act):
                chain = Chain(act, act_step)

                def copy(out, in_, scale=1.0):
                    return nc.scalar.activation(out, in_, ACT.Copy, scale=scale)

                def tanh(out, in_, scale=0.5):
                    return nc.scalar.activation(out, in_, ACT.Tanh, scale=scale)

                def root_mean(out, name, width):
                    filled(act, name)
                    is_drained(nc.scalar.activation(out, bank(name)[:, 0:TOK], ACT.Sqrt, scale=1.0 / width, bias=eps), name)

                def ret_tiles(name):
                    return layer_of(t[name], lyr).rearrange("b h (q p) n -> b p (h q) n", p=P)

                def ssd_tiles(name):
                    return layer_of(t[name], lyr).rearrange("b (k g) p n -> b (g p) k n", g=2)

                states = {"r": (ret_tiles("state_ret"), ret_tiles("new_ret_s")),
                          "s": (ssd_tiles("state_ssd"), ssd_tiles("new_ssd_s"))}

                def drain_unit(first, block_ops, blocks=8, before=None):
                    for b in range(blocks):
                        if before:
                            before(b)
                        act.wait_ge(proj_filled, first + (b + 1))
                        block_ops(b, banks[b % 4][:, 0:TOK]).then_inc(proj_drained, 1)

                def vec(name):
                    return layer_of(t[name], lyr)

                for name, row, n in (("norm1_w", PR_N1, 8), ("norm2_w", PR_N2, 8), ("s5_d", PR_D, 8),
                                     ("ssd_norm_w", PR_SN, 8), ("ssd_conv_b", PR_CB, 16)):
                    act.dma_start(vrow[row:row + n, :], vec(name).rearrange("(r p) -> r p", p=P)).then_inc(s["vec_in"], 16)
                act.dma_start(vrow[PR_CW:PR_FN, :], vec("ssd_conv_w").rearrange("t (r p) -> (t r) p", p=P))\
                   .then_inc(s["vec_in"], 16)
                act.dma_start(vrow[PR_FN:PR_ROWS, :], t["final_norm_w"].rearrange("(r p) -> r p", p=P))\
                   .then_inc(s["vec_in"], 16)
                act.dma_start(prow[:, 0, :], vec("s5_a_re").rearrange("(m g) p -> m (g p)", g=2)).then_inc(s["s5_in"], 16)
                act.dma_start(prow[:, 1, :], vec("s5_a_im").rearrange("(m g) p -> m (g p)", g=2)).then_inc(s["s5_in"], 16)
                act.dma_start(dtrow, vec("s5_log_dt").rearrange("(m g) -> m g", g=2)).then_inc(s["s5_in"], 16)
                for k in range(NB):
                    nc.scalar.activation(zr[:, k, :], h[:, k, :], ACT.Square).then_inc(s["squares"], 1)
                for ri, name in enumerate(("s5_b_re", "s5_b_im")):
                    act.dma_start(braw[:, ri, :, :], vec(name).rearrange("(m g) p c -> (g p) m c", g=2))\
                       .then_inc(s["b_in"], 16)
                for ri, name in enumerate(("s5_c_re", "s5_c_im")):
                    for dup in range(2):
                        act.dma_start(craw[:, ri, :, dup * 64:(dup + 1) * 64],
                                      vec(name).rearrange("(t g) c p -> (g c) t p", g=8)).then_inc(s["c_in"], 16)
                for ri, name in enumerate(("state_s5_re", "state_s5_im")):
                    for b2 in range(2):
                        p0 = 64 * b2 + 32 * ri
                        act.dma_start(h0raw[p0:p0 + 32, :, :],
                                      vec(name).rearrange("(bp b) (m g) p -> b m bp (g p)", b=2, g=2)[b2])\
                           .then_inc(s["h0_in"], 16)
                act.dma_start(convst, vec("state_conv").rearrange("b t c -> (b t) c")).then_inc(s["convst_in"], 16)
                for i, name in enumerate(("ssd_dt_bias", "ssd_a_log", "ssd_d")):
                    act.dma_start(c16[0:HEADS, i:i + 1], vec(name).rearrange("(h o) -> h o", o=1)).then_inc(s["head_in"], 16)
                act.dma_start(dtw, vec("w_in").rearrange("(k p) n -> p k n", p=P)[:, :, COL_DT:COL_DT + HEADS])\
                   .then_inc(s["dtw_in"], 16)
                act.dma_start(vec("new_conv_s")[:, 0:TAPS - 2, :], vec("state_conv")[:, 1:TAPS - 1, :])\
                   .then_inc(s["tails_out"], 16)

                filled(act, "prm")
                is_drained(copy(prm, bank("prm")[:, 0:PR_ROWS]), "prm")
                root_mean(rms, "n1", D_MODEL)
                act.wait_ge(s["s5_in"], 48)
                nc.scalar.activation(dtrow, dtrow, ACT.Exp).then_inc(s["trig_ready"], 1)
                filled(act, "s5p")
                is_drained(copy(s5v, bank("s5p")[:, 0:P].rearrange("p (a b) -> p a b", a=4)), "s5p")
                drained(act, "s5p")
                nc.scalar.activation(trig[:, 7, 0, :], s5v[:, 2, :], ACT.Exp).then_inc(s["trig_ready"], 1)
                for ri, nm in enumerate(("cre", "cim")):
                    for i in range(2):
                        filled(act, f"{nm}{i}")
                        src = bank(f"{nm}{i}").rearrange("p (m g c) -> p m g c", g=2, c=16)
                        copy(ct[0:64, ri, 16 * i:16 * i + 16, :], src[0:64, :, 0, :])
                        is_drained(copy(ct[64:128, ri, 16 * i:16 * i + 16, :], src[64:128, :, 1, :]), f"{nm}{i}")
                filled(act, "h0")
                is_drained(copy(sv[:, 0:SAMPLES, :].rearrange("p a b -> p (a b)"), bank("h0")[:, :]), "h0")
                filled(act, "cs")
                is_drained(copy(xc[:, :, TAPS - 1 + SEQ:].rearrange("p k (b t) -> p k b t", t=TAPS)[:, :, :, 0:TAPS - 1],
                                bank("cs")[:, 0:24 * CB].rearrange("p (k b t) -> p k b t", k=CB, t=TAPS - 1)), "cs")
                act.wait_ge(s["trig_arg"], 1)
                nc.scalar.activation(trig[:, 5, :, :], trig[:, 6, :, :], ACT.Sin).then_inc(s["trig_ready"], 1)
                drain_unit(0, lambda b, ps: copy(u[:, b, :], ps))
                new0 = TAPS - 1 + SEQ + TAPS - 1

                def xbc(k, ps):
                    copy(xc[:, k, TAPS - 1:TAPS - 1 + SEQ], ps[:, 0:SEQ])
                    copy(xc[:, k, new0:XC_W:TAPS], ps[:, SEQ:TOK])
                    return copy(tailc[:, k, :], ps[:, SEQ - (TAPS - 1):TOK])

                def conv_tanh(k):
                    act.wait_ge(s["conv_y"], k + 1)
                    tanh(convy[:, k % 3, 1, :], convy[:, k % 3, 0, :], 1.0).then_inc(s["conv_t"], 1)

                def in_x1(b):
                    if 3 <= b < 7:
                        for i in (2 * b - 6, 2 * b - 5):
                            for ri in range(2):
                                filled(act, f"V{2 * i + ri}")
                                c = 32 * ri + 4 * i
                                is_drained(copy(sv[:, 9:SLOTS, c:c + 4],
                                                bank(f"V{2 * i + ri}")[:, 0:288].rearrange("p (j k) -> p k j", j=4)),
                                           f"V{2 * i + ri}")
                    if b >= 5:
                        conv_tanh(b - 5)

                drain_unit(at("x0"), xbc)
                drain_unit(at("x1"), lambda b, ps: xbc(NB + b, ps), before=in_x1)
                for i in range(4):
                    filled(act, f"tail{i}")
                    is_drained(copy(tailr[:, i * 512:(i + 1) * 512], bank(f"tail{i}")[0:11, :]), f"tail{i}")
                for i in range(4):
                    drained(act, f"tail{i}")
                act.dma_start(vec("new_conv_p").rearrange("b t c -> (b t) c"), tailr[0:3, :]).then_inc(s["tails_out"], 16)
                act.dma_start(vec("new_conv_s")[:, TAPS - 2, :], tailr[3:11, :]).then_inc(s["tails_out"], 16)
                act.wait_ge(s["tails_out"], 48)

                def qk_block(b, ps):
                    copy(qk[:, b, :], ps)
                    copy(zr[0:64, b, :], ps[64:128, :])
                    return copy(zr[64:128, b, :], ps[0:64, :])
                drain_unit(at("qk"), qk_block, before=lambda b: conv_tanh(3 + b))
                drain_unit(at("v"), lambda b, ps: copy(v[:, b, :], ps), before=lambda b: conv_tanh(11 + b) if b < 5 else None)
                act.wait_ge(s["conv_silu"], 16)

                def g_block(b, ps):
                    act.wait_ge(s["rope_done"], b + 1)
                    copy(g[:, b, :], ps, 0.5)
                    return tanh(zr[:, b, :], ps)

                def keep_toeplitz(hf):
                    for i in range(4):
                        filled(act, f"K{hf}{i}")
                        src = bank(f"K{hf}{i}")[0:32, :].rearrange("p (j c) -> p j c", j=4)
                        for r in range(LIFT):
                            ins = copy(toep[32 * r:32 * r + 32, 4 * i:4 * i + 4, 32 * r:P], src[:, :, 0:P - 32 * r])
                        is_drained(ins, f"K{hf}{i}")

                def keep_outputs(hf):
                    act.wait_ge(s["g_silu"], 4 * hf + 4)
                    for i in range(4):
                        filled(act, f"Y{hf}{i}")
                    dst = zr[:, 4 * hf:4 * hf + 4, :]
                    for mm in range(4):
                        rows = slice(32 * mm, 32 * mm + 32)
                        copy(dst[rows, :, SEQ:TOK], psum[0:32, 4:8, 72 * mm:72 * mm + 8])
                        for r in range(LIFT):
                            chain.step(copy(dst[rows, :, r:SEQ:LIFT], psum[32 * r:32 * r + 32, 4:8, 72 * mm + 8:72 * mm + 72]))
                    for i in range(4):
                        is_drained(act.drain(), f"Y{hf}{i}")

                keep_toeplitz(0)
                drain_unit(at("g"), g_block, before=lambda b: keep_outputs(0) if b == 4 else None)
                keep_toeplitz(1)
                keep_outputs(1)
                filled(act, "nss")
                is_drained(copy(news.rearrange("p a b -> p (a b)"), bank("nss")[:, :]), "nss")
                filled(act, "nsp")
                is_drained(copy(newp, bank("nsp")[0:64, 0:P]), "nsp")
                drained(act, "nss")
                drained(act, "nsp")
                for ri, nm in enumerate(("re", "im")):
                    for b2 in range(2):
                        p0 = 64 * b2 + 32 * ri
                        act.dma_start(vec(f"new_s5_{nm}_s").rearrange("(bp b) (m g) p -> b m bp (g p)", b=2, g=2)[b2],
                                      news[p0:p0 + 32, :, :]).then_inc(s["s5st_out"], 16)
                    act.dma_start(vec(f"new_s5_{nm}_p").rearrange("b (m g) p -> (b m) (g p)", g=2),
                                  newp[32 * ri:32 * ri + 32, :]).then_inc(s["s5st_out"], 16)
                act.wait_ge(s["head_in"], 48)
                nc.scalar.activation(c16[0:HEADS, 3:4], c16[0:HEADS, 1:2], ACT.Exp).then_inc(s["alog_exp"], 1)
                act.wait_ge(s["dt_abs"], 1)
                nc.scalar.activation(dts[:, DT_E, :], dts[:, DT_E, :], ACT.Exp, scale=-1.0).then_inc(s["dt_exp"], 1)
                act.wait_ge(s["acum_ready"], 1)
                nc.scalar.activation(dts[:, DT_DW, 0:SEQ], dts[:, DT_AC, 0:SEQ], ACT.Exp, scale=-1.0,
                                     bias=dts[:, DT_AC, SEQ - 1:SEQ]).then_inc(s["wend_exp"], 1)
                nc.scalar.activation(dts[:, DT_RHS, 8:16], dts[:, DT_LA, SEQ:TOK], ACT.Exp).then_inc(s["dt_rows"], 1)

                def z_block(b, ps):
                    copy(zg[:, b, :], ps, 0.5)
                    return tanh(m_[:, b, :], ps)
                drain_unit(at("z"), z_block)
                for k in range(NB):
                    act.wait_ge(s["gelu_arg"], k + 1)
                    tanh(u[:, k, :], u[:, k, :], math.sqrt(2.0 / math.pi)).then_inc(s["gelu_tanh"], 1)
                for i in range(4):
                    filled(act, f"rv{i}")
                    is_drained(copy(vtok[:, i // 2, (i % 2) * 512:(i % 2) * 512 + 512], bank(f"rv{i}")[:, :]), f"rv{i}")
                for hh in range(4):
                    filled(act, f"ry{hh}")
                    is_drained(copy(v[:, 2 * hh:2 * hh + 2, 0:SEQ],
                                    bank(f"ry{hh}")[:, :].rearrange("p (a b) -> p a b", a=2)), f"ry{hh}")

                def store_states(pfx, dst):
                    for half in range(2):
                        filled(act, f"{pfx}{half}")
                        is_drained(copy(stout[:, 4 * half:4 * half + 4, :],
                                        bank(f"{pfx}{half}")[:, :].rearrange("p (a b) -> p a b", a=4)), f"{pfx}{half}")
                    for half in range(2):
                        drained(act, f"{pfx}{half}")
                    act.dma_start(dst, stout).then_inc(s["st_out"], 16)

                store_states("rst", vec("new_ret_p").rearrange("b h (q p) n -> p (b h q) n", p=P))
                def load_state(pfx, b):
                    before = 4 * (pfx == "s") + b // 2
                    if before:
                        act.wait_ge(s[f"dec_out{b % 2}"], 16 * before)
                    act.dma_start(dec[:, b % 2, :, :], states[pfx][0][b]).then_inc(s[f"dec_in{b % 2}"], 16)

                def store_state(pfx, b):
                    drained(act, f"{pfx}qb{b}")
                    act.dma_start(states[pfx][1][b], dec[:, b % 2, :, :]).then_inc(s[f"dec_out{b % 2}"], 16)

                def outer_products(pfx, b, vcol):
                    filled(act, f"{pfx}kb{b}")
                    if b > 0:
                        store_state(pfx, b - 1)
                    elif pfx == "s":
                        drained(act, "rqb7")
                    for blk in range(NB):
                        c = (blk // 2) * P
                        ins = copy(outer[:, blk, :], bank(f"{pfx}kb{b}")[:, c:c + P], vcol(blk, b))
                    is_drained(ins, f"{pfx}kb{b}")
                    if 1 <= b < SAMPLES - 1:
                        load_state(pfx, b + 1)

                def ret_v(blk, b):
                    return v[:, blk, SEQ + b:SEQ + b + 1]

                load_state("r", 0)
                load_state("r", 1)
                act.wait_ge(s["gelu_done"], 8)
                drain_unit(at("s5a"), lambda b, ps: copy(zr[:, b, :], ps, 0.25),
                           before=lambda b: outer_products("r", b, ret_v))
                store_state("r", 7)
                load_state("s", 0)
                load_state("s", 1)
                act.wait_ge(s["z_silu"], 8)

                def in_s5b(b):
                    if b == 0:
                        act.wait_ge(s["ret_yc"], 1)
                    if b < 4:
                        for k in (2 * b, 2 * b + 1):
                            nc.scalar.activation(sq8[:, k, :], v[:, k, :], ACT.Square).then_inc(s["retsq"], 1)
                    elif b == 7:
                        for hh in range(4):
                            root_mean(head_rms[:, hh, :], f"rn{hh}", RET_P)
                drain_unit(at("s5b"), lambda b, ps: tanh(m_[:, b, :], ps, 0.25), before=in_s5b)

                def gate0_block(b, ps):
                    act.wait_ge(s["gates_m"], b + 1)
                    return tanh(zr[:, b, :], ps)
                drain_unit(at("gate0"), gate0_block)
                filled(act, "sc")
                is_drained(copy(cols, bank("sc")[:, 0:232]), "sc")
                for tb in range(2):
                    filled(act, f"sb{tb}")
                    is_drained(copy(btok[:, tb, :], bank(f"sb{tb}")[:, :]), f"sb{tb}")

                def exponentials(m):
                    drained(act, f"sa{m}")
                    if m >= 1:
                        filled(act, f"sy{m - 1}")
                    for h2 in range(2):
                        nc.scalar.activation(ex[:, h2, :], seg[:, h2, :], ACT.Exp).then_inc(s["exp_ready"], 1)
                drain_unit(at("reto"), lambda b, ps: copy(u[:, b, :], ps), before=exponentials)
                act.wait_ge(s["st_out"], 16)
                store_states("sst", vec("new_ssd_p").rearrange("b (k g) p n -> (g p) (b k) n", g=2))

                def gate2_block(b, ps):
                    act.wait_ge(s["gates_m"], 9 + b)
                    return tanh(zr[:, b, :], ps)
                def ssd_v(blk, b):
                    return vs[:, blk, b:b + 1]

                drain_unit(at("gate2"), gate2_block, before=lambda b: outer_products("s", b, ssd_v))
                store_state("s", 7)

                def in_gate1(b):
                    if b < 4:
                        for k in (2 * b, 2 * b + 1):
                            act.wait_ge(s["ssd_yz"], k + 1)
                            nc.scalar.activation(sq8[:, k, :], xc[:, k, 0:TOK], ACT.Square).then_inc(s["ssdsq"], 1)
                    elif b == 7:
                        for gg in range(4):
                            root_mean(head_rms[:, gg, :], f"sn{gg}", 2 * P)
                drain_unit(at("gate1"), lambda b, ps: tanh(qk[:, b, :], ps), before=in_gate1)

                def ssdo_block(b, ps):
                    act.wait_ge(s["gates_m"], 17 + b)
                    return copy(u[:, b, :], ps)
                drain_unit(at("ssdo"), ssdo_block)
                drain_unit(at("wo"), lambda b, ps: copy(u[:, b, :], ps, 0.5))
                for k in range(NB):
                    act.wait_ge(s["resid"], k + 1)
                    nc.scalar.activation(zr[:, k, :], h[:, k, :], ACT.Square).then_inc(s["squares"], 1)
                root_mean(rms, "n2", D_MODEL)
                with act.Fori(0, 4) as j:
                    drain_unit(at("up0") + 8 * j,
                               lambda b, ps: nc.scalar.activation(hid[:, bass.ds(8 * j + b, 1), :], ps[:, None, :], ACT.Relu))
                with act.Fori(0, 2) as jj:
                    drain_unit(at("dn0") + 4 * jj,
                               lambda b, ps: copy(u[:, bass.ds(4 * jj + b, 1), :], ps[:, None, :]), blocks=4)
                act.wait_ge(s["st_out"], 32)
                act.wait_ge(s["s5st_out"], 96)
                for b in range(2):
                    act.wait_ge(s[f"dec_out{b}"], 16 * 8)

            @block.vector
            def _(dve):
                chain = Chain(dve, dve_step)
                V = nc.vector

                def inverse_root(name, src, dst):
                    drained(dve, name)
                    chain.link(V.reciprocal(dst, src))

                def cmul(re, im, ar, ai, br, bi, tmp):
                    chain.step(V.tensor_tensor(tmp[0], ar, br, ALU.mult))
                    chain.step(V.tensor_tensor(tmp[1], ai, bi, ALU.mult))
                    chain.step(V.tensor_tensor(tmp[2], ar, bi, ALU.mult))
                    chain.step(V.tensor_tensor(tmp[3], ai, br, ALU.mult))
                    chain.wait()
                    chain.step(V.tensor_tensor(re, tmp[0], tmp[1], ALU.subtract))
                    chain.step(V.tensor_tensor(im, tmp[2], tmp[3], ALU.add))
                    chain.wait()

                drained(dve, "prm")
                V.tensor_scalar(prm[:, PR_CB:PR_FN], prm[:, PR_CB:PR_FN], 0.5, None, ALU.mult).then_inc(s["prm_ready"], 1)
                dve.wait_ge(s["trig_ready"], 1)
                dve.wait_ge(s["s5_in"], 48)
                for i in range(2):
                    V.tensor_tensor(prow[:, 2 + i, :].rearrange("p (g n) -> p g n", g=2),
                                    prow[:, i, :].rearrange("p (g n) -> p g n", g=2),
                                    dtrow[:, :, None].to_broadcast([PAIRS, 2, 64]), ALU.mult).then_inc(s["s5a_cols"], 1)
                inverse_root("n1", rms, rstd)
                dve.wait_ge(s["prm_ready"], 1)
                for k in range(NB):
                    V.scalar_tensor_tensor(xn[:, k, :], h[:, k, :], prm[:, PR_N1 + k:PR_N1 + k + 1], rstd,
                                           ALU.mult, ALU.mult).then_inc(s["xn_ready"], 1)
                drained(dve, "s5p")
                ang = s5v[:, 3, :]
                big = 12582912.0
                for i, turn in enumerate((0.0, 0.25)):
                    chain.step(V.tensor_scalar(trig[:, 0, i, :], ang, 1.0 / TWO_PI, turn, ALU.mult, ALU.add))
                chain.wait()
                chain.link(V.tensor_scalar(trig[:, 1, :, :], trig[:, 0, :, :], big, None, ALU.add))
                chain.link(V.tensor_scalar(trig[:, 0, :, :], trig[:, 1, :, :], big, None, ALU.subtract))
                c1 = 6.28125
                c2 = float(np.float32(np.floor((TWO_PI - c1) * 2.0 ** 21) / 2.0 ** 21))
                c3 = TWO_PI - c1 - c2
                for i in range(2):
                    chain.step(V.scalar_tensor_tensor(trig[:, 2, i, :], trig[:, 0, i, :], -c1, ang, ALU.mult, ALU.add))
                chain.wait()
                chain.link(V.scalar_tensor_tensor(trig[:, 3, :, :], trig[:, 0, :, :], -c2, trig[:, 2, :, :],
                                                  ALU.mult, ALU.add))
                chain.link(V.scalar_tensor_tensor(trig[:, 2, :, :], trig[:, 0, :, :], -c3, trig[:, 3, :, :],
                                                  ALU.mult, ALU.add))
                chain.link(V.tensor_scalar(trig[:, 2, 1, :], trig[:, 2, 1, :], math.pi / 2, None, ALU.add))
                V.tensor_scalar(trig[:, 6, :, :], trig[:, 2, :, :], 3.1415925, -3.1415925, ALU.min, ALU.max)\
                    .then_inc(s["trig_arg"], 1)
                lre, lim = s5v[:, 0, :], s5v[:, 1, :]
                chain.step(V.tensor_tensor(trig[:, 3, 0, :], lre, lre, ALU.mult))
                chain.step(V.tensor_tensor(trig[:, 3, 1, :], lim, lim, ALU.mult))
                chain.wait()
                chain.link(V.tensor_tensor(trig[:, 4, 0, :], trig[:, 3, 0, :], trig[:, 3, 1, :], ALU.add))
                chain.step(V.reciprocal(trig[:, 4, 1, :], trig[:, 4, 0, :]))
                chain.step(V.memset(pwr[:, 0, 0, :], 1.0))
                chain.step(V.memset(pwr[:, 0, 1, :], 0.0))
                dve.wait_ge(s["trig_ready"], 3)
                chain.step(V.tensor_tensor(pwr[:, 1, 0, :], trig[:, 7, 0, :], trig[:, 5, 1, :], ALU.mult))
                chain.step(V.tensor_tensor(pwr[:, 1, 1, :], trig[:, 7, 0, :], trig[:, 5, 0, :], ALU.mult))
                chain.wait()
                small4 = [trig[:, 1, 0, :], trig[:, 1, 1, :], trig[:, 2, 0, :], trig[:, 2, 1, :]]
                for e_, a_, b_ in ((2, 1, 1), (3, 2, 1), (4, 2, 2)):
                    cmul(pwr[:, e_, 0, :], pwr[:, e_, 1, :], pwr[:, a_, 0, :], pwr[:, a_, 1, :],
                         pwr[:, b_, 0, :], pwr[:, b_, 1, :], small4)
                for dst_r, dst_i, e_ in ((a4r, a4i, 4), (a1r, a1i, 1)):
                    for c in range(2):
                        chain.step(V.tensor_copy(dst_r[:, 32 * c:32 * c + 32], pwr[:, e_, 0, :]))
                    chain.step(V.tensor_scalar(dst_i[:, 32:64], pwr[:, e_, 1, :], -1.0, None, ALU.mult))
                    chain.step(V.tensor_copy(dst_i[:, 0:32], pwr[:, e_, 1, :]))
                chain.wait()
                chain.link(V.tensor_scalar(trig[:, 0, 0, :], pwr[:, 1, 0, :], 1.0, None, ALU.subtract))
                chain.step(V.tensor_tensor(trig[:, 1, 0, :], trig[:, 0, 0, :], lre, ALU.mult))
                chain.step(V.tensor_tensor(trig[:, 1, 1, :], pwr[:, 1, 1, :], lim, ALU.mult))
                chain.step(V.tensor_tensor(trig[:, 2, 0, :], pwr[:, 1, 1, :], lre, ALU.mult))
                chain.step(V.tensor_tensor(trig[:, 2, 1, :], trig[:, 0, 0, :], lim, ALU.mult))
                chain.wait()
                chain.step(V.tensor_tensor(trig[:, 3, 0, :], trig[:, 1, 0, :], trig[:, 1, 1, :], ALU.add))
                chain.step(V.tensor_tensor(trig[:, 3, 1, :], trig[:, 2, 0, :], trig[:, 2, 1, :], ALU.subtract))
                chain.wait()
                for i in range(2):
                    chain.step(V.tensor_tensor(qfac[:, i, :], trig[:, 3, i, :], trig[:, 4, 1, :], ALU.mult))
                chain.wait()
                V.tensor_copy(trig[:, 5, 0, :], trig[:, 3, 0, :]).then_inc(s["powers_ready"], 1)

                def pairwise(ap, n):
                    return ap[:, :, None].to_broadcast([P, n, 16])

                dve.wait_ge(s["b_in"], 32)
                cmul(bb[:, 0, :, :], bb[:, 1, :, :], pairwise(qfac[:, 0, :], PAIRS), pairwise(qfac[:, 1, :], PAIRS),
                     braw[:, 0, :, :], braw[:, 1, :, :], [btmp[:, i, :, :] for i in range(4)])
                dve.wait_ge(s["pool_zero"], 3)
                dve.wait_ge(proj_drained, 8)
                for mm in range(4):
                    src = u[32 * mm:32 * mm + 32, :, :]
                    for r in range(LIFT):
                        V.tensor_copy(u4[32 * r:32 * r + 32, mm:PAIRS:4, 8:72], src[:, :, r:SEQ:LIFT])
                    V.tensor_copy(u4[0:32, mm:PAIRS:4, 0:8], src[:, :, SEQ:TOK])
                    ins = V.tensor_copy(u4[96:128, mm:PAIRS:4, 72:80], src[:, :, SEQ:TOK])
                ins.then_inc(s["u4_ready"], 1)
                for sl in range(2):
                    if sl == 1:
                        filled(dve, "G7")
                    for r in range(LIFT):
                        e_ = LIFT - 1 - r
                        tmp = [btmp[:, i, 16 * (r % 2):16 * (r % 2) + 16, :] for i in range(4)]
                        lo, hi = 16 * sl, 16 * sl + 16
                        ar, ai = pairwise(pwr[:, e_, 0, lo:hi], 16), pairwise(pwr[:, e_, 1, lo:hi], 16)
                        chain.step(V.tensor_tensor(tmp[0], ar, bb[:, 0, lo:hi, :], ALU.mult))
                        chain.step(V.tensor_tensor(tmp[1], ai, bb[:, 1, lo:hi, :], ALU.mult))
                        chain.step(V.tensor_tensor(tmp[2], ar, bb[:, 1, lo:hi, :], ALU.mult))
                        chain.step(V.tensor_tensor(tmp[3], ai, bb[:, 0, lo:hi, :], ALU.mult))
                        chain.wait()
                        tb_ = [x[:, :, None, :].to_broadcast([P, 16, 2, 16]) for x in tmp]
                        out = bd.rearrange("p i m (r g c) -> p i m r g c", r=LIFT, g=2)
                        chain.step(V.tensor_tensor(out[:, 0, :, r, :, :], tb_[0], tb_[1], ALU.subtract))
                        ins = V.tensor_tensor(out[:, 1, :, r, :, :], tb_[2], tb_[3], ALU.add)
                        if r == LIFT - 1:
                            ins.then_inc(s["bd_ready"], 1)
                        else:
                            chain.step(ins)
                    for ri in range(2):
                        for i in range(4):
                            nm = f"G{8 * sl + 4 * ri + i}"
                            filled(dve, nm)
                            is_drained(V.tensor_tensor(gw[:, ri, 16 * sl + 4 * i:16 * sl + 4 * i + 4, :],
                                                       bank(nm)[:, :].rearrange("p (j c) -> p j c", j=4),
                                                       s5mask[:, None, :].to_broadcast([P, 4, P]), ALU.mult), nm)
                drained(dve, "cs")

                def conv_silu(k):
                    dve.wait_ge(s["conv_t"], k + 1)
                    y, th = convy[:, k % 3, 0, :], convy[:, k % 3, 1, :]
                    V.scalar_tensor_tensor(xc[:, k, 0:SEQ], th[:, 0:SEQ], 1.0, y[:, 0:SEQ], ALU.add, ALU.mult)
                    first = TAPS - 1 + SEQ
                    V.scalar_tensor_tensor(xc[:, k, SEQ:TOK], th[:, first:CONV_OUT:TAPS], 1.0, y[:, first:CONV_OUT:TAPS],
                                           ALU.add, ALU.mult).then_inc(s["conv_silu"], 1)

                def rotary(k):
                    dve.wait_ge(proj_drained, at("qk") + k + 1)
                    cs_, sn_ = (cosq, sinq) if k < 4 else (cosk, sink)
                    chain.step(V.tensor_tensor(qk[:, k, :], qk[:, k, :], cs_, ALU.mult))
                    chain.step(V.tensor_tensor(zr[:, k, :], zr[:, k, :], sn_, ALU.mult))
                    chain.wait()
                    V.tensor_tensor(qk[:, k, :], qk[:, k, :], zr[:, k, :], ALU.add).then_inc(s["rope_done"], 1)

                for k in range(CB):
                    y = convy[:, k % 3, 0, :]
                    w0 = PR_CW + k
                    dve.wait_ge(proj_drained, at("x0") + k + 1)
                    chain.link(V.tensor_scalar(y, xc[:, k, 0:CONV_OUT], prm[:, w0:w0 + 1], prm[:, PR_CB + k:PR_CB + k + 1],
                                               ALU.mult, ALU.add))
                    for tap in range(1, TAPS):
                        wt = w0 + CB * tap
                        ins = V.scalar_tensor_tensor(y, xc[:, k, tap:tap + CONV_OUT], prm[:, wt:wt + 1], y,
                                                     ALU.mult, ALU.add)
                        if tap < TAPS - 1:
                            chain.link(ins)
                    ins.then_inc(s["conv_y"], 1)
                    if k >= 1:
                        conv_silu(k - 1)
                    if 5 <= k < 13:
                        rotary(k - 5)
                conv_silu(CB - 1)

                def output_matrices(hf):
                    lo, hi = 16 * hf, 16 * hf + 16
                    for tau in range(5):
                        pr, pi = pairwise(pwr[:, tau, 0, lo:hi], 16), pairwise(pwr[:, tau, 1, lo:hi], 16)
                        cr, ci = ct[:, 0, lo:hi, :], ct[:, 1, lo:hi, :]
                        chain.step(V.tensor_tensor(et[:, 0, :, :], cr, pr, ALU.mult))
                        chain.step(V.tensor_tensor(et[:, 1, :, :], ci, pi, ALU.mult))
                        chain.step(V.tensor_tensor(et[:, 2, :, :], cr, pi, ALU.mult))
                        chain.step(V.tensor_tensor(et[:, 3, :, :], ci, pr, ALU.mult))
                        chain.wait()
                        for g2 in range(2):
                            hv, cc = slice(64 * g2, 64 * g2 + 64), slice(16 * g2, 16 * g2 + 16)
                            chain.step(V.tensor_tensor(eb[hv, 0, :, tau, cc], et[hv, 0, :, :], et[hv, 1, :, :],
                                                       ALU.subtract))
                            chain.step(V.scalar_tensor_tensor(eb[hv, 1, :, tau, cc], et[hv, 2, :, :], -1.0,
                                                              et[hv, 3, :, :], ALU.mult, ALU.subtract))
                        chain.wait()
                    for g2 in range(2):
                        hv, cc = slice(64 * g2, 64 * g2 + 64), slice(16 * g2, 16 * g2 + 16)
                        for ri in range(2):
                            ins = V.tensor_copy(bblk[hv, ri, :, cc], bb[hv, ri, lo:hi, :])
                            if g2 + ri < 2:
                                chain.step(ins)
                    ins.then_inc(s["e_ready"], 1)

                filled(dve, "V12")
                filled(dve, "V13")
                filled(dve, "V14")
                filled(dve, "V15")
                for ri in range(4):
                    drained(dve, ("cre0", "cre1", "cim0", "cim1")[ri])
                chain.link(V.memset(view(O_GW, 8192), 0.0))
                output_matrices(0)

                def silu_g(k):
                    dve.wait_ge(proj_drained, at("g") + k + 1)
                    V.scalar_tensor_tensor(g[:, k, :], zr[:, k, :], 1.0, g[:, k, :], ALU.add, ALU.mult)\
                        .then_inc(s["g_silu"], 1)

                for k in range(4):
                    silu_g(k)
                filled(dve, "Y03")
                output_matrices(1)
                for k in range(4, NB):
                    silu_g(k)
                for k in range(NB):
                    drained(dve, f"Y{k // 4}{k % 4}")
                    chain.link(V.scalar_tensor_tensor(zr[:, k, :], u[:, k, :], prm[:, PR_D + k:PR_D + k + 1], zr[:, k, :],
                                                      ALU.mult, ALU.add))
                    chain.link(V.scalar_tensor_tensor(u[:, k, :], zr[:, k, :], 0.044715, zr[:, k, :], ALU.mult, ALU.mult))
                    V.scalar_tensor_tensor(u[:, k, :], u[:, k, :], 1.0, zr[:, k, :], ALU.add, ALU.mult)\
                        .then_inc(s["gelu_arg"], 1)
                filled(dve, "dt")
                dve.wait_ge(s["head_in"], 48)
                X, E_, S_, DL, LA, AC, DW, RH = (dts[:, i, :] for i in range(8))
                is_drained(V.tensor_scalar(X, bank("dt")[0:HEADS, 0:TOK], c16[0:HEADS, 0:1], None, ALU.add), "dt")
                drained(dve, "dt")
                chain.link(V.tensor_scalar(S_, X, -1.0, None, ALU.mult))
                V.tensor_tensor(E_, X, S_, ALU.max).then_inc(s["dt_abs"], 1)
                dve.wait_ge(s["dt_exp"], 1)
                chain.link(V.tensor_scalar(S_, E_, 2.0, None, ALU.add))
                chain.link(V.reciprocal(DL, S_))
                chain.link(V.tensor_tensor(S_, E_, DL, ALU.mult))
                chain.link(V.tensor_tensor(E_, S_, S_, ALU.mult))
                chain.link(V.tensor_scalar(DL, E_, 1.0 / 17.0, None, ALU.mult))
                for n in (15, 13, 11, 9, 7, 5, 3):
                    chain.link(V.scalar_tensor_tensor(DL, DL, 1.0 / n, E_, ALU.add, ALU.mult))
                chain.link(V.scalar_tensor_tensor(DL, DL, 1.0, S_, ALU.add, ALU.mult))
                chain.link(V.tensor_scalar(E_, X, 0.0, None, ALU.max))
                chain.link(V.scalar_tensor_tensor(DL, DL, 2.0, E_, ALU.mult, ALU.add))
                dve.wait_ge(s["alog_exp"], 1)
                chain.link(V.tensor_scalar(LA, DL, c16[0:HEADS, 3:4], -1.0, ALU.mult, ALU.mult))
                V.tensor_tensor_scan(AC[:, 0:SEQ], ones[0:HEADS, 0:1].to_broadcast([HEADS, SEQ]), LA[:, 0:SEQ], 0.0,
                                     ALU.mult, ALU.add).then_inc(s["acum_ready"], 1)
                V.tensor_copy(RH[:, 0:8], DL[:, SEQ:TOK]).then_inc(s["dt_rows"], 1)
                V.tensor_copy(RH[:, 16:17], c16[0:HEADS, 2:3]).then_inc(s["dt_rows"], 1)
                dve.wait_ge(s["wend_exp"], 1)
                V.tensor_tensor(DW[:, 0:SEQ], DW[:, 0:SEQ], DL[:, 0:SEQ], ALU.mult).then_inc(s["dt_rows"], 1)
                for k in range(NB):
                    dve.wait_ge(s["gelu_tanh"], k + 1)
                    V.scalar_tensor_tensor(u[:, k, :], u[:, k, :], 1.0, zr[:, k, :], ALU.add, ALU.mult)\
                        .then_inc(s["gelu_done"], 1)
                for k in range(NB):
                    dve.wait_ge(proj_drained, at("z") + k + 1)
                    V.scalar_tensor_tensor(zg[:, k, :], m_[:, k, :], 1.0, zg[:, k, :], ALU.add, ALU.mult)\
                        .then_inc(s["z_silu"], 1)
                def weigh_keys(tb):
                    filled(dve, f"rk{tb}")
                    is_drained(V.tensor_tensor(btok[:, tb, :].rearrange("p (a b) -> p a b", a=4),
                                               bank(f"rk{tb}")[:, :].rearrange("p (a b) -> p a b", a=4),
                                               wend[:, tb, :][:, :, None].to_broadcast([P, RET_H, P]), ALU.mult), f"rk{tb}")

                for hh in range(4):
                    filled(dve, f"rs{hh}")
                    if hh >= 2:
                        filled(dve, f"ry{hh - 2}")
                    is_drained(V.tensor_tensor(sc[:, hh % 2, :], bank(f"rs{hh}")[:, 0:SCORE_W], decay[:, hh, :], ALU.mult),
                               f"rs{hh}")
                    if hh == 1:
                        weigh_keys(0)
                        weigh_keys(1)

                def advance(pfx, nth, b, factor):
                    drained(dve, f"{pfx}kb{b}")
                    dve.wait_ge(s[f"dec_in{b % 2}"], 16 * (4 * nth + b // 2 + 1))
                    for blk in range(NB):
                        st = dec[:, b % 2, blk, :]
                        chain.step(V.scalar_tensor_tensor(st, st, factor(blk, b), outer[:, blk, :], ALU.mult, ALU.add))
                    chain.wait()
                    filled(dve, f"{pfx}qb{b}")
                    for blk in range(NB):
                        c = (blk // 2) * P
                        ins = V.tensor_tensor_reduce(outer[:, blk, :], dec[:, b % 2, blk, :],
                                                     bank(f"{pfx}qb{b}")[:, c:c + P], 1.0, 0.0, ALU.mult, ALU.add,
                                                     ys[:, blk, b:b + 1])
                    is_drained(ins, f"{pfx}qb{b}")

                for b in range(8):
                    advance("r", 0, b, lambda blk, b: gam[blk // 2])
                drained(dve, "rqb7")
                V.tensor_copy(v[:, :, SEQ:TOK], ys).then_inc(s["ret_yc"], 1)
                for k in range(NB):
                    dve.wait_ge(proj_drained, at("s5b") + k + 1)
                    V.scalar_tensor_tensor(m_[:, k, :], m_[:, k, :], 1.0, zr[:, k, :], ALU.add, ALU.mult)\
                        .then_inc(s["gates_m"], 1)
                for hh in range(4):
                    inverse_root(f"rn{hh}", head_rms[:, hh, :], head_rms[:, hh, :])
                    for k in (2 * hh, 2 * hh + 1):
                        chain.step(V.tensor_tensor(v[:, k, :], v[:, k, :], head_rms[:, hh, :], ALU.mult))
                    chain.wait()
                    for k in (2 * hh, 2 * hh + 1):
                        V.tensor_tensor(v[:, k, :], v[:, k, :], g[:, k, :], ALU.mult).then_inc(s["ret_norm"], 1)
                dve.wait_ge(s["gates_m"], 8)
                for k in range(NB):
                    dve.wait_ge(proj_drained, at("gate0") + k + 1)
                    V.scalar_tensor_tensor(m_[:, k, :], zr[:, k, :], 1.0, m_[:, k, :], ALU.add, ALU.mult)\
                        .then_inc(s["gates_m"], 1)
                drained(dve, "sc")
                per_block = cols[:, 96:232].rearrange("p (k n) -> p k n", k=NB)
                chain.step(V.tensor_tensor(vs, xc[:, 0:NB, SEQ:TOK], per_block[:, :, 0:8], ALU.mult))
                for i in range(4):
                    filled(dve, f"sv{i}")
                    tb, half = i // 2, i % 2
                    src = bank(f"sv{i}")[:, :].rearrange("p (a b) -> p a b", a=8)

                    def weight(row):
                        c = (2 * row + tb) * 16 + 8 * half
                        return cols[:, c:c + 8][:, :, None].to_broadcast([P, 8, HEAD_DIM])

                    def half_of(dst):
                        return dst[:, tb, half * 512:half * 512 + 512].rearrange("p (a b) -> p a b", a=8)
                    V.tensor_tensor(half_of(vtok), src, weight(1), ALU.mult)
                    is_drained(V.tensor_tensor(half_of(vw), src, weight(2), ALU.mult), f"sv{i}")

                def masked_scores(gg):
                    filled(dve, f"ss{gg}")
                    if gg >= 2:
                        dve.wait_ge(s["exp_masked"], 4 * (gg - 1))
                    elif gg == 0:
                        filled(dve, "ry2")
                        filled(dve, "ry3")
                    is_drained(V.tensor_tensor(sc[:, gg % 2, :], bank(f"ss{gg}")[:, 0:SCORE_W], causal, ALU.mult),
                               f"ss{gg}")

                def log_decays(m):
                    filled(dve, f"sa{m}")
                    if m >= 1:
                        dve.wait_ge(s["exp_ready"], 2 * m)
                    for h2 in range(2):
                        hd = 2 * m + h2
                        src = bank(f"sa{m}")[:, h2 * SEQ:(h2 + 1) * SEQ]
                        V.tensor_scalar(seg[:, h2, 0:SEQ], src, cols[:, hd:hd + 1], 0.0, ALU.subtract, ALU.min)
                        ins = V.tensor_scalar(seg[:, h2, SEQ:SCORE_W], src[:, P:SEQ], cols[:, 16 + hd:17 + hd], 0.0,
                                              ALU.subtract, ALU.min)
                    is_drained(ins, f"sa{m}")

                masked_scores(0)
                log_decays(0)
                for m in range(8):
                    if m % 2 and m < 7:
                        masked_scores((m + 1) // 2)
                    if m < 7:
                        log_decays(m + 1)
                    filled(dve, f"sy{m}")
                    is_drained(V.scalar_tensor_tensor(xc[:, m, 0:SEQ], xc[:, m, 0:SEQ], per_block[:, m, 16:17],
                                                      bank(f"sy{m}")[:, 0:SEQ], ALU.mult, ALU.add), f"sy{m}")
                for b in range(8):
                    advance("s", 1, b, lambda blk, b: per_block[:, blk, 8 + b:9 + b])
                chain.step(V.tensor_tensor(vs, xc[:, 0:NB, SEQ:TOK],
                                           per_block[:, :, 16:17].to_broadcast([P, NB, SAMPLES]), ALU.mult))
                drained(dve, "sqb7")
                chain.wait()
                for i in range(8):
                    drained(dve, f"sy{i}")
                chain.link(V.tensor_tensor(xc[:, 0:NB, SEQ:TOK], vs, ys, ALU.add))
                for k in range(NB):
                    V.tensor_tensor(xc[:, k, 0:TOK], xc[:, k, 0:TOK], zg[:, k, :], ALU.mult).then_inc(s["ssd_yz"], 1)
                for k in range(NB):
                    dve.wait_ge(proj_drained, at("gate2") + k + 1)
                    chain.link(V.scalar_tensor_tensor(u[:, k, :], zr[:, k, :], 1.0, u[:, k, :], ALU.add, ALU.mult))
                    V.tensor_tensor(m_[:, k, :], m_[:, k, :], u[:, k, :], ALU.add).then_inc(s["gates_m"], 1)
                for gg in range(4):
                    inverse_root(f"sn{gg}", head_rms[:, gg, :], head_rms[:, gg, :])
                    for k in (2 * gg, 2 * gg + 1):
                        V.scalar_tensor_tensor(xc[:, k, 0:TOK], xc[:, k, 0:TOK], prm[:, PR_SN + k:PR_SN + k + 1],
                                               head_rms[:, gg, :], ALU.mult, ALU.mult).then_inc(s["ssd_norm"], 1)
                for k in range(NB):
                    dve.wait_ge(proj_drained, at("ssdo") + k + 1)
                    chain.link(V.scalar_tensor_tensor(u[:, k, :], qk[:, k, :], 1.0, u[:, k, :], ALU.add, ALU.mult))
                    V.tensor_tensor(m_[:, k, :], m_[:, k, :], u[:, k, :], ALU.add).then_inc(s["merged"], 1)
                for k in range(NB):
                    dve.wait_ge(proj_drained, at("wo") + k + 1)
                    V.tensor_tensor(h[:, k, :], h[:, k, :], u[:, k, :], ALU.add).then_inc(s["resid"], 1)
                inverse_root("n2", rms, rstd)
                for k in range(NB):
                    V.scalar_tensor_tensor(xn[:, k, :], h[:, k, :], prm[:, PR_N2 + k:PR_N2 + k + 1], rstd,
                                           ALU.mult, ALU.mult).then_inc(s["xn_ready"], 1)
                with dve.Fori(0, 4) as j:
                    for b in range(8):
                        dve.wait_ge(proj_drained, at("up0") + 8 * j + (b + 1))
                        hb = hid[:, bass.ds(8 * j + b, 1), :]
                        V.tensor_tensor(hb, hb, hb, ALU.mult).then_inc(s["hid_ready"], 1)
                with dve.Fori(0, 2) as jj:
                    for b in range(4):
                        dve.wait_ge(proj_drained, at("dn0") + 4 * jj + (b + 1))
                        hb = h[:, bass.ds(4 * jj + b, 1), :]
                        V.tensor_tensor(hb, hb, u[:, bass.ds(4 * jj + b, 1), :], ALU.add)

            @block.gpsimd
            def _(pool):
                G = nc.gpsimd
                chain = Chain(pool, pool_step)
                G.memset(view(O_U4, PAIRS * U4_W), 0.0).then_inc(s["pool_zero"], 1)
                pool.wait_ge(s["pool_zero"], 1)
                G.memset(sv[:, 8, :], 0.0).then_inc(s["pool_zero"], 1)
                pool.wait_ge(s["pool_zero"], 2)
                G.memset(xc[:, :, 0:TAPS - 1], 0.0).then_inc(s["pool_zero"], 1)

                p1, p2 = trig[:, 2, :, :], trig[:, 3, :, :]
                pool.wait_ge(s["powers_ready"], 1)
                for i in range(12, 16):
                    drained(pool, f"V{i}")

                chain.link(G.memset(p1, 0.0))

                with pool.Fori(0, CHUNKS) as k:
                    now = sv[:, bass.ds(k + 8, 1), :].rearrange("p o (i m) -> p (o i) m", i=2)
                    new = sv[:, bass.ds(k + 9, 1), :].rearrange("p o (i m) -> p (o i) m", i=2)
                    wide = lambda ap: ap.rearrange("p (i m) -> p i m", i=2)
                    G.tensor_tensor(p1, wide(a4r), now, ALU.mult).then_inc(s["scan_step"], 1)
                    G.tensor_tensor(p2[:, ::-1, :], wide(a4i), now, ALU.mult).then_inc(s["scan_step"], 1)
                    pool.wait_ge(s["scan_step"], 1)
                    G.tensor_tensor(new, new, p1, ALU.add).then_inc(s["scan_step"], 1)
                    pool.wait_ge(s["scan_step"], 3)
                    G.tensor_tensor(new, new, p2, ALU.add).then_inc(s["scan_step"], 1)
                    pool.wait_ge(s["scan_step"], 4)
                    pool.sem_clear(s["scan_step"])
                G.memset(p1, 0.0).then_inc(s["scan_done"], 1)
                pool.wait_ge(s["scan_done"], 1)
                prod = trig.rearrange("p a b c -> p (a b c)").rearrange("p (s i m) -> p s i m", s=SAMPLES, i=2)
                h0 = sv[:, 0:SAMPLES, :].rearrange("p s (i m) -> p s i m", i=2)
                add = sv[:, 73:81, :].rearrange("p s (i m) -> p s i m", i=2)
                fac = lambda ap: ap.rearrange("p (i m) -> p i m", i=2)[:, None, :, :].to_broadcast([P, SAMPLES, 2, PAIRS])
                chain.link(G.tensor_tensor(prod, h0, fac(a1r), ALU.mult))
                chain.link(G.tensor_tensor(add, add, prod, ALU.add))
                chain.link(G.tensor_tensor(prod[:, :, ::-1, :], h0, fac(a1i), ALU.mult))
                G.tensor_tensor(add, add, prod, ALU.add).then_inc(s["newst_ready"], 1)

                for hd in range(HEADS):
                    pool.wait_ge(s["exp_ready"], hd + 1)
                    if hd % 4 == 0:
                        drained(pool, f"ss{hd // 4}")
                    G.tensor_tensor(ex[:, hd % 2, :], ex[:, hd % 2, :], sc[:, (hd // 4) % 2, :], ALU.mult)\
                        .then_inc(s["exp_masked"], 1)

        with nc.Fori(0, DEPTH) as lyr:
            with nc.Block() as block:
                layer(nc, block, t, lyr)
            nc.all_engine_barrier(sems_to_clear=sem_range)

        fms, frs = view(O_G, TOK), view(O_G + TOK, TOK)
        ytok = view(O_R, 2, D_MODEL)
        ysam = view(O_R + 2 * D_MODEL, D_MODEL, p1=SAMPLES)
        with nc.Block() as block:
            @block.scalar
            def _(act):
                for k in range(NB):
                    nc.scalar.activation(zr[:, k, :], h[:, k, :], ACT.Square).then_inc(s["squares"], 1)
                act.wait_ge(proj_filled, 1)
                nc.scalar.activation(fms, banks[0][:, 0:TOK], ACT.Sqrt, scale=1.0 / D_MODEL, bias=eps)\
                    .then_inc(s["mean_ready"], 1)
                for i in range(6):
                    act.wait_ge(proj_filled, 2 + i)
                    src = banks[(1 + i) % 4]
                    if i < 4:
                        ins = nc.scalar.activation(ytok[:, i // 2, (i % 2) * 512:(i % 2) * 512 + 512], src[:, :], ACT.Copy)
                    else:
                        ins = nc.scalar.activation(ysam[:, (i % 2) * 512:(i % 2) * 512 + 512], src[0:SAMPLES, :], ACT.Copy)
                    ins.then_inc(s["y_rows"], 1)

            @block.tensor
            def _(pe):
                for k in range(NB):
                    pe.wait_ge(s["squares"], k + 1)
                    mm = pe.matmul(banks[0][:, 0:TOK], ones, zr[:, k, :], start=(k == 0), stop=(k == NB - 1))
                mm.then_inc(proj_filled, 1)
                pe.wait_ge(s["xn_ready"], 8)
                for i in range(6):
                    if i == 3:
                        pe.wait_ge(s["mean_ready"], 1)
                    elif i > 3:
                        pe.wait_ge(s["y_rows"], i - 3)
                    dst = banks[(1 + i) % 4]
                    for j in range(4):
                        k = 4 * (i % 2) + j
                        if i < 4:
                            mm = pe.transpose(dst[:, j * P:(j + 1) * P], xn[:, k, (i // 2) * P:(i // 2 + 1) * P], ident)
                        else:
                            mm = pe.transpose(dst[0:SAMPLES, j * P:(j + 1) * P], xn[:, k, SEQ:TOK], ident)
                    mm.then_inc(proj_filled, 1)

            @block.vector
            def _(dve):
                dve.wait_ge(s["mean_ready"], 1)
                nc.vector.reciprocal(frs, fms).then_inc(s["rstd_ready"], 1)
                dve.wait_ge(s["rstd_ready"], 1)
                for k in range(NB):
                    nc.vector.scalar_tensor_tensor(xn[:, k, :], h[:, k, :], prm[:, PR_FN + k:PR_FN + k + 1], frs,
                                                   ALU.mult, ALU.mult).then_inc(s["xn_ready"], 1)

            @block.sync
            def _(sp):
                sp.wait_ge(s["y_rows"], 4)
                sp.dma_start(t["y_prompt"].rearrange("o (tb p) d -> p (o tb) d", p=P), ytok).then_inc(s["y_out"], 16)
                sp.wait_ge(s["y_rows"], 6)
                sp.dma_start(t["y_sample"].rearrange("b o d -> (b o) d"), ysam).then_inc(s["y_out"], 16)
                sp.wait_ge(s["y_out"], 32)


_INS = ["x_prompt", "x_sample", "state_s5_re", "state_s5_im", "state_ssd", "state_conv", "state_ret", "norm1_w", "w_in",
        "s5_a_re", "s5_a_im", "s5_log_dt", "s5_b_re", "s5_b_im", "s5_c_re", "s5_c_im", "s5_d", "w_s5_out",
        "ssd_conv_w", "ssd_conv_b", "ssd_dt_bias", "ssd_a_log", "ssd_d", "ssd_norm_w", "w_ssd_out", "w_ret_out",
        "w_out", "norm2_w", "w_mlp_up", "w_mlp_down", "final_norm_w"]
_OUTS = [("y_prompt", (1, SEQ, D_MODEL)), ("y_sample", (SAMPLES, 1, D_MODEL))]
for _sfx, _b in (("p", 1), ("s", SAMPLES)):
    _OUTS += [(f"new_s5_re_{_sfx}", (DEPTH, _b, S5_GROUPS, S5_STATE)), (f"new_s5_im_{_sfx}", (DEPTH, _b, S5_GROUPS, S5_STATE)),
              (f"new_ssd_{_sfx}", (DEPTH, _b, HEADS, HEAD_DIM, SSD_N)), (f"new_conv_{_sfx}", (DEPTH, _b, TAPS - 1, CONV_DIM)),
              (f"new_ret_{_sfx}", (DEPTH, _b, RET_H, RET_P, RET_N))]


def kernel(**inputs):
    import numpy as _np
    import concourse.bacc as _bacc
    from concourse.bass_utils import run_bass_kernel_spmd as _run

    nc = _bacc.Bacc("TRN2", target_bir_lowering=False, num_devices=1)
    arrays, t = {}, {}
    for name in _INS:
        a = _np.ascontiguousarray(inputs[name])
        arrays[f"in_{name}"] = a
        t[name] = nc.dram_tensor(f"in_{name}", a.shape, F32, kind="ExternalInput").ap()
    arrays["in_consts"] = constant_table()
    t["consts"] = nc.dram_tensor("in_consts", (P, CONST_W), F32, kind="ExternalInput").ap()
    for name, shape in _OUTS:
        t[name] = nc.dram_tensor(f"out_{name}", shape, F32, kind="ExternalOutput").ap()
    build_trunk(nc, t)
    r = _run(nc, [arrays], core_ids=[0])
    return tuple(r.results[0][f"out_{name}"] for name, _ in _OUTS)
```

```python
import math
from contextlib import ExitStack

import numpy as np

import concourse.bass as bass
from concourse import mybir

F32 = mybir.dt.float32
ALU = mybir.AluOpType
ACT = mybir.ActivationFunctionType

P = 128
D_MODEL = 1024
SEQ = 256
DEPTH = 2
SAMPLES = 8
PAST_LEN = 2048
TOK = SEQ + SAMPLES
NB = D_MODEL // P
D_FF = 4096
S5_GROUPS, S5_STATE, S5_CH = 64, 64, 16
PAIRS = S5_GROUPS // 2
LIFT = 4
CHUNKS = SEQ // LIFT
HEADS, HEAD_DIM, SSD_G, SSD_N = 16, 64, 4, 128
CONV_DIM = 2048
CB = CONV_DIM // P
TAPS = 4
XC_W = TAPS - 1 + SEQ + SAMPLES * TAPS
CONV_OUT = XC_W - (TAPS - 1)
RET_H, RET_N, RET_P = 4, 128, 256
ROPE_BASE = 10000.0
EPS = 1e-6
N_IN = 10256
COL_U, COL_Z, COL_X, COL_DT, COL_QK, COL_V, COL_G, COL_GATE = 0, 1024, 2048, 4096, 4112, 5136, 6160, 7184
SCORE_W = SEQ + P
RING = 4
TWO_PI = 2.0 * math.pi

C_IDENT, C_ONES, C_MASK = 0, 128, 256
C_EPS = 384
C_FIRST = 385
C_COSQ, C_SINQ, C_COSK, C_SINK = 385, 649, 913, 1177
C_DECAY = 1441
C_CAUSAL = C_DECAY + RET_H * SCORE_W
C_EXPAND = C_CAUSAL + SCORE_W
C_WEND = C_EXPAND + NB * P
CONST_W = C_WEND + 2 * RET_H


def retention_gammas():
    return [1.0 - 2.0 ** (-5.0 - h) for h in range(RET_H)]


def constant_table():
    t = np.zeros((P, CONST_W), np.float64)
    t[:, C_IDENT:C_IDENT + P] = np.eye(P)
    t[:, C_ONES:C_ONES + P] = 1.0
    row = np.arange(P)
    t[:, C_MASK:C_MASK + P] = ((row[:, None] // 16) % 2) == (row[None, :] // 64)
    half = RET_N // 2
    pos = np.concatenate([np.arange(SEQ), np.full(SAMPLES, PAST_LEN)]).astype(np.float64)
    inv = ROPE_BASE ** (-np.arange(half) / half)
    ang = inv[:, None] * pos[None, :]
    cos = np.concatenate([np.cos(ang), np.cos(ang)])
    sin = np.concatenate([-np.sin(ang), np.sin(ang)])
    t[:, C_COSQ:C_COSQ + TOK] = cos
    t[:, C_SINQ:C_SINQ + TOK] = sin
    t[:, C_COSK:C_COSK + TOK] = cos * RET_N ** -0.5
    t[:, C_SINK:C_SINK + TOK] = sin * RET_N ** -0.5
    dist = np.arange(SEQ)[None, :] - row[:, None]
    causal = (dist >= 0).astype(np.float64)
    for h, gamma in enumerate(retention_gammas()):
        decay = np.where(dist >= 0, gamma ** np.maximum(dist, 0), 0.0)
        t[:, C_DECAY + h * SCORE_W:C_DECAY + (h + 1) * SCORE_W] = np.concatenate([decay, decay[:, :P]], 1)
        for tb in range(2):
            t[:, C_WEND + tb * RET_H + h] = gamma ** (SEQ - 1 - tb * P - row)
    t[:, C_CAUSAL:C_CAUSAL + SCORE_W] = np.concatenate([causal, causal[:, :P]], 1)
    for m in range(NB):
        for h2 in range(2):
            t[2 * m + h2, C_EXPAND + m * P + h2 * 64:C_EXPAND + m * P + (h2 + 1) * 64] = 1.0
    t[:, C_EPS] = EPS
    return t.astype(np.float32)


O_CONST = 0
O_PRM = O_CONST + CONST_W
PRM_W = 600
O_H = O_PRM + PRM_W
O_XN = O_H + NB * TOK
O_RING = O_XN + NB * TOK
CHUNK_W = 8 * 256
O_U = O_RING + RING * CHUNK_W
O_Z = O_U + NB * TOK
O_G = O_Z + NB * TOK
O_QK = O_G + NB * TOK
O_V = O_QK + NB * TOK
O_XC = O_V + NB * TOK
O_R = O_XC + CB * XC_W
SLOTS = 1 + CHUNKS + 2 * SAMPLES
U4_W = CHUNKS + 2 * SAMPLES
O_SV = O_R
O_U4 = O_SV + SLOTS * 64
O_GW = O_U4 + PAIRS * U4_W
O_BB = O_GW + 8192
O_CT = O_BB + 1024
O_SM = O_CT + 1024
O_DTS = O_R
O_VTOK = O_DTS + 8 * TOK
O_VW = O_VTOK + NB * TOK
O_BTOK = O_VW + 2048
O_SC = O_BTOK + 1024
O_SEG = O_SC + 2 * SCORE_W
O_EXP = O_SEG + 2 * SCORE_W
O_DEC = O_EXP + 2 * SCORE_W
O_TMP = O_DEC + 3072
O_STOUT = O_TMP + 2048
O_ZG = O_STOUT + 1024
O_M = O_ZG + NB * TOK
SB_W = max(O_SM + 2048, O_M + NB * TOK)
O_HID = O_R

UNITS = ["u", "x0", "x1", "qk", "v", "g", "z", "s5a", "s5b", "gate0", "reto", "gate2", "gate1", "ssdo", "wo",
         "up0", "up1", "up2", "up3", "dn0", "dn1", "dn2", "dn3"]
BLOCKS = {}
_at = 0
for _n in UNITS:
    BLOCKS[_n] = _at
    _at += 2 if _n.startswith("dn") else 8

MIXER_FILLS = (
    ["n1", "prm", "s5p", "cre0", "cre1", "cim0", "cim1", "h0", "cs"]
    + [f"G{i}" for i in range(16)] + [f"V{i}" for i in range(16)] + [f"tail{i}" for i in range(4)]
    + [f for hf in range(2) for f in ([f"K{hf}{i}" for i in range(4)] + [f"Y{hf}{i}" for i in range(4)])]
    + ["nss", "nsp", "dt"]
    + [f"rv{i}" for i in range(4)] + ["rs0", "rs1", "rk0", "rk1", "ry0", "rs2", "ry1", "rs3", "ry2", "ry3", "rst0", "rst1"]
    + [f for b in range(8) for f in (f"rkb{b}", f"rqb{b}")] + [f"rn{h}" for h in range(4)]
    + ["sc"] + [f"sv{i}" for i in range(4)] + ["sb0", "sb1"]
    + ["ss0", "sa0"]
    + [f for m in range(8) for f in (([f"sy{m - 1}"] if m else [])
                                     + ([f"ss{(m + 1) // 2}"] if m % 2 and m < 7 else [])
                                     + ([f"sa{m + 1}"] if m < 7 else [])
                                     + ([f"skb{m // 2}", f"sqb{m // 2}"] if m % 2 else []))] + ["sy7"]
    + [f for b in range(4, 8) for f in (f"skb{b}", f"sqb{b}")] + [f"sn{h}" for h in range(4)]
    + ["n2", "sst0", "sst1"]
)
RET_SAMPLE_AT = {("s5a", 0): 0, ("s5a", 1): 1, ("s5a", 3): 2, ("s5a", 5): 3, ("s5a", 7): 4,
                 ("s5b", 0): 5, ("s5b", 2): 6, ("s5b", 3): 7}
TURN = MIXER_FILLS.index("Y00") % 4
FILL = {n: ((i - TURN) % 4, i // 4 + 1) for i, n in enumerate(MIXER_FILLS)}

PR_N1, PR_N2, PR_D, PR_SN, PR_CB, PR_CW, PR_FN, PR_ROWS = 0, 8, 16, 24, 32, 48, 112, 120
PR_DTW, PR_C16, PR_COLS, PR_VS = 120, 248, 256, 488


def build_trunk(nc, t):
    ctx = ExitStack()
    with ctx:
        arena = ctx.enter_context(nc.sbuf_tensor("arena", [P, SB_W], F32))
        small = ctx.enter_context(nc.sbuf_tensor("small", [P, 192], F32))
        psum = ctx.enter_context(nc.psum_tensor("psum", [P, 8, 512], F32))
        table_warm = ctx.enter_context(nc.sbuf_tensor("table_warm", [P, 1], F32))
        banks = [psum[:, i, :] for i in range(8)]

        def sem(name):
            return ctx.enter_context(nc.semaphore(name))

        def view(off, *dims, p0=0, p1=P):
            n = int(np.prod(dims))
            ap = arena[p0:p1, off:off + n]
            names = "abcd"[:len(dims)]
            if len(dims) > 1:
                ap = ap.rearrange(f"p ({' '.join(names)}) -> p {' '.join(names)}",
                                  **{k: d for k, d in zip(names, dims)})
            return ap

        ident = view(O_CONST + C_IDENT, P)
        ones = view(O_CONST + C_ONES, P)
        s5mask = view(O_CONST + C_MASK, P)
        cosq, sinq = view(O_CONST + C_COSQ, TOK), view(O_CONST + C_SINQ, TOK)
        cosk, sink = view(O_CONST + C_COSK, TOK), view(O_CONST + C_SINK, TOK)
        decay = view(O_CONST + C_DECAY, RET_H, SCORE_W)
        causal = view(O_CONST + C_CAUSAL, SCORE_W)
        expand = view(O_CONST + C_EXPAND, NB, P)
        wend = view(O_CONST + C_WEND, 2, RET_H)
        eps = view(O_CONST + C_EPS, 1)
        prm = view(O_PRM, PR_ROWS)
        dtw = view(O_PRM + PR_DTW, 8, 16)
        c16 = view(O_PRM + PR_C16, 8)
        cols = view(O_PRM + PR_COLS, 232)
        h = view(O_H, NB, TOK)
        xn = view(O_XN, NB, TOK)
        ring = view(O_RING, RING, 8, 256)
        u = view(O_U, NB, TOK)
        zr = view(O_Z, NB, TOK)
        g = view(O_G, NB, TOK)
        qk = view(O_QK, NB, TOK)
        v = view(O_V, NB, TOK)
        xc = view(O_XC, CB, XC_W)
        sv = view(O_SV, SLOTS, 64)
        u4 = view(O_U4, PAIRS, U4_W)
        gw = view(O_GW, 2, PAIRS, P)
        bb = view(O_BB, 2, PAIRS, 16)
        ct = view(O_CT, 2, PAIRS, 16)

        tables_in = sem("tables_in")
        w_landed = [sem(f"w_landed{i}") for i in range(RING)]
        chunk_used = sem("chunk_used")
        proj_filled = sem("proj_filled")
        proj_drained = sem("proj_drained")
        bank_filled = [sem(f"bank_filled{i}") for i in range(4)]
        bank_drained = [sem(f"bank_drained{i}") for i in range(4)]
        dve_step, act_step, pool_step = sem("dve_step"), sem("act_step"), sem("pool_step")
        names = """const_in x_rest square_sum vec_in s5_in b_in c_in h0_in convst_in head_in dtw_in squares mean_ready
            rstd_ready xn_ready prm_ready s5a_cols trig_arg trig_ready powers_ready pool_zero u4_ready
            bd_ready conv_y conv_t conv_silu tails_out rope_done g_silu pairs_joined scan_done newst_ready
            s5st_out e_ready gelu_arg gelu_tanh gelu_done z_silu st_out pair_sums dec_in0 dec_in1 dec_in2
            dec_out0 dec_out1 dec_out2 ret_yc retsq ret_norm gates_m dt_abs dt_exp alog_exp acum_ready
            wend_exp dt_rows exp_ready exp_masked ssd_yz ssdsq ssd_norm merged hid_ready resid x_in y_rows
            y_out scan_step""".split()
        s = {n: sem(n) for n in names}
        all_sems = w_landed + [chunk_used, proj_filled, proj_drained] + bank_filled + bank_drained \
            + [dve_step, act_step, pool_step] + list(s.values())
        numbers = sorted(x.num for x in all_sems)
        sem_range = range(numbers[0], numbers[-1] + 1)
        assert len(numbers) == len(sem_range)

        def bank(name):
            return banks[4 + FILL[name][0]]

        def filled(eng, name):
            eng.wait_ge(bank_filled[FILL[name][0]], FILL[name][1])

        def drained(eng, name):
            eng.wait_ge(bank_drained[FILL[name][0]], FILL[name][1])

        def is_drained(ins, name):
            ins.then_inc(bank_drained[FILL[name][0]], 1)

        class Chain:

            def __init__(self, eng, semaphore):
                self.eng, self.sem, self.n = eng, semaphore, 0

            def step(self, ins):
                ins.then_inc(self.sem, 1)
                self.n += 1

            def wait(self):
                self.eng.wait_ge(self.sem, self.n)

            def link(self, ins):
                self.step(ins)
                self.wait()

        def layer_of(ap, lyr):
            dims = " ".join("abcde"[:len(ap.shape) - 1])
            first, rest = dims.split(" ")[0], " ".join(dims.split(" ")[1:])
            return ap[bass.ds(lyr, 1)].rearrange(f"o {dims} -> (o {first}) {rest}".strip())

        xld = view(O_R, 2, D_MODEL)
        xsld = view(O_R + 2 * D_MODEL, D_MODEL, p1=SAMPLES)
        with nc.Block() as block:
            @block.sync
            def _(sp):
                sp.dma_start(arena[:, O_CONST:O_CONST + C_FIRST], t["consts"][:, 0:C_FIRST]).then_inc(s["const_in"], 16)
                x_blocks = t["x_prompt"].rearrange("o (tb p) d -> p (o tb) d", p=P)
                sp.dma_start(xld[:, :, 0:D_MODEL // 2], x_blocks[:, :, 0:D_MODEL // 2]).then_inc(s["x_in"], 16)
                sp.dma_start(xsld, t["x_sample"].rearrange("b o d -> (b o) d")).then_inc(s["x_in"], 16)
                sp.dma_start(xld[:, :, D_MODEL // 2:], x_blocks[:, :, D_MODEL // 2:]).then_inc(s["x_rest"], 16)
                sp.dma_start(arena[:, O_CONST + C_FIRST:O_CONST + CONST_W], t["consts"][:, C_FIRST:CONST_W])\
                  .then_inc(tables_in, 16)

            @block.tensor
            def _(pe):
                pe.wait_ge(s["const_in"], 16)
                pe.wait_ge(s["x_in"], 32)
                for k in range(NB):
                    if k == 4:
                        pe.wait_ge(s["x_rest"], 16)
                    if k >= 4:
                        pe.wait_ge(proj_drained, k - 3)
                    for tb in range(2):
                        pe.transpose(banks[k % 4][:, tb * P:(tb + 1) * P], xld[:, tb, k * P:(k + 1) * P], ident)
                    pe.transpose(banks[k % 4][:, SEQ:TOK], xsld[:, k * P:(k + 1) * P],
                                 ident[0:SAMPLES, 0:SAMPLES]).then_inc(proj_filled, 1)

            @block.scalar
            def _(act):
                for k in range(NB):
                    act.wait_ge(proj_filled, k + 1)
                    nc.scalar.activation(h[:, k, :], banks[k % 4][:, 0:TOK], ACT.Copy).then_inc(proj_drained, 1)

        nc.all_engine_barrier(sems_to_clear=sem_range)

        def add_squares(chain, dve):
            half = NB // 2
            for k in range(half):
                chain.step(nc.vector.tensor_tensor(zr[:, k, :], h[:, k, :], h[:, k, :], ALU.mult))
            chain.wait()
            chain.link(nc.vector.tensor_tensor(zr[:, 0:2, :], zr[:, 0:2, :], zr[:, 2:4, :], ALU.add))
            for k in (half, half + 1, half + 2, half + 3):
                dve.wait_ge(s["squares"], k - half + 1)
                chain.link(nc.vector.tensor_tensor(zr[:, k % 2, :], zr[:, k % 2, :], zr[:, k, :], ALU.add))
            nc.vector.tensor_tensor(zr[:, 0, :], zr[:, 0, :], zr[:, 1, :], ALU.add).then_inc(s["square_sum"], 1)

        pwr = view(O_SM, 5, 2, PAIRS)
        a4r, a4i = view(O_SM + 320, 64), view(O_SM + 384, 64)
        qfac = view(O_SM + 448, 2, PAIRS)
        trig = view(O_SM + 512, 8, 2, PAIRS)
        a8w = view(O_SM + 896, 2, 64)
        s5v = view(O_SM + 1024, 4, PAIRS)
        vrow = view(O_SM + 1152, P)
        prow = view(O_SM + 1280, 4, P, p1=PAIRS)
        dtrow = view(O_SM + 1792, 2, p1=PAIRS)
        a1r, a1i = small[:, 64:128], small[:, 128:192]
        et = view(O_SM + 1024, 4, 16, 16)
        news = view(O_STOUT, 4, P)
        newp = view(O_STOUT + 512, P, p1=64)
        braw = view(O_SV + 1024, 2, PAIRS, 16)
        btmp = view(O_SV + 2048, 4, PAIRS, 16)
        bd = view(O_QK, 2, 16, P)
        convst = view(O_GW, CONV_DIM, p1=SAMPLES * (TAPS - 1))
        craw = view(O_GW + 2048, 2, 8, P)
        h0raw = view(O_GW + 4096, 4, P)
        eb = view(O_GW, 2, 16, 5, 32)
        toep = view(O_GW + 5120, 16, P)
        bblk = view(O_GW + 7168, 2, 16, 32)
        rms, rstd = view(O_G, TOK), view(O_G + TOK, TOK)
        convy = view(O_G, 3, 2, CONV_OUT)
        tailc = view(O_G + 1900, CB, 11)
        tailr = view(O_Z, CONV_DIM, p1=11)
        dts = view(O_DTS, 8, TOK, p1=HEADS)
        DT_X, DT_E, DT_S, DT_DELTA, DT_LA, DT_AC, DT_DW, DT_RHS = range(8)
        vtok, vw = view(O_VTOK, 2, D_MODEL), view(O_VW, 2, D_MODEL)
        btok = view(O_BTOK, 2, 512)
        sc = view(O_SC, 2, SCORE_W)
        seg, ex = view(O_SEG, 2, SCORE_W), view(O_EXP, 2, SCORE_W)
        dec = view(O_DEC, 3, NB, P)
        outer = view(O_TMP, 2, NB, P)
        stout = view(O_STOUT, NB, P)
        zg = view(O_ZG, NB, TOK)
        m_ = view(O_M, NB, TOK)
        sq8 = view(O_VTOK, NB, TOK)
        head_rms = view(O_SEG, 4, TOK)
        hid = view(O_HID, 32, TOK)
        vs, ys = view(O_PRM + PR_VS, NB, SAMPLES), small[:, 0:64].rearrange("p (a b) -> p a b", a=NB)
        gam = retention_gammas()

        def at(name):
            return BLOCKS[name]

        def layer(nc, block, t, lyr):
            def vec(name):
                return layer_of(t[name], lyr)

            @block.sync
            def _(sp):
                def cols_of(name, col0):
                    w = layer_of(t[name], lyr).rearrange("(k p) n -> p k n", p=P)
                    return lambda c: w[:, :, bass.ds(col0 + 256 * c, 256)]

                def load(unit_no, source, before, chunks=range(RING)):
                    for c in chunks:
                        before(c)
                        sp.dma_start(ring[:, c, :, :], source(c)).then_inc(w_landed[c], 16)

                def after_unit(first_block):
                    return lambda c: sp.wait_ge(proj_filled, first_block + 2 * c + 2)

                load(0, cols_of("w_in", COL_U), lambda c: None, chunks=(0,))
                for name, row, n in (("norm1_w", PR_N1, 8), ("norm2_w", PR_N2, 8), ("s5_d", PR_D, 8),
                                     ("ssd_norm_w", PR_SN, 8), ("ssd_conv_b", PR_CB, 16)):
                    sp.dma_start(vrow[row:row + n, :], vec(name).rearrange("(r p) -> r p", p=P)).then_inc(s["vec_in"], 16)
                sp.dma_start(vrow[PR_CW:PR_FN, :], vec("ssd_conv_w").rearrange("t (r p) -> (t r) p", p=P))\
                  .then_inc(s["vec_in"], 16)
                sp.dma_start(vrow[PR_FN:PR_ROWS, :], t["final_norm_w"].rearrange("(r p) -> r p", p=P))\
                  .then_inc(s["vec_in"], 16)
                sp.dma_start(prow[:, 0, :], vec("s5_a_re").rearrange("(m g) p -> m (g p)", g=2)).then_inc(s["s5_in"], 16)
                sp.dma_start(prow[:, 1, :], vec("s5_a_im").rearrange("(m g) p -> m (g p)", g=2)).then_inc(s["s5_in"], 16)
                sp.dma_start(dtrow, vec("s5_log_dt").rearrange("(m g) -> m g", g=2)).then_inc(s["s5_in"], 16)
                load(0, cols_of("w_in", COL_U), lambda c: None, chunks=(1, 2, 3))
                for ri, name in enumerate(("s5_b_re", "s5_b_im")):
                    sp.dma_start(braw[:, ri, :, :], vec(name).rearrange("(m g) p c -> (g p) m c", g=2))\
                       .then_inc(s["b_in"], 16)
                with sp.Fori(0, 2) as j:
                    load(1 + j, cols_of("w_in", COL_X + j * 1024), after_unit(at("u") + 8 * j))
                for name, arr, col in (("qk", "w_in", COL_QK), ("v", "w_in", COL_V), ("g", "w_in", COL_G),
                                       ("z", "w_in", COL_Z), ("s5a", "w_s5_out", 0), ("s5b", "w_s5_out", 1024),
                                       ("gate0", "w_in", COL_GATE), ("reto", "w_ret_out", 0),
                                       ("gate2", "w_in", COL_GATE + 2048), ("gate1", "w_in", COL_GATE + 1024),
                                       ("ssdo", "w_ssd_out", 0), ("wo", "w_out", 0)):
                    n = UNITS.index(name)
                    load(n, cols_of(arr, col), after_unit(at(UNITS[n - 1])))
                with sp.Fori(0, 4) as j:
                    load(15 + j, cols_of("w_mlp_up", j * 1024), after_unit(at("wo") + 8 * j))
                down = layer_of(t["w_mlp_down"], lyr).rearrange("(r k p) n -> p r k n", r=4, p=P)
                load(19, lambda c: down[:, c, :, 0:256], after_unit(at("up3")))
                with sp.Fori(1, 4) as j:
                    def before(c):
                        if c < 3:
                            sp.wait_ge(chunk_used, 3 * j + (c - 2))
                        else:
                            sp.wait_ge(proj_filled, at("dn0") + 2 * j)
                    load(19 + j, lambda c: down[:, c, :, bass.ds(j * 256, 256)], before)

            @block.tensor
            def _(pe):
                def open_fill(name):
                    b, f = FILL[name]
                    if f > 1:
                        pe.wait_ge(bank_drained[b], f - 1)
                    return banks[4 + b]

                def close_fill(ins, name):
                    ins.then_inc(bank_filled[FILL[name][0]], 1)

                def unit(n, first, rhs, fresh=False, ready=None, before=None):
                    for b in range(8):
                        c = b // 2
                        if before:
                            before(b)
                        if b % 2 == 0:
                            pe.wait_ge(w_landed[c], n * 16 + 16)
                        if not (fresh and b < 4):
                            pe.wait_ge(proj_drained, first + (b - 3))
                        for k in range(8):
                            if ready and b == 0:
                                pe.wait_ge(s[ready[0]], ready[1] + k + 1)
                            mm = pe.matmul(banks[b % 4][:, 0:TOK], ring[:, c, k, (b % 2) * P:(b % 2) * P + P],
                                           rhs[:, k, :], start=(k == 0), stop=(k == 7))
                        mm.then_inc(proj_filled, 1)

                def named(name, rhs, **kw):
                    unit(UNITS.index(name), at(name), rhs, **kw)

                def sum_squares(name, src, blocks, ready, first):
                    o = open_fill(name)
                    for i, k in enumerate(blocks):
                        pe.wait_ge(s[ready], first + i + 1)
                        mm = pe.matmul(o[:, 0:TOK], ones, src[:, k, :], start=(i == 0), stop=(i == len(blocks) - 1))
                    close_fill(mm, name)

                o = open_fill("n1")
                pe.wait_ge(s["square_sum"], 1)
                close_fill(pe.matmul(o[:, 0:TOK], ones, zr[:, 0, :], start=True, stop=True), "n1")
                pe.wait_ge(s["vec_in"], 112)
                o = open_fill("prm")
                close_fill(pe.transpose(o[:, 0:PR_ROWS], vrow[0:PR_ROWS, :], ident[0:PR_ROWS, 0:PR_ROWS]), "prm")

                def s5_vectors():
                    o = open_fill("s5p")
                    pe.wait_ge(s["s5a_cols"], 2)
                    for i in range(4):
                        mm = pe.transpose(o[:, i * 32:(i + 1) * 32], prow[:, i, :], ident[0:32, 0:32])
                    close_fill(mm, "s5p")

                def c_and_states():
                    pe.wait_ge(s["c_in"], 64)
                    for ri, nm in enumerate(("cre", "cim")):
                        for i in range(2):
                            o = open_fill(f"{nm}{i}")
                            for j in range(4):
                                mm = pe.transpose(o[:, j * P:(j + 1) * P], craw[:, ri, 4 * i + j, :], ident)
                            close_fill(mm, f"{nm}{i}")
                    pe.wait_ge(s["h0_in"], 64)
                    o = open_fill("h0")
                    for j in range(4):
                        mm = pe.transpose(o[:, j * P:(j + 1) * P], h0raw[:, j, :], ident)
                    close_fill(mm, "h0")
                    pe.wait_ge(s["convst_in"], 16)
                    o = open_fill("cs")
                    for j in range(CB):
                        mm = pe.transpose(o[:, j * 24:(j + 1) * 24], convst[:, j * P:(j + 1) * P], ident[0:24, 0:24])
                    close_fill(mm, "cs")

                unit(0, 0, xn, fresh=True, ready=("xn_ready", 0), before=lambda b: s5_vectors() if b == 2 else None)

                def s5_input_matrices(sl):
                    pe.wait_ge(s["bd_ready"], sl + 1)
                    for ri in range(2):
                        for i in range(4):
                            nm = f"G{8 * sl + 4 * ri + i}"
                            o = open_fill(nm)
                            for j in range(4):
                                mm = pe.transpose(o[:, j * P:(j + 1) * P], bd[:, ri, 4 * i + j, :], ident)
                            close_fill(mm, nm)

                def s5_chunk_inputs(i):
                    for ri in range(2):
                        nm = f"V{2 * i + ri}"
                        o = open_fill(nm)
                        drained(pe, f"G{8 * (i // 4) + 4 * ri + i % 4}")
                        for j in range(4):
                            m = 4 * i + j
                            mm = pe.matmul(o[:, j * 72:(j + 1) * 72], gw[:, ri, m, :], u4[:, m, 8:80],
                                           start=True, stop=True)
                        close_fill(mm, nm)

                def in_x0(b):
                    if b == 1:
                        c_and_states()
                    elif b == 5:
                        s5_input_matrices(0)

                def in_x1(b):
                    if b == 2:
                        s5_input_matrices(1)
                        pe.wait_ge(s["u4_ready"], 1)
                    elif 3 <= b < 7:
                        s5_chunk_inputs(2 * b - 6)
                        s5_chunk_inputs(2 * b - 5)

                named("x0", xn, before=in_x0)
                named("x1", xn, before=in_x1)
                pe.wait_ge(proj_drained, 24)
                for i in range(4):
                    o = open_fill(f"tail{i}")
                    for j in range(4):
                        mm = pe.transpose(o[0:11, j * P:(j + 1) * P], tailc[:, 4 * i + j, :], ident)
                    close_fill(mm, f"tail{i}")
                named("qk", xn)

                def s5_toeplitz(hf):
                    pe.wait_ge(s["e_ready"], hf + 1)
                    for i in range(4):
                        nm = f"K{hf}{i}"
                        o = open_fill(nm)
                        for j in range(4):
                            lm = 4 * i + j
                            pe.matmul(o[0:32, j * P:(j + 1) * P], bblk[:, 0, lm, :],
                                      eb[:, 0, lm, 0:4, :].rearrange("p a b -> p (a b)"), start=True, stop=False)
                            mm = pe.matmul(o[0:32, j * P:(j + 1) * P], bblk[:, 1, lm, :],
                                           eb[:, 1, lm, 0:4, :].rearrange("p a b -> p (a b)"), start=False, stop=True)
                        close_fill(mm, nm)

                def s5_outputs(hf):
                    if hf == 0:
                        pe.wait_ge(s["scan_done"], 2)
                    for i in range(4):
                        nm = f"Y{hf}{i}"
                        o = open_fill(nm)
                        drained(pe, f"K{hf}{i}")
                        for j in range(4):
                            lm, m = 4 * i + j, 16 * hf + 4 * i + j
                            out = o[:, j * 72:(j + 1) * 72]
                            pe.matmul(out, toep[:, lm, :], u4[:, m, 0:72], start=True, stop=False)
                            pe.matmul(out, eb[:, 0, lm, 1:5, :].rearrange("p a b -> p (a b)"), sv[:, 0:72, m],
                                      start=False, stop=False)
                            mm = pe.matmul(out, eb[:, 1, lm, 1:5, :].rearrange("p a b -> p (a b)"),
                                           sv[:, 0:72, 32 + m], start=False, stop=True)
                        close_fill(mm, nm)

                named("v", xn, before=lambda b: s5_toeplitz(0) if b == 4 else None)
                named("g", xn, before=lambda b: s5_outputs(0) if b == 4 else None)
                def spread(name, column):
                    o = open_fill(name)
                    for j in range(4):
                        mm = pe.transpose(o[:, j * P:(j + 1) * P], column(j).to_broadcast([P, P]), ident)
                    close_fill(mm, name)

                def spread_ret(b):
                    spread(f"rkb{b}", lambda j: qk[:, 4 + j, SEQ + b:SEQ + b + 1])
                    spread(f"rqb{b}", lambda j: qk[:, j, SEQ + b:SEQ + b + 1])

                def spread_ssd(b):
                    spread(f"skb{b}", lambda j: xc[:, 8 + j, SEQ + b:SEQ + b + 1])
                    spread(f"sqb{b}", lambda j: xc[:, 12 + j, SEQ + b:SEQ + b + 1])

                def s5_states_and_steps():
                    pe.wait_ge(s["newst_ready"], 1)
                    o = open_fill("nss")
                    for j in range(4):
                        mm = pe.transpose(o[:, j * P:(j + 1) * P],
                                          sv[:, 73 + 2 * j:75 + 2 * j, :].rearrange("p a b -> p (a b)"), ident)
                    close_fill(mm, "nss")
                    o = open_fill("nsp")
                    close_fill(pe.transpose(o[0:64, 0:P], sv[:, 72, :], ident), "nsp")
                    pe.wait_ge(s["dtw_in"], 16)
                    o = open_fill("dt")
                    for k in range(8):
                        mm = pe.matmul(o[0:HEADS, 0:TOK], dtw[:, k, :], xn[:, k, :], start=(k == 0), stop=(k == 7))
                    close_fill(mm, "dt")

                def in_z(b):
                    if b == 1:
                        s5_toeplitz(1)
                    elif b == 3:
                        s5_outputs(1)
                    elif b == 5:
                        s5_states_and_steps()
                named("z", xn, before=in_z)

                for i in range(4):
                    o = open_fill(f"rv{i}")
                    for j in range(4):
                        tb = i // 2
                        mm = pe.transpose(o[:, j * P:(j + 1) * P], v[:, 4 * (i % 2) + j, tb * P:(tb + 1) * P], ident)
                    close_fill(mm, f"rv{i}")
                def scores(name, keys, queries):
                    o = open_fill(name)
                    pe.matmul(o[:, 0:SEQ], keys[:, 0:P], queries[:, 0:SEQ], start=True, stop=True)
                    close_fill(pe.matmul(o[:, SEQ:SCORE_W], keys[:, P:SEQ], queries[:, P:SEQ],
                                         start=True, stop=True), name)

                def ret_scores(hh):
                    scores(f"rs{hh}", qk[:, 4 + hh, :], qk[:, hh, :])

                def ret_outputs(hh):
                    o = open_fill(f"ry{hh}")
                    drained(pe, f"rs{hh}")
                    if hh == 0:
                        drained(pe, "rv3")
                    for ph in range(2):
                        vcol = (2 * hh + ph) * P
                        pe.matmul(o[:, ph * SEQ:(ph + 1) * SEQ], vtok[:, 0, vcol:vcol + P], sc[:, hh % 2, 0:SEQ],
                                  start=True, stop=False)
                        mm = pe.matmul(o[:, ph * SEQ + P:(ph + 1) * SEQ], vtok[:, 1, vcol:vcol + P],
                                       sc[:, hh % 2, SEQ:SCORE_W], start=False, stop=True)
                    close_fill(mm, f"ry{hh}")

                pe.wait_ge(s["rope_done"], 8)
                ret_scores(0)
                ret_scores(1)
                for tb in range(2):
                    o = open_fill(f"rk{tb}")
                    for hh in range(4):
                        mm = pe.transpose(o[:, hh * P:(hh + 1) * P], qk[:, 4 + hh, tb * P:(tb + 1) * P], ident)
                    close_fill(mm, f"rk{tb}")
                ret_outputs(0)
                for hh in range(1, 4):
                    if hh < 3:
                        ret_scores(hh + 1)
                    ret_outputs(hh)

                def end_states(name, half, left, right):
                    o = open_fill(name)
                    for j in range(4):
                        for tb in range(2):
                            mm = pe.matmul(o[:, j * P:(j + 1) * P], left(tb, 4 * half + j), right(tb, 4 * half + j),
                                           start=(tb == 0), stop=(tb == 1))
                    close_fill(mm, name)

                drained(pe, "rk1")
                for half in range(2):
                    end_states(f"rst{half}", half, lambda tb, b: vtok[:, tb, b * P:(b + 1) * P],
                               lambda tb, b: btok[:, tb, (b // 2) * P:(b // 2 + 1) * P])

                def ret_sample(unit_name):
                    def at_block(b):
                        if (unit_name, b) in RET_SAMPLE_AT:
                            spread_ret(RET_SAMPLE_AT[unit_name, b])
                    return at_block
                named("s5a", u, ready=("gelu_done", 0), before=ret_sample("s5a"))
                named("s5b", u, before=ret_sample("s5b"))
                def group_means(pfx):
                    for hh in range(4):
                        o = open_fill(f"{pfx}{hh}")
                        pe.wait_ge(s["pair_sums"], 4 * (pfx == "sn") + hh + 1)
                        close_fill(pe.matmul(o[:, 0:TOK], ones, sq8[:, 2 * hh, :], start=True, stop=True), f"{pfx}{hh}")

                named("gate0", xn, before=lambda b: group_means("rn") if b == 1 else None)
                pe.wait_ge(s["dt_rows"], 4)
                pe.wait_ge(tables_in, 16)
                o = open_fill("sc")
                for i, r in enumerate((DT_AC, DT_DELTA, DT_DW)):
                    for tb in range(2):
                        c = (2 * i + tb) * 16
                        pe.transpose(o[:, c:c + 16], dts[:, r, tb * P:(tb + 1) * P], ident[0:16, 0:16])
                for b in range(NB):
                    mm = pe.matmul(o[:, 96 + 17 * b:96 + 17 * b + 17], expand[0:HEADS, b, :], dts[:, DT_RHS, 0:17],
                                   start=True, stop=True)
                close_fill(mm, "sc")
                for i in range(4):
                    o = open_fill(f"sv{i}")
                    for j in range(4):
                        tb = i // 2
                        mm = pe.transpose(o[:, j * P:(j + 1) * P], xc[:, 4 * (i % 2) + j, tb * P:(tb + 1) * P], ident)
                    close_fill(mm, f"sv{i}")
                for tb in range(2):
                    o = open_fill(f"sb{tb}")
                    for gg in range(4):
                        mm = pe.transpose(o[:, gg * P:(gg + 1) * P], xc[:, 8 + gg, tb * P:(tb + 1) * P], ident)
                    close_fill(mm, f"sb{tb}")

                def head_decays(m):
                    o = open_fill(f"sa{m}")
                    for h2 in range(2):
                        for tb in range(2):
                            c = tb * HEADS + 2 * m + h2
                            mm = pe.transpose(o[:, h2 * SEQ + tb * P:h2 * SEQ + (tb + 1) * P],
                                              cols[:, c:c + 1].to_broadcast([P, P]), ident)
                    close_fill(mm, f"sa{m}")

                drained(pe, "sc")
                scores("ss0", xc[:, 8, :], xc[:, 12, :])
                head_decays(0)

                def head_outputs(m):
                    o = open_fill(f"sy{m}")
                    if m == 0:
                        drained(pe, "sv3")
                    for h2 in range(2):
                        pe.wait_ge(s["exp_masked"], 2 * m + h2 + 1)
                        hc = (2 * m + h2) * HEAD_DIM
                        pe.matmul(o[64 * h2:64 * h2 + 64, 0:SEQ], vtok[:, 0, hc:hc + HEAD_DIM], ex[:, h2, 0:SEQ],
                                  start=True, stop=False)
                        mm = pe.matmul(o[64 * h2:64 * h2 + 64, P:SEQ], vtok[:, 1, hc:hc + HEAD_DIM],
                                       ex[:, h2, SEQ:SCORE_W], start=False, stop=True)
                    close_fill(mm, f"sy{m}")

                def in_reto(m):
                    if m > 0:
                        head_outputs(m - 1)
                    if m % 2 and m < 7:
                        gg = (m + 1) // 2
                        scores(f"ss{gg}", xc[:, 8 + gg, :], xc[:, 12 + gg, :])
                    if m < 7:
                        head_decays(m + 1)
                    if m % 2:
                        spread_ssd(m // 2)

                named("reto", v, ready=("ret_norm", 0), before=in_reto)
                head_outputs(7)
                named("gate2", xn, before=lambda b: spread_ssd(4 + b // 2) if b % 2 == 0 else None)
                named("gate1", xn, before=lambda b: group_means("sn") if b == 5 else None)
                named("ssdo", xc[:, :, 0:TOK], ready=("ssd_norm", 0))
                named("wo", m_, ready=("merged", 0))
                sum_squares("n2", zr, range(NB), "squares", NB // 2)
                drained(pe, "sb1")
                for half in range(2):
                    end_states(f"sst{half}", half, lambda tb, b: vw[:, tb, b * P:(b + 1) * P],
                               lambda tb, b: btok[:, tb, (b // 2) * P:(b // 2 + 1) * P])
                with pe.Fori(0, 4) as j:
                    unit(15 + j, at("up0") + 8 * j, xn, ready=("xn_ready", 8))
                with pe.Fori(0, 2) as jj:
                    for half in range(2):
                        for c in range(4):
                            pe.wait_ge(w_landed[c], (2 * jj + half) * 16 + 320)
                            pe.wait_ge(s["hid_ready"], 8 * c + 8)
                            for b in range(2):
                                if c == 0:
                                    pe.wait_ge(proj_drained, at("dn0") + 4 * jj + (2 * half + b - 3))
                                for k in range(8):
                                    mm = pe.matmul(banks[2 * half + b][:, 0:TOK], ring[:, c, k, b * P:(b + 1) * P],
                                                   hid[:, 8 * c + k, :], start=(c == 0 and k == 0),
                                                   stop=(c == 3 and k == 7))
                                if c == 3:
                                    mm.then_inc(proj_filled, 1)
                            if c < 3:
                                mm.then_inc(chunk_used, 1)

            @block.scalar
            def _(act):
                chain = Chain(act, act_step)

                def copy(out, in_, scale=1.0):
                    return nc.scalar.activation(out, in_, ACT.Copy, scale=scale)

                def tanh(out, in_, scale=0.5):
                    return nc.scalar.activation(out, in_, ACT.Tanh, scale=scale)

                def fetch_sqrt_table():
                    nc.scalar.activation(table_warm[:, :], eps, ACT.Sqrt)

                def root_mean(out, name, width):
                    filled(act, name)
                    is_drained(nc.scalar.activation(out, bank(name)[:, 0:TOK], ACT.Sqrt, scale=1.0 / width, bias=eps), name)

                def ret_tiles(name):
                    return layer_of(t[name], lyr).rearrange("b h (q p) n -> b p (h q) n", p=P)

                def ssd_tiles(name):
                    return layer_of(t[name], lyr).rearrange("b (k g) p n -> b (g p) k n", g=2)

                states = {"r": (ret_tiles("state_ret"), ret_tiles("new_ret_s")),
                          "s": (ssd_tiles("state_ssd"), ssd_tiles("new_ssd_s"))}

                def drain_unit(first, block_ops, blocks=8, before=None):
                    for b in range(blocks):
                        if before:
                            before(b)
                        act.wait_ge(proj_filled, first + (b + 1))
                        block_ops(b, banks[b % 4][:, 0:TOK]).then_inc(proj_drained, 1)

                fetch_sqrt_table()
                for k in range(NB // 2, NB):
                    nc.scalar.activation(zr[:, k, :], h[:, k, :], ACT.Square).then_inc(s["squares"], 1)
                root_mean(rms, "n1", D_MODEL)
                filled(act, "prm")
                is_drained(copy(prm, bank("prm")[:, 0:PR_ROWS]), "prm")
                for ri, name in enumerate(("s5_c_re", "s5_c_im")):
                    for dup in range(2):
                        act.dma_start(craw[:, ri, :, dup * 64:(dup + 1) * 64],
                                      vec(name).rearrange("(t g) c p -> (g c) t p", g=8)).then_inc(s["c_in"], 16)
                for ri, name in enumerate(("state_s5_re", "state_s5_im")):
                    for b2 in range(2):
                        p0 = 64 * b2 + 32 * ri
                        act.dma_start(h0raw[p0:p0 + 32, :, :],
                                      vec(name).rearrange("(bp b) (m g) p -> b m bp (g p)", b=2, g=2)[b2])\
                           .then_inc(s["h0_in"], 16)
                act.dma_start(convst, vec("state_conv").rearrange("b t c -> (b t) c")).then_inc(s["convst_in"], 16)
                for i, name in enumerate(("ssd_dt_bias", "ssd_a_log", "ssd_d")):
                    act.dma_start(c16[0:HEADS, i:i + 1], vec(name).rearrange("(h o) -> h o", o=1)).then_inc(s["head_in"], 16)
                act.dma_start(dtw, vec("w_in").rearrange("(k p) n -> p k n", p=P)[:, :, COL_DT:COL_DT + HEADS])\
                   .then_inc(s["dtw_in"], 16)
                act.dma_start(vec("new_conv_s")[:, 0:TAPS - 2, :], vec("state_conv")[:, 1:TAPS - 1, :])\
                   .then_inc(s["tails_out"], 16)
                def in_u(b):
                    if b == 0:
                        act.wait_ge(s["s5_in"], 48)
                        nc.scalar.activation(dtrow, dtrow, ACT.Exp).then_inc(s["trig_ready"], 1)
                    elif b == 2:
                        filled(act, "s5p")
                        is_drained(copy(s5v, bank("s5p")[:, 0:P].rearrange("p (a b) -> p a b", a=4)), "s5p")
                        drained(act, "s5p")
                        nc.scalar.activation(trig[:, 7, 0, :], s5v[:, 2, :], ACT.Exp).then_inc(s["trig_ready"], 1)
                    elif b == 4:
                        act.wait_ge(s["trig_arg"], 1)
                        nc.scalar.activation(trig[:, 5, :, :], trig[:, 6, :, :], ACT.Sin).then_inc(s["trig_ready"], 1)

                def in_x0(b):
                    if b != 1:
                        return
                    for ri, nm in enumerate(("cre", "cim")):
                        for i in range(2):
                            filled(act, f"{nm}{i}")
                            src = bank(f"{nm}{i}").rearrange("p (m g c) -> p m g c", g=2, c=16)
                            copy(ct[0:64, ri, 16 * i:16 * i + 16, :], src[0:64, :, 0, :])
                            is_drained(copy(ct[64:128, ri, 16 * i:16 * i + 16, :], src[64:128, :, 1, :]), f"{nm}{i}")
                    filled(act, "h0")
                    is_drained(copy(sv[:, 0:SAMPLES, :].rearrange("p a b -> p (a b)"), bank("h0")[:, :]), "h0")
                    filled(act, "cs")
                    is_drained(copy(xc[:, :, TAPS - 1 + SEQ:].rearrange("p k (b t) -> p k b t", t=TAPS)[:, :, :, 0:TAPS - 1],
                                    bank("cs")[:, 0:24 * CB].rearrange("p (k b t) -> p k b t", k=CB, t=TAPS - 1)), "cs")

                drain_unit(0, lambda b, ps: copy(u[:, b, :], ps), before=in_u)
                new0 = TAPS - 1 + SEQ + TAPS - 1

                def xbc(k, ps):
                    copy(xc[:, k, TAPS - 1:TAPS - 1 + SEQ], ps[:, 0:SEQ])
                    copy(xc[:, k, new0:XC_W:TAPS], ps[:, SEQ:TOK])
                    return copy(tailc[:, k, :], ps[:, SEQ - (TAPS - 1):TOK])

                def conv_tanh(k):
                    act.wait_ge(s["conv_y"], k + 1)
                    tanh(convy[:, k % 3, 1, :], convy[:, k % 3, 0, :], 1.0).then_inc(s["conv_t"], 1)

                def in_x1(b):
                    if 3 <= b < 7:
                        for i in (2 * b - 6, 2 * b - 5):
                            for ri in range(2):
                                filled(act, f"V{2 * i + ri}")
                                c = 32 * ri + 4 * i
                                is_drained(copy(sv[:, 9:SLOTS, c:c + 4],
                                                bank(f"V{2 * i + ri}")[:, 0:288].rearrange("p (j k) -> p k j", j=4)),
                                           f"V{2 * i + ri}")
                    if 4 <= b < 7:
                        for k in range(3 * (b - 4), 3 * (b - 3)):
                            conv_tanh(k)

                drain_unit(at("x0"), xbc, before=in_x0)
                drain_unit(at("x1"), lambda b, ps: xbc(NB + b, ps), before=in_x1)
                for i in range(4):
                    filled(act, f"tail{i}")
                    is_drained(copy(tailr[:, i * 512:(i + 1) * 512], bank(f"tail{i}")[0:11, :]), f"tail{i}")
                for i in range(4):
                    drained(act, f"tail{i}")
                act.dma_start(vec("new_conv_p").rearrange("b t c -> (b t) c"), tailr[0:3, :]).then_inc(s["tails_out"], 16)
                act.dma_start(vec("new_conv_s")[:, TAPS - 2, :], tailr[3:11, :]).then_inc(s["tails_out"], 16)
                for k in range(9, 13):
                    conv_tanh(k)
                act.wait_ge(s["tails_out"], 48)

                def qk_block(b, ps):
                    copy(qk[:, b, :], ps)
                    copy(zr[0:64, b, :], ps[64:128, :])
                    return copy(zr[64:128, b, :], ps[0:64, :])
                def in_qk(b):
                    if b < 3:
                        conv_tanh(13 + b)
                drain_unit(at("qk"), qk_block, before=in_qk)

                def g_block(b, ps):
                    act.wait_ge(s["rope_done"], b + 1)
                    copy(g[:, b, :], ps, 0.5)
                    return tanh(zr[:, b, :], ps)

                def keep_toeplitz(hf):
                    for i in range(4):
                        filled(act, f"K{hf}{i}")
                        src = bank(f"K{hf}{i}")[0:32, :].rearrange("p (j c) -> p j c", j=4)
                        for r in range(LIFT):
                            ins = copy(toep[32 * r:32 * r + 32, 4 * i:4 * i + 4, 32 * r:P], src[:, :, 0:P - 32 * r])
                        is_drained(ins, f"K{hf}{i}")

                def keep_outputs(hf):
                    act.wait_ge(s["g_silu"], 4 * hf + 4)
                    for i in range(4):
                        filled(act, f"Y{hf}{i}")
                    dst = zr[:, 4 * hf:4 * hf + 4, :]
                    for mm in range(4):
                        rows = slice(32 * mm, 32 * mm + 32)
                        copy(dst[rows, :, SEQ:TOK], psum[0:32, 4:8, 72 * mm:72 * mm + 8])
                        for r in range(LIFT):
                            chain.step(copy(dst[rows, :, r:SEQ:LIFT], psum[32 * r:32 * r + 32, 4:8, 72 * mm + 8:72 * mm + 72]))
                    for i in range(4):
                        is_drained(act.drain(), f"Y{hf}{i}")

                act.wait_ge(s["pairs_joined"], 1)
                drain_unit(at("v"), lambda b, ps: copy(v[:, b, :], ps), before=lambda b: keep_toeplitz(0) if b == 4 else None)
                act.wait_ge(s["conv_silu"], 16)
                drain_unit(at("g"), g_block, before=lambda b: keep_outputs(0) if b == 4 else None)
                def load_state(n):
                    if n >= 3:
                        act.wait_ge(s[f"dec_out{n % 3}"], 16 * (n // 3))
                    act.dma_start(dec[:, n % 3, :, :], states["rs"[n // 8]][0][n % 8]).then_inc(s[f"dec_in{n % 3}"], 16)

                def store_state(n):
                    drained(act, f"{'rs'[n // 8]}qb{n % 8}")
                    act.dma_start(states["rs"[n // 8]][1][n % 8], dec[:, n % 3, :, :]).then_inc(s[f"dec_out{n % 3}"], 16)

                def outer_products(n, vcol):
                    pfx, b = "rs"[n // 8], n % 8
                    if n < 15:
                        load_state(n + 1)
                    filled(act, f"{pfx}kb{b}")
                    if n >= 2:
                        drained(act, f"{'rs'[(n - 2) // 8]}qb{(n - 2) % 8}")
                    for blk in range(NB):
                        c = (blk // 2) * P
                        ins = copy(outer[:, b % 2, blk, :], bank(f"{pfx}kb{b}")[:, c:c + P], vcol(blk, b))
                    is_drained(ins, f"{pfx}kb{b}")
                    if b > 0:
                        store_state(n - 1)

                def ret_v(blk, b):
                    return v[:, blk, SEQ + b:SEQ + b + 1]

                def s5_states():
                    filled(act, "nss")
                    is_drained(copy(news.rearrange("p a b -> p (a b)"), bank("nss")[:, :]), "nss")
                    filled(act, "nsp")
                    is_drained(copy(newp, bank("nsp")[0:64, 0:P]), "nsp")
                    drained(act, "nss")
                    drained(act, "nsp")
                    for ri, nm in enumerate(("re", "im")):
                        for b2 in range(2):
                            p0 = 64 * b2 + 32 * ri
                            act.dma_start(vec(f"new_s5_{nm}_s").rearrange("(bp b) (m g) p -> b m bp (g p)", b=2, g=2)[b2],
                                          news[p0:p0 + 32, :, :]).then_inc(s["s5st_out"], 16)
                        act.dma_start(vec(f"new_s5_{nm}_p").rearrange("b (m g) p -> (b m) (g p)", g=2),
                                      newp[32 * ri:32 * ri + 32, :]).then_inc(s["s5st_out"], 16)

                def step_exponentials():
                    act.wait_ge(s["head_in"], 48)
                    nc.scalar.activation(c16[0:HEADS, 3:4], c16[0:HEADS, 1:2], ACT.Exp).then_inc(s["alog_exp"], 1)
                    act.wait_ge(s["dt_abs"], 1)
                    nc.scalar.activation(dts[:, DT_E, :], dts[:, DT_E, :], ACT.Exp, scale=-1.0).then_inc(s["dt_exp"], 1)

                def z_block(b, ps):
                    copy(zg[:, b, :], ps, 0.5)
                    return tanh(m_[:, b, :], ps)

                def in_z(b):
                    if b == 0:
                        act.wait_ge(s["newst_ready"], 1)
                        keep_toeplitz(1)
                    elif b == 3:
                        keep_outputs(1)
                        load_state(0)
                    elif b == 5:
                        s5_states()
                    elif b == 6:
                        step_exponentials()
                drain_unit(at("z"), z_block, before=in_z)
                for i in range(4):
                    filled(act, f"rv{i}")
                    is_drained(copy(vtok[:, i // 2, (i % 2) * 512:(i % 2) * 512 + 512], bank(f"rv{i}")[:, :]), f"rv{i}")
                for k in range(NB):
                    act.wait_ge(s["gelu_arg"], k + 1)
                    tanh(u[:, k, :], u[:, k, :], math.sqrt(2.0 / math.pi)).then_inc(s["gelu_tanh"], 1)
                act.wait_ge(s["acum_ready"], 1)
                nc.scalar.activation(dts[:, DT_DW, 0:SEQ], dts[:, DT_AC, 0:SEQ], ACT.Exp, scale=-1.0,
                                     bias=dts[:, DT_AC, SEQ - 1:SEQ]).then_inc(s["wend_exp"], 1)
                nc.scalar.activation(dts[:, DT_RHS, 8:16], dts[:, DT_LA, SEQ:TOK], ACT.Exp).then_inc(s["dt_rows"], 1)

                for hh in range(4):
                    filled(act, f"ry{hh}")
                    is_drained(copy(v[:, 2 * hh:2 * hh + 2, 0:SEQ],
                                    bank(f"ry{hh}")[:, :].rearrange("p (a b) -> p a b", a=2)), f"ry{hh}")

                def store_states(pfx, dst):
                    for half in range(2):
                        filled(act, f"{pfx}{half}")
                        is_drained(copy(stout[:, 4 * half:4 * half + 4, :],
                                        bank(f"{pfx}{half}")[:, :].rearrange("p (a b) -> p a b", a=4)), f"{pfx}{half}")
                    for half in range(2):
                        drained(act, f"{pfx}{half}")
                    act.dma_start(dst, stout).then_inc(s["st_out"], 16)

                act.wait_ge(s["s5st_out"], 96)
                store_states("rst", vec("new_ret_p").rearrange("b h (q p) n -> p (b h q) n", p=P))
                act.wait_ge(s["gelu_done"], 8)

                def ret_sample(unit_name, b):
                    if (unit_name, b) in RET_SAMPLE_AT:
                        outer_products(RET_SAMPLE_AT[unit_name, b], ret_v)
                drain_unit(at("s5a"), lambda b, ps: copy(zr[:, b, :], ps, 0.25), before=lambda b: ret_sample("s5a", b))
                act.wait_ge(s["z_silu"], 8)

                def in_s5b(b):
                    ret_sample("s5b", b)
                    if b == 4:
                        store_state(7)
                        act.wait_ge(s["ret_yc"], 1)
                    if b >= 4:
                        for k in (2 * b - 8, 2 * b - 7):
                            nc.scalar.activation(sq8[:, k, :], v[:, k, :], ACT.Square).then_inc(s["retsq"], 1)
                drain_unit(at("s5b"), lambda b, ps: tanh(m_[:, b, :], ps, 0.25), before=in_s5b)

                def gate0_block(b, ps):
                    act.wait_ge(s["gates_m"], b + 1)
                    return tanh(zr[:, b, :], ps)

                def in_gate0(b):
                    if b == 2:
                        for hh in range(4):
                            root_mean(head_rms[:, hh, :], f"rn{hh}", RET_P)
                drain_unit(at("gate0"), gate0_block, before=in_gate0)
                filled(act, "sc")
                is_drained(copy(cols, bank("sc")[:, 0:232]), "sc")
                for tb in range(2):
                    filled(act, f"sb{tb}")
                    is_drained(copy(btok[:, tb, :], bank(f"sb{tb}")[:, :]), f"sb{tb}")

                def exponentials(m):
                    drained(act, f"sa{m}")
                    if m >= 1:
                        filled(act, f"sy{m - 1}")
                    for h2 in range(2):
                        nc.scalar.activation(ex[:, h2, :], seg[:, h2, :], ACT.Exp).then_inc(s["exp_ready"], 1)

                def ssd_v(blk, b):
                    return vs[:, blk, b:b + 1]

                def in_reto(b):
                    exponentials(b)
                    if b % 2:
                        outer_products(8 + b // 2, ssd_v)
                drain_unit(at("reto"), lambda b, ps: copy(u[:, b, :], ps), before=in_reto)
                def gate2_block(b, ps):
                    act.wait_ge(s["gates_m"], 9 + b)
                    return tanh(zr[:, b, :], ps)
                drain_unit(at("gate2"), gate2_block, before=lambda b: outer_products(12 + b // 2, ssd_v) if b % 2 == 0 else None)
                store_state(15)

                def in_gate1(b):
                    if b < 4:
                        for k in (2 * b, 2 * b + 1):
                            act.wait_ge(s["ssd_yz"], k + 1)
                            nc.scalar.activation(sq8[:, k, :], xc[:, k, 0:TOK], ACT.Square).then_inc(s["ssdsq"], 1)
                    elif b == 6:
                        for gg in range(4):
                            root_mean(head_rms[:, gg, :], f"sn{gg}", 2 * P)
                drain_unit(at("gate1"), lambda b, ps: tanh(qk[:, b, :], ps), before=in_gate1)

                def ssdo_block(b, ps):
                    act.wait_ge(s["gates_m"], 17 + b)
                    return copy(u[:, b, :], ps)
                drain_unit(at("ssdo"), ssdo_block)
                fetch_sqrt_table()
                drain_unit(at("wo"), lambda b, ps: copy(u[:, b, :], ps, 0.5))
                for k in range(NB):
                    act.wait_ge(s["resid"], k + 1)
                    nc.scalar.activation(zr[:, k, :], h[:, k, :], ACT.Square).then_inc(s["squares"], 1)
                root_mean(rms, "n2", D_MODEL)
                act.wait_ge(s["st_out"], 16)
                store_states("sst", vec("new_ssd_p").rearrange("b (k g) p n -> (g p) (b k) n", g=2))
                with act.Fori(0, 4) as j:
                    drain_unit(at("up0") + 8 * j,
                               lambda b, ps: nc.scalar.activation(hid[:, bass.ds(8 * j + b, 1), :], ps[:, None, :], ACT.Relu))
                with act.Fori(0, 2) as jj:
                    drain_unit(at("dn0") + 4 * jj,
                               lambda b, ps: copy(u[:, bass.ds(4 * jj + b, 1), :], ps[:, None, :]), blocks=4)
                act.wait_ge(s["st_out"], 32)
                for place in range(3):
                    act.wait_ge(s[f"dec_out{place}"], 16 * len(range(place, 16, 3)))

            @block.vector
            def _(dve):
                chain = Chain(dve, dve_step)
                V = nc.vector

                def inverse_root(name, src, dst):
                    drained(dve, name)
                    chain.link(V.reciprocal(dst, src))

                def cmul(re, im, ar, ai, br, bi, tmp):
                    chain.step(V.tensor_tensor(tmp[0], ar, br, ALU.mult))
                    chain.step(V.tensor_tensor(tmp[1], ai, bi, ALU.mult))
                    chain.step(V.tensor_tensor(tmp[2], ar, bi, ALU.mult))
                    chain.step(V.tensor_tensor(tmp[3], ai, br, ALU.mult))
                    chain.wait()
                    chain.step(V.tensor_tensor(re, tmp[0], tmp[1], ALU.subtract))
                    chain.step(V.tensor_tensor(im, tmp[2], tmp[3], ALU.add))
                    chain.wait()

                add_squares(chain, dve)
                inverse_root("n1", rms, rstd)
                drained(dve, "prm")
                for k in range(NB):
                    V.scalar_tensor_tensor(xn[:, k, :], h[:, k, :], prm[:, PR_N1 + k:PR_N1 + k + 1], rstd,
                                           ALU.mult, ALU.mult).then_inc(s["xn_ready"], 1)
                V.tensor_scalar(prm[:, PR_CB:PR_FN], prm[:, PR_CB:PR_FN], 0.5, None, ALU.mult).then_inc(s["prm_ready"], 1)
                dve.wait_ge(s["trig_ready"], 1)
                dve.wait_ge(s["s5_in"], 48)
                for i in range(2):
                    V.tensor_tensor(prow[:, 2 + i, :].rearrange("p (g n) -> p g n", g=2),
                                    prow[:, i, :].rearrange("p (g n) -> p g n", g=2),
                                    dtrow[:, :, None].to_broadcast([PAIRS, 2, 64]), ALU.mult).then_inc(s["s5a_cols"], 1)
                drained(dve, "s5p")
                ang = s5v[:, 3, :]
                big = 12582912.0
                for i, turn in enumerate((0.0, 0.25)):
                    chain.step(V.tensor_scalar(trig[:, 0, i, :], ang, 1.0 / TWO_PI, turn, ALU.mult, ALU.add))
                chain.wait()
                chain.link(V.tensor_scalar(trig[:, 1, :, :], trig[:, 0, :, :], big, None, ALU.add))
                chain.link(V.tensor_scalar(trig[:, 0, :, :], trig[:, 1, :, :], big, None, ALU.subtract))
                c1 = 6.28125
                c2 = float(np.float32(np.floor((TWO_PI - c1) * 2.0 ** 21) / 2.0 ** 21))
                c3 = TWO_PI - c1 - c2
                for i in range(2):
                    chain.step(V.scalar_tensor_tensor(trig[:, 2, i, :], trig[:, 0, i, :], -c1, ang, ALU.mult, ALU.add))
                chain.wait()
                chain.link(V.scalar_tensor_tensor(trig[:, 3, :, :], trig[:, 0, :, :], -c2, trig[:, 2, :, :],
                                                  ALU.mult, ALU.add))
                chain.link(V.scalar_tensor_tensor(trig[:, 2, :, :], trig[:, 0, :, :], -c3, trig[:, 3, :, :],
                                                  ALU.mult, ALU.add))
                chain.link(V.tensor_scalar(trig[:, 2, 1, :], trig[:, 2, 1, :], math.pi / 2, None, ALU.add))
                V.tensor_scalar(trig[:, 6, :, :], trig[:, 2, :, :], 3.1415925, -3.1415925, ALU.min, ALU.max)\
                    .then_inc(s["trig_arg"], 1)
                lre, lim = s5v[:, 0, :], s5v[:, 1, :]
                chain.step(V.tensor_tensor(trig[:, 3, 0, :], lre, lre, ALU.mult))
                chain.step(V.tensor_tensor(trig[:, 3, 1, :], lim, lim, ALU.mult))
                chain.wait()
                chain.link(V.tensor_tensor(trig[:, 4, 0, :], trig[:, 3, 0, :], trig[:, 3, 1, :], ALU.add))
                chain.step(V.reciprocal(trig[:, 4, 1, :], trig[:, 4, 0, :]))
                chain.step(V.memset(pwr[:, 0, 0, :], 1.0))
                chain.step(V.memset(pwr[:, 0, 1, :], 0.0))
                dve.wait_ge(s["trig_ready"], 3)
                chain.step(V.tensor_tensor(pwr[:, 1, 0, :], trig[:, 7, 0, :], trig[:, 5, 1, :], ALU.mult))
                chain.step(V.tensor_tensor(pwr[:, 1, 1, :], trig[:, 7, 0, :], trig[:, 5, 0, :], ALU.mult))
                chain.wait()
                small4 = [trig[:, 1, 0, :], trig[:, 1, 1, :], trig[:, 2, 0, :], trig[:, 2, 1, :]]
                for e_, a_, b_ in ((2, 1, 1), (3, 2, 1), (4, 2, 2)):
                    cmul(pwr[:, e_, 0, :], pwr[:, e_, 1, :], pwr[:, a_, 0, :], pwr[:, a_, 1, :],
                         pwr[:, b_, 0, :], pwr[:, b_, 1, :], small4)
                a8 = trig[:, 5, :, :]
                cmul(a8[:, 0, :], a8[:, 1, :], pwr[:, 4, 0, :], pwr[:, 4, 1, :], pwr[:, 4, 0, :], pwr[:, 4, 1, :], small4)
                for dst_r, dst_i, power in ((a4r, a4i, pwr[:, 4, :, :]), (a1r, a1i, pwr[:, 1, :, :]),
                                            (a8w[:, 0, :], a8w[:, 1, :], a8)):
                    for c in range(2):
                        chain.step(V.tensor_copy(dst_r[:, 32 * c:32 * c + 32], power[:, 0, :]))
                    chain.step(V.tensor_scalar(dst_i[:, 32:64], power[:, 1, :], -1.0, None, ALU.mult))
                    chain.step(V.tensor_copy(dst_i[:, 0:32], power[:, 1, :]))
                chain.wait()
                chain.link(V.tensor_scalar(trig[:, 0, 0, :], pwr[:, 1, 0, :], 1.0, None, ALU.subtract))
                chain.step(V.tensor_tensor(trig[:, 1, 0, :], trig[:, 0, 0, :], lre, ALU.mult))
                chain.step(V.tensor_tensor(trig[:, 1, 1, :], pwr[:, 1, 1, :], lim, ALU.mult))
                chain.step(V.tensor_tensor(trig[:, 2, 0, :], pwr[:, 1, 1, :], lre, ALU.mult))
                chain.step(V.tensor_tensor(trig[:, 2, 1, :], trig[:, 0, 0, :], lim, ALU.mult))
                chain.wait()
                chain.step(V.tensor_tensor(trig[:, 3, 0, :], trig[:, 1, 0, :], trig[:, 1, 1, :], ALU.add))
                chain.step(V.tensor_tensor(trig[:, 3, 1, :], trig[:, 2, 0, :], trig[:, 2, 1, :], ALU.subtract))
                chain.wait()
                for i in range(2):
                    chain.step(V.tensor_tensor(qfac[:, i, :], trig[:, 3, i, :], trig[:, 4, 1, :], ALU.mult))
                chain.wait()
                V.tensor_copy(trig[:, 4, 0, :], trig[:, 3, 0, :]).then_inc(s["powers_ready"], 1)

                def pairwise(ap, n):
                    return ap[:, :, None].to_broadcast([P, n, 16])

                dve.wait_ge(s["b_in"], 32)
                cmul(bb[:, 0, :, :], bb[:, 1, :, :], pairwise(qfac[:, 0, :], PAIRS), pairwise(qfac[:, 1, :], PAIRS),
                     braw[:, 0, :, :], braw[:, 1, :, :], [btmp[:, i, :, :] for i in range(4)])
                dve.wait_ge(s["pool_zero"], 3)
                dve.wait_ge(proj_drained, 8)
                for mm in range(4):
                    src = u[32 * mm:32 * mm + 32, :, :]
                    for r in range(LIFT):
                        V.tensor_copy(u4[32 * r:32 * r + 32, mm:PAIRS:4, 8:72], src[:, :, r:SEQ:LIFT])
                    V.tensor_copy(u4[0:32, mm:PAIRS:4, 0:8], src[:, :, SEQ:TOK])
                    ins = V.tensor_copy(u4[96:128, mm:PAIRS:4, 72:80], src[:, :, SEQ:TOK])
                ins.then_inc(s["u4_ready"], 1)
                for sl in range(2):
                    if sl == 1:
                        filled(dve, "G7")
                    for r in range(LIFT):
                        e_ = LIFT - 1 - r
                        tmp = [btmp[:, i, 16 * (r % 2):16 * (r % 2) + 16, :] for i in range(4)]
                        lo, hi = 16 * sl, 16 * sl + 16
                        ar, ai = pairwise(pwr[:, e_, 0, lo:hi], 16), pairwise(pwr[:, e_, 1, lo:hi], 16)
                        chain.step(V.tensor_tensor(tmp[0], ar, bb[:, 0, lo:hi, :], ALU.mult))
                        chain.step(V.tensor_tensor(tmp[1], ai, bb[:, 1, lo:hi, :], ALU.mult))
                        chain.step(V.tensor_tensor(tmp[2], ar, bb[:, 1, lo:hi, :], ALU.mult))
                        chain.step(V.tensor_tensor(tmp[3], ai, bb[:, 0, lo:hi, :], ALU.mult))
                        chain.wait()
                        tb_ = [x[:, :, None, :].to_broadcast([P, 16, 2, 16]) for x in tmp]
                        out = bd.rearrange("p i m (r g c) -> p i m r g c", r=LIFT, g=2)
                        chain.step(V.tensor_tensor(out[:, 0, :, r, :, :], tb_[0], tb_[1], ALU.subtract))
                        ins = V.tensor_tensor(out[:, 1, :, r, :, :], tb_[2], tb_[3], ALU.add)
                        if r == LIFT - 1:
                            ins.then_inc(s["bd_ready"], 1)
                        else:
                            chain.step(ins)
                    for ri in range(2):
                        for i in range(4):
                            nm = f"G{8 * sl + 4 * ri + i}"
                            filled(dve, nm)
                            is_drained(V.tensor_tensor(gw[:, ri, 16 * sl + 4 * i:16 * sl + 4 * i + 4, :],
                                                       bank(nm)[:, :].rearrange("p (j c) -> p j c", j=4),
                                                       s5mask[:, None, :].to_broadcast([P, 4, P]), ALU.mult), nm)
                drained(dve, "cs")
                dve.wait_ge(s["prm_ready"], 1)

                def conv_silu(k):
                    dve.wait_ge(s["conv_t"], k + 1)
                    y, th = convy[:, k % 3, 0, :], convy[:, k % 3, 1, :]
                    V.scalar_tensor_tensor(xc[:, k, 0:SEQ], th[:, 0:SEQ], 1.0, y[:, 0:SEQ], ALU.add, ALU.mult)
                    first = TAPS - 1 + SEQ
                    V.scalar_tensor_tensor(xc[:, k, SEQ:TOK], th[:, first:CONV_OUT:TAPS], 1.0, y[:, first:CONV_OUT:TAPS],
                                           ALU.add, ALU.mult).then_inc(s["conv_silu"], 1)

                def rotary(k):
                    dve.wait_ge(proj_drained, at("qk") + k + 1)
                    cs_, sn_ = (cosq, sinq) if k < 4 else (cosk, sink)
                    chain.step(V.tensor_tensor(qk[:, k, :], qk[:, k, :], cs_, ALU.mult))
                    chain.step(V.tensor_tensor(zr[:, k, :], zr[:, k, :], sn_, ALU.mult))
                    chain.wait()
                    V.tensor_tensor(qk[:, k, :], qk[:, k, :], zr[:, k, :], ALU.add).then_inc(s["rope_done"], 1)

                for k in range(CB):
                    y = convy[:, k % 3, 0, :]
                    w0 = PR_CW + k
                    dve.wait_ge(proj_drained, at("x0") + k + 1)
                    chain.link(V.tensor_scalar(y, xc[:, k, 0:CONV_OUT], prm[:, w0:w0 + 1], prm[:, PR_CB + k:PR_CB + k + 1],
                                               ALU.mult, ALU.add))
                    for tap in range(1, TAPS):
                        wt = w0 + CB * tap
                        ins = V.scalar_tensor_tensor(y, xc[:, k, tap:tap + CONV_OUT], prm[:, wt:wt + 1], y,
                                                     ALU.mult, ALU.add)
                        if tap < TAPS - 1:
                            chain.link(ins)
                    ins.then_inc(s["conv_y"], 1)
                    if k >= 1:
                        conv_silu(k - 1)
                conv_silu(CB - 1)

                def output_matrices(hf):
                    lo, hi = 16 * hf, 16 * hf + 16
                    for tau in range(5):
                        pr, pi = pairwise(pwr[:, tau, 0, lo:hi], 16), pairwise(pwr[:, tau, 1, lo:hi], 16)
                        cr, ci = ct[:, 0, lo:hi, :], ct[:, 1, lo:hi, :]
                        chain.step(V.tensor_tensor(et[:, 0, :, :], cr, pr, ALU.mult))
                        chain.step(V.tensor_tensor(et[:, 1, :, :], ci, pi, ALU.mult))
                        chain.step(V.tensor_tensor(et[:, 2, :, :], cr, pi, ALU.mult))
                        chain.step(V.tensor_tensor(et[:, 3, :, :], ci, pr, ALU.mult))
                        chain.wait()
                        for g2 in range(2):
                            hv, cc = slice(64 * g2, 64 * g2 + 64), slice(16 * g2, 16 * g2 + 16)
                            chain.step(V.tensor_tensor(eb[hv, 0, :, tau, cc], et[hv, 0, :, :], et[hv, 1, :, :],
                                                       ALU.subtract))
                            chain.step(V.scalar_tensor_tensor(eb[hv, 1, :, tau, cc], et[hv, 2, :, :], -1.0,
                                                              et[hv, 3, :, :], ALU.mult, ALU.subtract))
                        chain.wait()
                    for g2 in range(2):
                        hv, cc = slice(64 * g2, 64 * g2 + 64), slice(16 * g2, 16 * g2 + 16)
                        for ri in range(2):
                            ins = V.tensor_copy(bblk[hv, ri, :, cc], bb[hv, ri, lo:hi, :])
                            if g2 + ri < 2:
                                chain.step(ins)
                    ins.then_inc(s["e_ready"], 1)

                filled(dve, "V12")
                filled(dve, "V13")
                filled(dve, "V14")
                filled(dve, "V15")
                for ri in range(4):
                    drained(dve, ("cre0", "cre1", "cim0", "cim1")[ri])
                chain.link(V.memset(view(O_GW, 8192), 0.0))
                output_matrices(0)
                dve.wait_ge(tables_in, 16)
                for k in range(NB):
                    rotary(k)

                def silu_g(k):
                    dve.wait_ge(proj_drained, at("g") + k + 1)
                    V.scalar_tensor_tensor(g[:, k, :], zr[:, k, :], 1.0, g[:, k, :], ALU.add, ALU.mult)\
                        .then_inc(s["g_silu"], 1)

                for k in range(4):
                    silu_g(k)
                filled(dve, "Y03")
                output_matrices(1)
                for k in range(4, NB):
                    silu_g(k)
                def advance(n, factor):
                    pfx, b, place = "rs"[n // 8], n % 8, n % 3
                    drained(dve, f"{pfx}kb{b}")
                    dve.wait_ge(s[f"dec_in{place}"], 16 * (n // 3 + 1))
                    for blk in range(NB):
                        st = dec[:, place, blk, :]
                        chain.step(V.scalar_tensor_tensor(st, st, factor(blk, b), outer[:, b % 2, blk, :],
                                                          ALU.mult, ALU.add))
                    chain.wait()
                    filled(dve, f"{pfx}qb{b}")
                    for blk in range(NB):
                        c = (blk // 2) * P
                        ins = V.tensor_tensor_reduce(outer[:, b % 2, blk, :], dec[:, place, blk, :],
                                                     bank(f"{pfx}qb{b}")[:, c:c + P], 1.0, 0.0, ALU.mult, ALU.add,
                                                     ys[:, blk, b:b + 1])
                    is_drained(ins, f"{pfx}qb{b}")

                def ret_gamma(blk, b):
                    return gam[blk // 2]

                for k in range(NB):
                    drained(dve, f"Y{k // 4}{k % 4}")
                    chain.link(V.scalar_tensor_tensor(zr[:, k, :], u[:, k, :], prm[:, PR_D + k:PR_D + k + 1], zr[:, k, :],
                                                      ALU.mult, ALU.add))
                    chain.link(V.scalar_tensor_tensor(u[:, k, :], zr[:, k, :], 0.044715, zr[:, k, :], ALU.mult, ALU.mult))
                    V.scalar_tensor_tensor(u[:, k, :], u[:, k, :], 1.0, zr[:, k, :], ALU.add, ALU.mult)\
                        .then_inc(s["gelu_arg"], 1)
                filled(dve, "dt")
                dve.wait_ge(s["head_in"], 48)
                X, E_, S_, DL, LA, AC, DW, RH = (dts[:, i, :] for i in range(8))
                is_drained(V.tensor_scalar(X, bank("dt")[0:HEADS, 0:TOK], c16[0:HEADS, 0:1], None, ALU.add), "dt")
                drained(dve, "dt")
                chain.link(V.tensor_scalar(S_, X, -1.0, None, ALU.mult))
                V.tensor_tensor(E_, X, S_, ALU.max).then_inc(s["dt_abs"], 1)
                dve.wait_ge(s["dt_exp"], 1)
                chain.link(V.tensor_scalar(S_, E_, 2.0, None, ALU.add))
                chain.link(V.reciprocal(DL, S_))
                chain.link(V.tensor_tensor(S_, E_, DL, ALU.mult))
                chain.link(V.tensor_tensor(E_, S_, S_, ALU.mult))
                chain.link(V.tensor_scalar(DL, E_, 1.0 / 17.0, None, ALU.mult))
                for n in (15, 13, 11, 9, 7, 5, 3):
                    chain.link(V.scalar_tensor_tensor(DL, DL, 1.0 / n, E_, ALU.add, ALU.mult))
                chain.link(V.scalar_tensor_tensor(DL, DL, 1.0, S_, ALU.add, ALU.mult))
                chain.link(V.tensor_scalar(E_, X, 0.0, None, ALU.max))
                chain.link(V.scalar_tensor_tensor(DL, DL, 2.0, E_, ALU.mult, ALU.add))
                dve.wait_ge(s["alog_exp"], 1)
                chain.link(V.tensor_scalar(LA, DL, c16[0:HEADS, 3:4], -1.0, ALU.mult, ALU.mult))
                V.tensor_tensor_scan(AC[:, 0:SEQ], ones[0:HEADS, 0:1].to_broadcast([HEADS, SEQ]), LA[:, 0:SEQ], 0.0,
                                     ALU.mult, ALU.add).then_inc(s["acum_ready"], 1)
                V.tensor_copy(RH[:, 0:8], DL[:, SEQ:TOK]).then_inc(s["dt_rows"], 1)
                V.tensor_copy(RH[:, 16:17], c16[0:HEADS, 2:3]).then_inc(s["dt_rows"], 1)
                def weigh_keys(tb):
                    filled(dve, f"rk{tb}")
                    is_drained(V.tensor_tensor(btok[:, tb, :].rearrange("p (a b) -> p a b", a=4),
                                               bank(f"rk{tb}")[:, :].rearrange("p (a b) -> p a b", a=4),
                                               wend[:, tb, :][:, :, None].to_broadcast([P, RET_H, P]), ALU.mult), f"rk{tb}")

                for hh in range(4):
                    filled(dve, f"rs{hh}")
                    if hh >= 2:
                        filled(dve, f"ry{hh - 2}")
                    is_drained(V.tensor_tensor(sc[:, hh % 2, :], bank(f"rs{hh}")[:, 0:SCORE_W], decay[:, hh, :], ALU.mult),
                               f"rs{hh}")
                    if hh == 1:
                        weigh_keys(0)
                        weigh_keys(1)
                for k in range(NB):
                    dve.wait_ge(s["gelu_tanh"], k + 1)
                    V.scalar_tensor_tensor(u[:, k, :], u[:, k, :], 1.0, zr[:, k, :], ALU.add, ALU.mult)\
                        .then_inc(s["gelu_done"], 1)
                for k in range(NB):
                    dve.wait_ge(proj_drained, at("z") + k + 1)
                    V.scalar_tensor_tensor(zg[:, k, :], m_[:, k, :], 1.0, zg[:, k, :], ALU.add, ALU.mult)\
                        .then_inc(s["z_silu"], 1)
                dve.wait_ge(s["wend_exp"], 1)
                V.tensor_tensor(DW[:, 0:SEQ], DW[:, 0:SEQ], DL[:, 0:SEQ], ALU.mult).then_inc(s["dt_rows"], 1)

                for b in range(8):
                    advance(b, ret_gamma)
                drained(dve, "rqb7")
                V.tensor_copy(v[:, :, SEQ:TOK], ys).then_inc(s["ret_yc"], 1)
                for k in range(NB):
                    dve.wait_ge(proj_drained, at("s5b") + k + 1)
                    V.scalar_tensor_tensor(m_[:, k, :], m_[:, k, :], 1.0, zr[:, k, :], ALU.add, ALU.mult)\
                        .then_inc(s["gates_m"], 1)
                for hh in range(4):
                    inverse_root(f"rn{hh}", head_rms[:, hh, :], head_rms[:, hh, :])
                    for k in (2 * hh, 2 * hh + 1):
                        chain.step(V.tensor_tensor(v[:, k, :], v[:, k, :], head_rms[:, hh, :], ALU.mult))
                    chain.wait()
                    for k in (2 * hh, 2 * hh + 1):
                        V.tensor_tensor(v[:, k, :], v[:, k, :], g[:, k, :], ALU.mult).then_inc(s["ret_norm"], 1)
                dve.wait_ge(s["gates_m"], 8)
                for k in range(NB):
                    dve.wait_ge(proj_drained, at("gate0") + k + 1)
                    V.scalar_tensor_tensor(m_[:, k, :], zr[:, k, :], 1.0, m_[:, k, :], ALU.add, ALU.mult)\
                        .then_inc(s["gates_m"], 1)
                drained(dve, "sc")
                per_block = cols[:, 96:232].rearrange("p (k n) -> p k n", k=NB)
                chain.step(V.tensor_tensor(vs, xc[:, 0:NB, SEQ:TOK], per_block[:, :, 0:8], ALU.mult))
                for i in range(4):
                    filled(dve, f"sv{i}")
                    tb, half = i // 2, i % 2
                    src = bank(f"sv{i}")[:, :].rearrange("p (a b) -> p a b", a=8)

                    def weight(row):
                        c = (2 * row + tb) * 16 + 8 * half
                        return cols[:, c:c + 8][:, :, None].to_broadcast([P, 8, HEAD_DIM])

                    def half_of(dst):
                        return dst[:, tb, half * 512:half * 512 + 512].rearrange("p (a b) -> p a b", a=8)
                    V.tensor_tensor(half_of(vtok), src, weight(1), ALU.mult)
                    is_drained(V.tensor_tensor(half_of(vw), src, weight(2), ALU.mult), f"sv{i}")

                def masked_scores(gg):
                    filled(dve, f"ss{gg}")
                    if gg >= 2:
                        dve.wait_ge(s["exp_masked"], 4 * (gg - 1))
                    elif gg == 0:
                        filled(dve, "ry2")
                        filled(dve, "ry3")
                    is_drained(V.tensor_tensor(sc[:, gg % 2, :], bank(f"ss{gg}")[:, 0:SCORE_W], causal, ALU.mult),
                               f"ss{gg}")

                def log_decays(m):
                    filled(dve, f"sa{m}")
                    if m >= 1:
                        dve.wait_ge(s["exp_ready"], 2 * m)
                    for h2 in range(2):
                        hd = 2 * m + h2
                        src = bank(f"sa{m}")[:, h2 * SEQ:(h2 + 1) * SEQ]
                        V.tensor_scalar(seg[:, h2, 0:SEQ], src, cols[:, hd:hd + 1], 0.0, ALU.subtract, ALU.min)
                        ins = V.tensor_scalar(seg[:, h2, SEQ:SCORE_W], src[:, P:SEQ], cols[:, 16 + hd:17 + hd], 0.0,
                                              ALU.subtract, ALU.min)
                    is_drained(ins, f"sa{m}")

                def ssd_decay(blk, b):
                    return per_block[:, blk, 8 + b:9 + b]

                masked_scores(0)
                log_decays(0)
                for m in range(8):
                    if m % 2 and m < 7:
                        masked_scores((m + 1) // 2)
                    if m < 7:
                        log_decays(m + 1)
                    filled(dve, f"sy{m}")
                    is_drained(V.scalar_tensor_tensor(xc[:, m, 0:SEQ], xc[:, m, 0:SEQ], per_block[:, m, 16:17],
                                                      bank(f"sy{m}")[:, 0:SEQ], ALU.mult, ALU.add), f"sy{m}")
                    if m % 2:
                        advance(8 + m // 2, ssd_decay)
                for b in range(4, 8):
                    advance(8 + b, ssd_decay)
                chain.step(V.tensor_tensor(vs, xc[:, 0:NB, SEQ:TOK],
                                           per_block[:, :, 16:17].to_broadcast([P, NB, SAMPLES]), ALU.mult))
                drained(dve, "sqb7")
                chain.wait()
                for i in range(8):
                    drained(dve, f"sy{i}")
                chain.link(V.tensor_tensor(xc[:, 0:NB, SEQ:TOK], vs, ys, ALU.add))
                for k in range(NB):
                    V.tensor_tensor(xc[:, k, 0:TOK], xc[:, k, 0:TOK], zg[:, k, :], ALU.mult).then_inc(s["ssd_yz"], 1)
                for k in range(NB):
                    dve.wait_ge(proj_drained, at("gate2") + k + 1)
                    chain.link(V.scalar_tensor_tensor(u[:, k, :], zr[:, k, :], 1.0, u[:, k, :], ALU.add, ALU.mult))
                    V.tensor_tensor(m_[:, k, :], m_[:, k, :], u[:, k, :], ALU.add).then_inc(s["gates_m"], 1)
                for gg in range(4):
                    inverse_root(f"sn{gg}", head_rms[:, gg, :], head_rms[:, gg, :])
                    for k in (2 * gg, 2 * gg + 1):
                        V.scalar_tensor_tensor(xc[:, k, 0:TOK], xc[:, k, 0:TOK], prm[:, PR_SN + k:PR_SN + k + 1],
                                               head_rms[:, gg, :], ALU.mult, ALU.mult).then_inc(s["ssd_norm"], 1)
                for k in range(NB):
                    dve.wait_ge(proj_drained, at("ssdo") + k + 1)
                    chain.link(V.scalar_tensor_tensor(u[:, k, :], qk[:, k, :], 1.0, u[:, k, :], ALU.add, ALU.mult))
                    V.tensor_tensor(m_[:, k, :], m_[:, k, :], u[:, k, :], ALU.add).then_inc(s["merged"], 1)
                for k in range(NB):
                    dve.wait_ge(proj_drained, at("wo") + k + 1)
                    V.tensor_tensor(h[:, k, :], h[:, k, :], u[:, k, :], ALU.add).then_inc(s["resid"], 1)
                inverse_root("n2", rms, rstd)
                for k in range(NB):
                    V.scalar_tensor_tensor(xn[:, k, :], h[:, k, :], prm[:, PR_N2 + k:PR_N2 + k + 1], rstd,
                                           ALU.mult, ALU.mult).then_inc(s["xn_ready"], 1)
                with dve.Fori(0, 4) as j:
                    for b in range(8):
                        dve.wait_ge(proj_drained, at("up0") + 8 * j + (b + 1))
                        hb = hid[:, bass.ds(8 * j + b, 1), :]
                        V.tensor_tensor(hb, hb, hb, ALU.mult).then_inc(s["hid_ready"], 1)
                with dve.Fori(0, 2) as jj:
                    for b in range(4):
                        dve.wait_ge(proj_drained, at("dn0") + 4 * jj + (b + 1))
                        hb = h[:, bass.ds(4 * jj + b, 1), :]
                        V.tensor_tensor(hb, hb, u[:, bass.ds(4 * jj + b, 1), :], ALU.add)

            @block.gpsimd
            def _(pool):
                G = nc.gpsimd
                chain = Chain(pool, pool_step)
                G.memset(view(O_U4, PAIRS * U4_W), 0.0).then_inc(s["pool_zero"], 1)
                pool.wait_ge(s["pool_zero"], 1)
                G.memset(sv[:, 8, :], 0.0).then_inc(s["pool_zero"], 1)
                pool.wait_ge(s["pool_zero"], 2)
                G.memset(xc[:, :, 0:TAPS - 1], 0.0).then_inc(s["pool_zero"], 1)

                halves = lambda lo: sv[:, lo:lo + CHUNKS, :].rearrange("p (j two) (i m) -> p j two i m", two=2, i=2)
                wide = lambda ap: ap.rearrange("p (i m) -> p i m", i=2)[:, None, :, :]

                def add_advanced(dst, src, tmp):
                    shape = [P, src.shape[1], 2, PAIRS]
                    chain.link(G.tensor_tensor(tmp, src, wide(a4r).to_broadcast(shape), ALU.mult))
                    chain.link(G.tensor_tensor(dst, dst, tmp, ALU.add))
                    chain.link(G.tensor_tensor(tmp[:, :, ::-1, :], src, wide(a4i).to_broadcast(shape), ALU.mult))
                    return G.tensor_tensor(dst, dst, tmp, ALU.add)

                pool.wait_ge(s["powers_ready"], 1)
                for i in range(12, 16):
                    drained(pool, f"V{i}")
                add_advanced(halves(9)[:, :, 1], halves(9)[:, :, 0], view(O_V, CHUNKS // 2, 2, PAIRS))\
                    .then_inc(s["pairs_joined"], 1)
                pool.wait_ge(s["pairs_joined"], 1)
                both = trig.rearrange("p a b c -> p (a b c)")[:, 0:128].rearrange("p (w i m) -> p w i m", w=2, i=2)
                steps = 4
                with pool.Fori(0, CHUNKS // 2 // steps) as j:
                    for q in range(steps):
                        at8 = 2 * steps * j + (8 + 2 * q)
                        now = sv[:, bass.ds(at8, 1), :].to_broadcast([P, 2, 64])
                        new = sv[:, bass.ds(at8 + 2, 1), :].rearrange("p o (i m) -> p (o i) m", i=2)
                        if q > 0:
                            pool.wait_ge(s["scan_step"], 3 * q)
                        G.tensor_tensor(both.rearrange("p w i m -> p w (i m)"), a8w, now, ALU.mult)\
                            .then_inc(s["scan_step"], 1)
                        pool.wait_ge(s["scan_step"], 3 * q + 1)
                        G.tensor_tensor(new, new, both[:, 0, :, :], ALU.add).then_inc(s["scan_step"], 1)
                        pool.wait_ge(s["scan_step"], 3 * q + 2)
                        G.tensor_tensor(new, new, both[:, 1, ::-1, :], ALU.add).then_inc(s["scan_step"], 1)
                    pool.wait_ge(s["scan_step"], 3 * steps)
                    pool.sem_clear(s["scan_step"])
                pool.wait_ge(s["e_ready"], 1)
                fill_tmp = view(O_SM + 1024, CHUNKS // 4, 2, PAIRS)
                for part in range(2):
                    js = slice(part * CHUNKS // 4, (part + 1) * CHUNKS // 4)
                    add_advanced(halves(9)[:, js, 0], halves(8)[:, js, 0], fill_tmp).then_inc(s["scan_done"], 1)
                    pool.wait_ge(s["scan_done"], part + 1)
                prod = trig.rearrange("p a b c -> p (a b c)").rearrange("p (s i m) -> p s i m", s=SAMPLES, i=2)
                h0 = sv[:, 0:SAMPLES, :].rearrange("p s (i m) -> p s i m", i=2)
                add = sv[:, 73:81, :].rearrange("p s (i m) -> p s i m", i=2)
                fac = lambda ap: ap.rearrange("p (i m) -> p i m", i=2)[:, None, :, :].to_broadcast([P, SAMPLES, 2, PAIRS])
                chain.link(G.tensor_tensor(prod, h0, fac(a1r), ALU.mult))
                chain.link(G.tensor_tensor(add, add, prod, ALU.add))
                chain.link(G.tensor_tensor(prod[:, :, ::-1, :], h0, fac(a1i), ALU.mult))
                G.tensor_tensor(add, add, prod, ALU.add).then_inc(s["newst_ready"], 1)

                def add_pairs(squared):
                    for hh in range(4):
                        pool.wait_ge(s[squared], 2 * hh + 2)
                        G.tensor_tensor(sq8[:, 2 * hh, :], sq8[:, 2 * hh, :], sq8[:, 2 * hh + 1, :], ALU.add)\
                            .then_inc(s["pair_sums"], 1)

                add_pairs("retsq")
                for hd in range(HEADS):
                    pool.wait_ge(s["exp_ready"], hd + 1)
                    if hd % 4 == 0:
                        drained(pool, f"ss{hd // 4}")
                    G.tensor_tensor(ex[:, hd % 2, :], ex[:, hd % 2, :], sc[:, (hd // 4) % 2, :], ALU.mult)\
                        .then_inc(s["exp_masked"], 1)
                add_pairs("ssdsq")

        with nc.Fori(0, DEPTH) as lyr:
            with nc.Block() as block:
                layer(nc, block, t, lyr)
            nc.all_engine_barrier(sems_to_clear=sem_range)

        fms, frs = view(O_G, TOK), view(O_G + TOK, TOK)
        ytok = view(O_R, 2, D_MODEL)
        ysam = view(O_R + 2 * D_MODEL, D_MODEL, p1=SAMPLES)
        with nc.Block() as block:
            @block.scalar
            def _(act):
                nc.scalar.activation(table_warm[:, :], eps, ACT.Sqrt)
                for k in range(NB // 2, NB):
                    nc.scalar.activation(zr[:, k, :], h[:, k, :], ACT.Square).then_inc(s["squares"], 1)
                act.wait_ge(proj_filled, 1)
                nc.scalar.activation(fms, banks[0][:, 0:TOK], ACT.Sqrt, scale=1.0 / D_MODEL, bias=eps)\
                    .then_inc(s["mean_ready"], 1)
                for i in range(6):
                    act.wait_ge(proj_filled, 2 + i)
                    src = banks[(1 + i) % 4]
                    if i < 4:
                        ins = nc.scalar.activation(ytok[:, i // 2, (i % 2) * 512:(i % 2) * 512 + 512], src[:, :], ACT.Copy)
                    else:
                        ins = nc.scalar.activation(ysam[:, (i % 2) * 512:(i % 2) * 512 + 512], src[0:SAMPLES, :], ACT.Copy)
                    ins.then_inc(s["y_rows"], 1)

            @block.tensor
            def _(pe):
                pe.wait_ge(s["square_sum"], 1)
                pe.matmul(banks[0][:, 0:TOK], ones, zr[:, 0, :], start=True, stop=True).then_inc(proj_filled, 1)
                for i in range(6):
                    if i == 3:
                        pe.wait_ge(s["mean_ready"], 1)
                    elif i > 3:
                        pe.wait_ge(s["y_rows"], i - 3)
                    dst = banks[(1 + i) % 4]
                    for j in range(4):
                        k = 4 * (i % 2) + j
                        pe.wait_ge(s["xn_ready"], k + 1)
                        if i < 4:
                            mm = pe.transpose(dst[:, j * P:(j + 1) * P], xn[:, k, (i // 2) * P:(i // 2 + 1) * P], ident)
                        else:
                            mm = pe.transpose(dst[0:SAMPLES, j * P:(j + 1) * P], xn[:, k, SEQ:TOK], ident)
                    mm.then_inc(proj_filled, 1)

            @block.vector
            def _(dve):
                add_squares(Chain(dve, dve_step), dve)
                dve.wait_ge(s["mean_ready"], 1)
                nc.vector.reciprocal(frs, fms).then_inc(s["rstd_ready"], 1)
                dve.wait_ge(s["rstd_ready"], 1)
                for k in range(NB):
                    nc.vector.scalar_tensor_tensor(xn[:, k, :], h[:, k, :], prm[:, PR_FN + k:PR_FN + k + 1], frs,
                                                   ALU.mult, ALU.mult).then_inc(s["xn_ready"], 1)

            @block.sync
            def _(sp):
                y_blocks = t["y_prompt"].rearrange("o (tb p) d -> p (o tb) d", p=P)
                for tb in range(2):
                    sp.wait_ge(s["y_rows"], 2 * tb + 2)
                    sp.dma_start(y_blocks[:, tb, :], ytok[:, tb, :]).then_inc(s["y_out"], 16)
                sp.wait_ge(s["y_rows"], 6)
                sp.dma_start(t["y_sample"].rearrange("b o d -> (b o) d"), ysam).then_inc(s["y_out"], 16)
                sp.wait_ge(s["y_out"], 48)


_INS = ["x_prompt", "x_sample", "state_s5_re", "state_s5_im", "state_ssd", "state_conv", "state_ret", "norm1_w", "w_in",
        "s5_a_re", "s5_a_im", "s5_log_dt", "s5_b_re", "s5_b_im", "s5_c_re", "s5_c_im", "s5_d", "w_s5_out",
        "ssd_conv_w", "ssd_conv_b", "ssd_dt_bias", "ssd_a_log", "ssd_d", "ssd_norm_w", "w_ssd_out", "w_ret_out",
        "w_out", "norm2_w", "w_mlp_up", "w_mlp_down", "final_norm_w"]
_OUTS = [("y_prompt", (1, SEQ, D_MODEL)), ("y_sample", (SAMPLES, 1, D_MODEL))]
for _sfx, _b in (("p", 1), ("s", SAMPLES)):
    _OUTS += [(f"new_s5_re_{_sfx}", (DEPTH, _b, S5_GROUPS, S5_STATE)), (f"new_s5_im_{_sfx}", (DEPTH, _b, S5_GROUPS, S5_STATE)),
              (f"new_ssd_{_sfx}", (DEPTH, _b, HEADS, HEAD_DIM, SSD_N)), (f"new_conv_{_sfx}", (DEPTH, _b, TAPS - 1, CONV_DIM)),
              (f"new_ret_{_sfx}", (DEPTH, _b, RET_H, RET_P, RET_N))]


def kernel(**inputs):
    import numpy as _np
    import concourse.bacc as _bacc
    from concourse.bass_utils import run_bass_kernel_spmd as _run

    nc = _bacc.Bacc("TRN2", target_bir_lowering=False, num_devices=1)
    arrays, t = {}, {}
    for name in _INS:
        a = _np.ascontiguousarray(inputs[name])
        arrays[f"in_{name}"] = a
        t[name] = nc.dram_tensor(f"in_{name}", a.shape, F32, kind="ExternalInput").ap()
    arrays["in_consts"] = constant_table()
    t["consts"] = nc.dram_tensor("in_consts", (P, CONST_W), F32, kind="ExternalInput").ap()
    for name, shape in _OUTS:
        t[name] = nc.dram_tensor(f"out_{name}", shape, F32, kind="ExternalOutput").ap()
    build_trunk(nc, t)
    r = _run(nc, [arrays], core_ids=[0])
    return tuple(r.results[0][f"out_{name}"] for name, _ in _OUTS)
```
